# Optimizing a Trainium2 kernel written in Bass

```python
import math
import jax
import jax.numpy as jnp
from jax import lax
import numpy as np

D_MODEL = 1024
BATCH = 1
SEQ = 128
DEPTH = 2
DEC_BATCH = 1
DEC_SEQ = 256
PAST_LEN = 128

GRID_W = 64
BRANCH_W = 512
N_BRANCH = 4
H_A = 4
DH_A = 128
MLSTM_CHUNK = 128
H_B = 8
DH_B = 64
NA_ROWS = 8
NA_COLS = 16
NA_QCB = 16
NA_KSPAN = 32
H_C = 8
KV_C = 2
DH_C = 64
SWA_WINDOW = 128
SWA_BLK = 128
H_D = 4
DH_D = 64
QBLK = 128
N_GROUPS = 4
EXP_PER_GROUP = 4
N_EXPERTS = N_GROUPS * EXP_PER_GROUP
TOP_K_INNER = 2
D_EXPERT = 256
ROPE_BASE = 10000.0
EPS = 1e-6
IN_SPLITS = (H_A * DH_A, H_A * DH_A, H_A * DH_A, H_A * DH_A, 2 * H_A, 2 * H_A,
             H_B * DH_B, H_B * DH_B, H_B * DH_B,
             H_C * DH_C, KV_C * DH_C, KV_C * DH_C,
             H_D * 2 * DH_D, H_D * 2 * DH_D, H_D * 2 * DH_D,
             N_BRANCH * D_MODEL)
N_IN = sum(IN_SPLITS)

kernel_name = 'hybrid_diffusion_trunk_step'

F32 = jnp.float32

def rmsnorm(x, g):
    xf = x.astype(F32)
    y = xf * lax.rsqrt(jnp.mean(xf * xf, axis=-1, keepdims=True) + EPS)
    return (y * g.astype(F32)).astype(x.dtype)

def axial_rope(x):
    T, dh = x.shape[1], x.shape[-1]
    half = dh // 2
    nf = half // 2
    inv = ROPE_BASE ** (-jnp.arange(nf, dtype=F32) / nf)
    t = jnp.arange(T)

    def rot(xh, pos):
        ang = pos.astype(F32)[:, None] * inv[None, :]
        cos = jnp.cos(ang)[:, None, :].astype(x.dtype)
        sin = jnp.sin(ang)[:, None, :].astype(x.dtype)
        x1, x2 = xh[..., :nf], xh[..., nf:]
        return jnp.concatenate([x1 * cos - x2 * sin, x1 * sin + x2 * cos], axis=-1)

    return jnp.concatenate([rot(x[..., :half], t // GRID_W), rot(x[..., half:], t % GRID_W)], axis=-1)

def mlstm_chunkwise(q, k, v, ig, fg, C0, n0, m0):
    B, T, H, dh = q.shape
    nc = T // MLSTM_CHUNK

    def chunks(a):
        a = a.reshape((B, nc, MLSTM_CHUNK) + a.shape[2:])
        return jnp.moveaxis(a, (1, 3), (0, 2))

    qc = chunks(q.astype(F32))
    kc = chunks(k.astype(F32) * (dh ** -0.5))
    vc = chunks(v.astype(F32))
    ic = chunks(ig.astype(F32))
    lfc = chunks(jax.nn.log_sigmoid(fg.astype(F32)))
    causal = jnp.tril(jnp.ones((MLSTM_CHUNK, MLSTM_CHUNK), bool))

    def step(carry, inp):
        C, n, m = carry
        qx, kx, vx, ix, lf = inp
        b = jnp.cumsum(lf, axis=-1)
        logd = jnp.where(causal, b[..., :, None] - b[..., None, :] + ix[..., None, :], -jnp.inf)
        inter = b + m[..., None]
        m_t = jnp.maximum(inter, jnp.max(logd, axis=-1))
        w = jnp.exp(logd - m_t[..., None])
        a = jnp.exp(inter - m_t)
        s = jnp.einsum('bhtk,bhsk->bhts', qx, kx) * w
        num = a[..., None] * jnp.einsum('bhvk,bhtk->bhtv', C, qx) + jnp.einsum('bhts,bhsv->bhtv', s, vx)
        den = a * jnp.einsum('bhk,bhtk->bht', n, qx) + jnp.sum(s, axis=-1)
        h = num / jnp.maximum(jnp.abs(den), jnp.exp(-m_t))[..., None]
        bL = b[..., -1]
        g = bL[..., None] - b + ix
        m_new = jnp.maximum(bL + m, jnp.max(g, axis=-1))
        decay = jnp.exp(bL + m - m_new)
        wk = jnp.exp(g - m_new[..., None])
        C_new = decay[..., None, None] * C + jnp.einsum('bhs,bhsv,bhsk->bhvk', wk, vx, kx)
        n_new = decay[..., None] * n + jnp.einsum('bhs,bhsk->bhk', wk, kx)
        return (C_new, n_new, m_new), h

    (C, n, m), hs = lax.scan(step, (C0.astype(F32), n0.astype(F32), m0.astype(F32)), (qc, kc, vc, ic, lfc))
    h = jnp.moveaxis(hs, (0, 2), (1, 3)).reshape(B, T, H, dh)
    return h.astype(q.dtype), C, n, m

def mlstm_bidir(q, k, v, ig, fg, C0, n0, m0):
    flip = lambda a: jnp.flip(a, axis=1)
    h_f, C_f, n_f, m_f = mlstm_chunkwise(q, k, v, ig[:, :, 0], fg[:, :, 0], C0[:, 0], n0[:, 0], m0[:, 0])
    h_b, C_b, n_b, m_b = mlstm_chunkwise(flip(q), flip(k), flip(v), flip(ig[:, :, 1]), flip(fg[:, :, 1]),
                                         C0[:, 1], n0[:, 1], m0[:, 1])
    h = h_f + flip(h_b)
    return h, jnp.stack([C_f, C_b], axis=1), jnp.stack([n_f, n_b], axis=1), jnp.stack([m_f, m_b], axis=1)

def ctx_attend(q, k, v, sink=None):
    B, T = q.shape[:2]
    nq = T // QBLK
    qb = jnp.moveaxis(q.reshape((B, nq, QBLK) + q.shape[2:]), 1, 0)
    scale = q.shape[-1] ** -0.5

    def one(qx):
        s = jnp.einsum('bqhgd,bkhd->bhgqk', qx, k).astype(F32) * scale
        if sink is not None:
            sk = jnp.broadcast_to(sink.astype(F32)[None, :, :, None, None], s.shape[:-1] + (1,))
            p = jax.nn.softmax(jnp.concatenate([s, sk], axis=-1), axis=-1)[..., :-1]
        else:
            p = jax.nn.softmax(s, axis=-1)
        return jnp.einsum('bhgqk,bkhd->bqhgd', p.astype(v.dtype), v)

    out = lax.map(one, qb)
    return jnp.moveaxis(out, 0, 1).reshape(B, T, -1)

def nat_latent(q, k, v, kc, vc, rpb):
    B, T, H, d = q.shape
    rows = T // GRID_W
    kr = min(NA_ROWS, rows)
    ncb = GRID_W // NA_QCB
    r = np.arange(rows)
    rs = np.clip(r - kr // 2, 0, rows - kr)
    krow = rs[:, None] + np.arange(kr)[None, :]
    j = np.arange(ncb)
    ks = np.clip(j * NA_QCB - NA_COLS // 2, 0, GRID_W - NA_KSPAN)
    kcol = ks[:, None] + np.arange(NA_KSPAN)[None, :]
    tok = krow[:, None, :, None] * GRID_W + kcol[None, :, None, :]
    nkey = kr * NA_KSPAN
    kb = jnp.take(k, tok.reshape(-1), axis=1).reshape(B, rows, ncb, nkey, H, d)
    vb = jnp.take(v, tok.reshape(-1), axis=1).reshape(B, rows, ncb, nkey, H, d)
    qb = q.reshape(B, rows, ncb, NA_QCB, H, d)
    qcol = j[:, None] * NA_QCB + np.arange(NA_QCB)[None, :]
    cs = np.clip(qcol - NA_COLS // 2, 0, GRID_W - NA_COLS)
    colvalid = (kcol[:, None, :] >= cs[:, :, None]) & (kcol[:, None, :] < cs[:, :, None] + NA_COLS)
    valid = np.broadcast_to(colvalid[:, :, None, :], (ncb, NA_QCB, kr, NA_KSPAN)).reshape(ncb, NA_QCB, nkey)
    ri = krow - r[:, None] + (NA_ROWS - 1)
    ci = np.clip(kcol[:, None, :] - qcol[:, :, None] + (NA_COLS - 1), 0, 2 * NA_COLS - 2)
    bias = rpb[:, ri[:, None, None, :, None], ci[None, :, :, None, :]]
    bias = jnp.transpose(bias.reshape(H, rows, ncb, NA_QCB, nkey), (1, 2, 0, 3, 4))
    scale = d ** -0.5
    s_nb = jnp.einsum('brjqhd,brjkhd->brjhqk', qb, kb).astype(F32) * scale + bias.astype(F32)[None]
    s_nb = jnp.where(valid[None, None, :, None], s_nb, -jnp.inf)
    s_ctx = jnp.einsum('brjqhd,bphd->brjhqp', qb, kc).astype(F32) * scale
    p = jax.nn.softmax(jnp.concatenate([s_nb, s_ctx], axis=-1), axis=-1).astype(v.dtype)
    out = (jnp.einsum('brjhqk,brjkhd->brjqhd', p[..., :nkey], vb)
           + jnp.einsum('brjhqp,bphd->brjqhd', p[..., nkey:], vc))
    return out.reshape(B, T, H * d)

def swa_latent(q, k, v, kc, vc, sink):
    B, T, KV, G, d = q.shape
    nb = T // SWA_BLK

    def slabs(a):
        ap = jnp.pad(a, ((0, 0), (SWA_BLK, SWA_BLK), (0, 0), (0, 0))).reshape(B, nb + 2, SWA_BLK, KV, d)
        return jnp.concatenate([ap[:, :nb], ap[:, 1:nb + 1], ap[:, 2:]], axis=2)

    ksl, vsl = slabs(k), slabs(v)
    qb = q.reshape(B, nb, SWA_BLK, KV, G, d)
    scale = d ** -0.5
    s_band = jnp.einsum('bnqhgd,bnkhd->bnhgqk', qb, ksl).astype(F32) * scale
    qi = np.arange(SWA_BLK)[:, None]
    kj = np.arange(3 * SWA_BLK)[None, :]
    kpos = np.arange(nb)[:, None, None] * SWA_BLK - SWA_BLK + kj[None]
    valid = (np.abs(kj - SWA_BLK - qi)[None] <= SWA_WINDOW) & (kpos >= 0) & (kpos < T)
    s_band = jnp.where(valid[None, :, None, None], s_band, -jnp.inf)
    s_ctx = jnp.einsum('bnqhgd,bphd->bnhgqp', qb, kc).astype(F32) * scale
    sk = jnp.broadcast_to(sink.astype(F32)[None, None, :, :, None, None], s_band.shape[:-1] + (1,))
    p = jax.nn.softmax(jnp.concatenate([s_band, s_ctx, sk], axis=-1), axis=-1).astype(v.dtype)
    nk = 3 * SWA_BLK
    P = kc.shape[1]
    out = (jnp.einsum('bnhgqk,bnkhd->bnqhgd', p[..., :nk], vsl)
           + jnp.einsum('bnhgqp,bphd->bnqhgd', p[..., nk:nk + P], vc))
    return out.reshape(B, T, KV * G * d)

def diff_attend(q, k, v, lam):
    B, T, H = q.shape[:3]
    nq = T // QBLK
    qb = jnp.moveaxis(q.reshape((B, nq, QBLK) + q.shape[2:]), 1, 0)
    scale = q.shape[-1] ** -0.5

    def one(qx):
        s = jnp.einsum('bqhcd,bkhcd->bhcqk', qx, k).astype(F32) * scale
        p = jax.nn.softmax(s, axis=-1)
        pd = p[:, :, 0] - lam * p[:, :, 1]
        return jnp.einsum('bhqk,bkhe->bqhe', pd.astype(v.dtype), v)

    out = lax.map(one, qb)
    return jnp.moveaxis(out, 0, 1).reshape(B, T, H, v.shape[-1])

def mixer_sublayer(h, lp, ctx, lam_init):
    (w_in, i_bias, f_bias, a_norm, rpb, sink, lq1, lk1, lq2, lk2, subln, w_branch, w_out) = lp
    B, T, _ = h.shape
    offs = np.cumsum(IN_SPLITS)[:-1].tolist()
    (aq, ak, av, ao, aig, afg, bq, bk, bv, cq, ck, cv, dq, dk, dv, gt) = jnp.split(h @ w_in, offs, axis=-1)
    aq, ak, av = (a.reshape(B, T, H_A, DH_A) for a in (aq, ak, av))
    aig = aig.reshape(B, T, 2, H_A) + i_bias
    afg = afg.reshape(B, T, 2, H_A) + f_bias
    bq, bk, bv = (a.reshape(B, T, H_B, DH_B) for a in (bq, bk, bv))
    cq = cq.reshape(B, T, KV_C, H_C // KV_C, DH_C)
    ck = ck.reshape(B, T, KV_C, DH_C)
    cv = cv.reshape(B, T, KV_C, DH_C)
    dq = dq.reshape(B, T, H_D, 2, DH_D)
    dk = dk.reshape(B, T, H_D, 2, DH_D)
    dv = dv.reshape(B, T, H_D, 2 * DH_D)
    sink = sink.reshape(KV_C, H_C // KV_C)
    lam = jnp.exp(jnp.sum(lq1.astype(F32) * lk1.astype(F32))) - jnp.exp(jnp.sum(lq2.astype(F32) * lk2.astype(F32))) + lam_init
    if ctx is None:
        C0 = jnp.zeros((B, 2, H_A, DH_A, DH_A), F32)
        n0 = jnp.zeros((B, 2, H_A, DH_A), F32)
        m0 = jnp.zeros((B, 2, H_A), F32)
        ya, Cs, ns, ms = mlstm_bidir(aq, ak, av, aig, afg, C0, n0, m0)
        yb = ctx_attend(bq[:, :, :, None], bk, bv)
        yc = ctx_attend(cq, ck, cv, sink)
        yd = diff_attend(dq, dk, dv, lam)
        new = (bk, bv, ck, cv, dk.reshape(B, T, H_D, 2 * DH_D), dv, Cs, ns, ms)
    else:
        (kb_c, vb_c, kc_c, vc_c, kd_c, vd_c, C0, n0, m0) = ctx
        ya, _, _, _ = mlstm_bidir(aq, ak, av, aig, afg, C0, n0, m0)
        yb = nat_latent(bq, bk, bv, kb_c, vb_c, rpb)
        cq_r = axial_rope(cq.reshape(B, T, H_C, DH_C)).reshape(cq.shape)
        yc = swa_latent(cq_r, axial_rope(ck), cv, kc_c, vc_c, sink)
        dq_r = axial_rope(dq.reshape(B, T, 2 * H_D, DH_D)).reshape(dq.shape)
        dk_r = axial_rope(dk.reshape(B, T, 2 * H_D, DH_D)).reshape(dk.shape)
        kd = jnp.concatenate([dk_r, kd_c.reshape(B, -1, H_D, 2, DH_D)], axis=1)
        vd = jnp.concatenate([dv, vd_c], axis=1)
        yd = diff_attend(dq_r, kd, vd, lam)
        new = None
    ya = jax.nn.sigmoid(ao) * rmsnorm(ya, a_norm.reshape(H_A, DH_A)).reshape(B, T, BRANCH_W)
    yd = (rmsnorm(yd, subln) * (1.0 - lam_init)).reshape(B, T, BRANCH_W)
    branches = jnp.stack([ya, yb, yc, yd], axis=2)
    proj = jnp.einsum('btnw,nwd->btnd', branches, w_branch)
    gates = jax.nn.sigmoid(gt.reshape(B, T, N_BRANCH, D_MODEL))
    out = jnp.sum(gates * proj, axis=2) @ w_out
    return out, new

def hier_moe(h, w_rg, w_re, w_g, w_u, w_d):
    lead = h.shape[:-1]
    x = h.reshape(-1, D_MODEL)
    glog = (x @ w_rg).astype(F32)
    gprob = jax.nn.softmax(glog, axis=-1)
    gsel = jnp.argmax(glog, axis=-1)
    gw = jnp.take_along_axis(gprob, gsel[:, None], axis=-1)
    elog = (x @ w_re).astype(F32).reshape(-1, N_GROUPS, EXP_PER_GROUP)
    elog_g = jnp.take_along_axis(elog, gsel[:, None, None], axis=1)[:, 0]
    top_p, top_i = lax.top_k(jax.nn.softmax(elog_g, axis=-1), TOP_K_INNER)
    top_p = top_p / jnp.sum(top_p, axis=-1, keepdims=True)
    eidx = gsel[:, None] * EXP_PER_GROUP + top_i
    gate = jnp.sum(jax.nn.one_hot(eidx, N_EXPERTS, dtype=F32) * (gw * top_p)[..., None], axis=1)
    hid = jax.nn.silu(jnp.einsum('nd,edf->nef', x, w_g)) * jnp.einsum('nd,edf->nef', x, w_u)
    y = jnp.einsum('nef,efd->nd', hid * gate[..., None].astype(hid.dtype), w_d)
    return y.reshape(lead + (D_MODEL,))

def trunk_layer(x, cond, lp_norm, lp_mix, lp_moe, ctx, lam_init):
    norm_mix_l, norm_ffn_l, w_mod_l, b_mod_l = lp_norm
    mod = jax.nn.silu(cond) @ w_mod_l + b_mod_l
    sh1, sc1, g1, sh2, sc2, g2 = jnp.split(mod[..., None, :], 6, axis=-1)
    h = rmsnorm(x, norm_mix_l) * (1.0 + sc1) + sh1
    y, new = mixer_sublayer(h, lp_mix, ctx, lam_init)
    x = x + g1 * y
    h = rmsnorm(x, norm_ffn_l) * (1.0 + sc2) + sh2
    x = x + g2 * hier_moe(h, *lp_moe)
    return x, new

def setup_inputs(seed: int = 0) -> dict:
    key = jax.random.key(seed)
    ks = iter(jax.random.split(key, 48))
    nrm = lambda shape, s=1.0: jax.random.normal(next(ks), shape, F32) * s
    D = D_MODEL
    return {
        'x_prompt': nrm((BATCH, SEQ, D)),
        'x_sample': nrm((DEC_BATCH, DEC_SEQ, D)),
        'cache_nat_k': nrm((DEC_BATCH, DEPTH, PAST_LEN, H_B, DH_B)),
        'cache_nat_v': nrm((DEC_BATCH, DEPTH, PAST_LEN, H_B, DH_B)),
        'cache_swa_k': nrm((DEC_BATCH, DEPTH, PAST_LEN, KV_C, DH_C)),
        'cache_swa_v': nrm((DEC_BATCH, DEPTH, PAST_LEN, KV_C, DH_C)),
        'cache_diff_k': nrm((DEC_BATCH, DEPTH, PAST_LEN, H_D, 2 * DH_D)),
        'cache_diff_v': nrm((DEC_BATCH, DEPTH, PAST_LEN, H_D, 2 * DH_D)),
        'state_mlstm_C': nrm((DEC_BATCH, DEPTH, 2, H_A, DH_A, DH_A), 0.1),
        'state_mlstm_n': nrm((DEC_BATCH, DEPTH, 2, H_A, DH_A), 0.1),
        'state_mlstm_m': nrm((DEC_BATCH, DEPTH, 2, H_A), 0.5),
        'c': nrm((DEC_BATCH, D)),
        'c_ctx': nrm((D,)),
        'norm_mix': 1.0 + nrm((DEPTH, D), 0.02),
        'norm_ffn': 1.0 + nrm((DEPTH, D), 0.02),
        'norm_final': 1.0 + nrm((D,), 0.02),
        'w_mod': nrm((DEPTH, D, 6 * D), 0.5 * D ** -0.5),
        'b_mod': nrm((DEPTH, 6 * D), 0.02),
        'w_in': nrm((DEPTH, D, N_IN), D ** -0.5),
        'mlstm_i_bias': nrm((DEPTH, 2, H_A), 0.1),
        'mlstm_f_bias': 3.0 + nrm((DEPTH, 2, H_A), 0.5),
        'mlstm_norm': 1.0 + nrm((DEPTH, H_A * DH_A), 0.02),
        'nat_rpb': nrm((DEPTH, H_B, 2 * NA_ROWS - 1, 2 * NA_COLS - 1), 0.02),
        'swa_sink': nrm((DEPTH, H_C), 0.5),
        'diff_lq1': nrm((DEPTH, DH_D), 0.1),
        'diff_lk1': nrm((DEPTH, DH_D), 0.1),
        'diff_lq2': nrm((DEPTH, DH_D), 0.1),
        'diff_lk2': nrm((DEPTH, DH_D), 0.1),
        'diff_subln': 1.0 + nrm((DEPTH, 2 * DH_D), 0.02),
        'w_branch': nrm((DEPTH, N_BRANCH, BRANCH_W, D), BRANCH_W ** -0.5),
        'w_out': nrm((DEPTH, D, D), D ** -0.5),
        'router_group': nrm((DEPTH, D, N_GROUPS), D ** -0.5),
        'router_expert': nrm((DEPTH, D, N_EXPERTS), D ** -0.5),
        'w_exp_gate': nrm((DEPTH, N_EXPERTS, D, D_EXPERT), D ** -0.5),
        'w_exp_up': nrm((DEPTH, N_EXPERTS, D, D_EXPERT), D ** -0.5),
        'w_exp_down': nrm((DEPTH, N_EXPERTS, D_EXPERT, D), D_EXPERT ** -0.5),
    }

def reference(x_prompt, x_sample, cache_nat_k, cache_nat_v, cache_swa_k, cache_swa_v, cache_diff_k,
              cache_diff_v, state_mlstm_C, state_mlstm_n, state_mlstm_m, c, c_ctx, norm_mix, norm_ffn,
              norm_final, w_mod, b_mod, w_in, mlstm_i_bias, mlstm_f_bias, mlstm_norm, nat_rpb, swa_sink,
              diff_lq1, diff_lk1, diff_lq2, diff_lk2, diff_subln, w_branch, w_out, router_group,
              router_expert, w_exp_gate, w_exp_up, w_exp_down):
    yp, ys = x_prompt, x_sample
    nk, nv, sk, sv, dk, dv, mC, mn, mm = [], [], [], [], [], [], [], [], []
    for l in range(DEPTH):
        lam_init = 0.8 - 0.6 * math.exp(-0.3 * l)
        lp_norm = (norm_mix[l], norm_ffn[l], w_mod[l], b_mod[l])
        lp_mix = (w_in[l], mlstm_i_bias[l], mlstm_f_bias[l], mlstm_norm[l], nat_rpb[l], swa_sink[l],
                  diff_lq1[l], diff_lk1[l], diff_lq2[l], diff_lk2[l], diff_subln[l], w_branch[l], w_out[l])
        lp_moe = (router_group[l], router_expert[l], w_exp_gate[l], w_exp_up[l], w_exp_down[l])
        yp, ctx_new = trunk_layer(yp, c_ctx, lp_norm, lp_mix, lp_moe, None, lam_init)
        for lst, t in zip((nk, nv, sk, sv, dk, dv, mC, mn, mm), ctx_new):
            lst.append(t)
        ctx_l = (cache_nat_k[:, l], cache_nat_v[:, l], cache_swa_k[:, l], cache_swa_v[:, l],
                 cache_diff_k[:, l], cache_diff_v[:, l], state_mlstm_C[:, l], state_mlstm_n[:, l],
                 state_mlstm_m[:, l])
        ys, _ = trunk_layer(ys, c, lp_norm, lp_mix, lp_moe, ctx_l, lam_init)
    y_prompt = rmsnorm(yp, norm_final)
    y_sample = rmsnorm(ys, norm_final)
    new_nat_k = jnp.stack(nk, axis=1)
    new_nat_v = jnp.stack(nv, axis=1)
    new_swa_k = jnp.stack(sk, axis=1)
    new_swa_v = jnp.stack(sv, axis=1)
    new_diff_k = jnp.stack(dk, axis=1)
    new_diff_v = jnp.stack(dv, axis=1)
    new_mlstm_C = jnp.stack(mC, axis=1)
    new_mlstm_n = jnp.stack(mn, axis=1)
    new_mlstm_m = jnp.stack(mm, axis=1)
    return (y_prompt, y_sample, new_nat_k, new_nat_v, new_swa_k, new_swa_v, new_diff_k, new_diff_v,
            new_mlstm_C, new_mlstm_n, new_mlstm_m)


_drawn_inputs = setup_inputs


def setup_inputs(seed=0):
    import zlib

    import numpy as np

    out = dict(_drawn_inputs(seed))
    spreads = {}
    factors = {'cache_swa_k': 3.52,
     'cache_swa_v': 2.844,
     'state_mlstm_C': 4.487,
     'state_mlstm_n': 8.0,
     'state_mlstm_m': 7.549,
     'norm_ffn': 3.877,
     'norm_final': 2.852,
     'mlstm_norm': 8.0,
     'nat_rpb': 8.0,
     'swa_sink': 8.0,
     'diff_lq1': 6.142,
     'diff_lk1': 6.558,
     'diff_lq2': 8.0,
     'diff_lk2': 3.121,
     'diff_subln': 8.0}
    for name, (base, spread) in spreads.items():
        noise = np.random.default_rng([zlib.crc32(name.encode()), seed]).standard_normal(out[name].shape)
        drawn = base * np.exp(spread * noise) if base else spread * noise
        out[name] = jnp.asarray(drawn.astype(out[name].dtype))
    for name, factor in factors.items():
        out[name] = (out[name] * factor).astype(out[name].dtype)
    return out
```

```python
from contextlib import ExitStack

import numpy as np

import concourse.bass as bass
from concourse import mybir

F32 = mybir.dt.float32
F32R = mybir.dt.float32r
ALU = mybir.AluOpType
ACT = mybir.ActivationFunctionType
AX = mybir.AxisListType.X

P = 128
D = 1024
DEPTH = 2
T_LAT, T_CTX, PAST = 256, 128, 128
TILES = (T_LAT + T_CTX) // P
GRID_W = 64
H_A, DH_A = 4, 128
H_B, DH_B = 8, 64
KV_C = 2
H_D = 4
NEXP, DEXP = 16, 256
KD = D // P
EPS = 1e-6
NEG = -1e30

CHUNKS = [("proj", s, 512, 4) for s in ("Aq", "Ak", "Av", "Ao", "Bq", "Bk", "Bv", "Cq")]
CHUNKS += [("proj", "Ckv", 256, 2)]
CHUNKS += [("proj", s, 512, 4) for s in ("Dq", "Dk", "Dv")]
for _n in range(4):
    for _h in range(2):
        CHUNKS += [("gate", (_n, _h), 512, 4), ("branch", (_n, _h), 512, 2)]
CHUNKS += [("wout", _h, 512, 4) for _h in range(2)]
CHUNK_NO = {c[1] if c[0] == "proj" else c[:2]: i for i, c in enumerate(CHUNKS)}
GEMM = []
for _c, (_kind, _arg, _w, _nu) in enumerate(CHUNKS):
    GEMM += [(_c, _i, _nu) for _i in range(_nu)]
NG = len(GEMM)
FIRST_UNIT = {}
for _g, (_c, _i, _nu) in enumerate(GEMM):
    if _i == 0:
        FIRST_UNIT[_c] = _g
LAST_UNIT = {c: FIRST_UNIT[c] + CHUNKS[c][3] - 1 for c in FIRST_UNIT}
EU = 6
EXPERT_UNITS = [(0, 0), (0, 1)]
for _e in range(16):
    EXPERT_UNITS += [(_e, 2), (_e, 3)] + ([(_e + 1, 0), (_e + 1, 1)] if _e < 15 else []) + [(_e, 4), (_e, 5)]
NMOD = 6 * KD
TYPES = "ABCD"
TP = [(ty, w, j) for ty in "ABCD" for w in "qk" for j in range(2 if (ty, w) == ("C", "k") else 4)]
MU = [(0, 0), (1, 1), (0, 2), (1, 2), (0, 1), (1, 0)]
MUPD = [0, 1, 2, 3]
AU = [(ty, t, j) for ty in "BCD" for t in range(TILES) for j in range(4)]
ROPE = [("C", "q", 0), ("C", "q", 1), ("C", "k", 0), ("C", "k", 1), ("C", "k", 2),
        ("D", "q", 0), ("D", "q", 1), ("D", "k", 0), ("D", "k", 1)]
BIASED = [u for u, (ty, t, j) in enumerate(AU) if ty in "BC" and t < 2]
SMALL = 36


def schedule():
    after = {g: [] for g in range(-1, NG)}

    def put(g, *steps):
        after[g] += steps

    put(4, ("mgate",))
    put(5, ("tp", "A", "q", 0), ("tp", "A", "q", 1))
    put(6, ("tp", "A", "q", 2), ("tp", "A", "q", 3), ("mcum",))
    put(9, ("tp", "A", "k", 0), ("tp", "A", "k", 1))
    put(10, ("tp", "A", "k", 2), ("tp", "A", "k", 3))
    for m in range(len(MU)):
        put(11 + 4 * m, ("m1", m))
        put(13 + 4 * m, ("m2", m))
        put(14 + 4 * m, ("m3", m))
    put(LAST_UNIT[CHUNK_NO["Bv"]] + 2, ("dma", "outB"))
    put(LAST_UNIT[CHUNK_NO["Ckv"]] + 1, ("rope", "C", "q", 0), ("rope", "C", "k", 0), ("rope", "C", "k", 2))
    put(LAST_UNIT[CHUNK_NO["Ckv"]] + 2, ("rope", "C", "q", 1), ("rope", "C", "k", 1), ("dma", "outC"))
    put(35, ("dma", "loadB"), ("hn", 0))
    for i in range(4):
        put(36 + i, ("tp", "B", "q", i), ("tp", "B", "k", i))
        put(39 + i, ("to", 0, i))
    put(LAST_UNIT[CHUNK_NO["Dk"]] + 1, ("rope", "D", "q", 0), ("rope", "D", "q", 1))
    put(LAST_UNIT[CHUNK_NO["Dk"]] + 2, ("rope", "D", "k", 0), ("rope", "D", "k", 1))
    put(LAST_UNIT[CHUNK_NO["Dv"]] + 2, ("dma", "outD"))

    def attention(g, first):
        for i in range(12 + 3):
            at = g + (i if i < 9 else 9 + (i - 9) // 2)
            if i >= 3:
                put(at, ("pv", first + i - 3))
            if 2 <= i < 14:
                put(at, ("pt", first + i - 2))
            if i < 12:
                put(at, ("sc", first + i))
        return g + 12

    g = attention(40, 0)
    put(g - 3, ("dma", "keysC"))
    put(g - 1, ("dma", "valuesC"))
    for i in range(4):
        put(g - 3 + i // 2, ("tp", "C", "q", i))
    put(g - 1, ("tp", "C", "k", 0), ("tp", "C", "k", 1))
    g = attention(g, 12)
    put(g - 3, ("dma", "keysD"))
    put(g - 1, ("dma", "valuesD"))
    for i in range(4):
        put(g - 3 + i // 2, ("tp", "D", "q", i))
        put(g - 2 + i // 2, ("tp", "D", "k", i))
    g = attention(g, 24)
    put(g, ("hn", 1))
    for i in range(4):
        put(g + 3, ("to", 1, i))
    d_done = g + 3
    for j in range(16, NMOD):
        put(36 + j, ("mod", j))
        if j % KD == KD - 1:
            put(36 + j, ("modv", j // KD))
            put(37 + j, ("modt", j // KD))
    put(36 + 25, ("gt", 0))
    put(36 + 49, ("gt", 1))
    put(g - 12, ("dma", "gate1"))
    for c in range(4):
        put(LAST_UNIT[CHUNK_NO["gate", (3, 1)]], ("mt", c))
    for c in range(4, 8):
        put(LAST_UNIT[CHUNK_NO["branch", (3, 1)]], ("mt", c))
    put(max(d_done, LAST_UNIT[CHUNK_NO["gate", (3, 0)]]), ("dma", "loadX"))

    steps = [("mod", j) for j in range(8)] + [("modv", 0), ("modt", 0)]
    steps += [("mod", j) for j in range(8, 16)] + [("modv", 1), ("modt", 1), ("norm", 0)]
    for g in range(NG):
        steps.append(("gemm", g))
        steps += after[g]
    branch3 = steps.index(("gemm", FIRST_UNIT[CHUNK_NO["branch", (3, 0)]]))
    assert d_done < NG
    late = [s for s in steps[branch3:] if s in [("to", 1, i) for i in range(4)] or s == ("hn", 1) or
            (s[0] in ("sc", "pt", "pv") and s[1] >= 24)]
    steps = steps[:branch3] + late + [s for s in steps[branch3:] if s not in late]
    steps += [("dma", "gate2"), ("norm", 1), ("route",), ("experts",), ("end",)]
    return steps


SCHEDULE = schedule()
TP_NO = {s[1:]: i for i, s in enumerate(s for s in SCHEDULE if s[0] == "tp")}
assert set(TP_NO) == set(TP)
STREAM = [s for s in SCHEDULE if s[0] in ("mod", "gemm")]
NU = len(STREAM) + NEXP * EU
RAW = 6
CONV = 3
assert NU % RAW == 0 and len(STREAM) % RAW == 0 and NG % CONV == 0

POS_OF = [p for p, s in enumerate(STREAM) if s[0] == "gemm"]
MODPOS = [p for p, s in enumerate(STREAM) if s[0] == "mod"]

PC_NMIX, PC_NFFN, PC_BMOD, PC_N = 0, KD, 2 * KD, 2 * KD + NMOD
PCOLS = PC_N + 2 * H_A
ROWS = {}
_o = 0
for _name, _n in (("ib", 8), ("fb", 8), ("sink", 8), ("lq", 256), ("lam", 2), ("anorm", 512), ("subln", 128), ("m0", 8)):
    ROWS[_name] = (_o, _o + _n)
    _o += _n
PROWS = _o


class Signal:

    def __init__(self, handle, name, per_layer, unit=1, credit=0):
        self.handle, self.name, self.per_layer, self.unit, self.credit, self.n = handle, name, per_layer, unit, credit, 0

    def of(self, instruction):
        instruction.then_inc(self.handle, self.unit)
        self.n += 1

    def value(self, layer, index):
        return (layer * self.per_layer + (index + 1 + self.credit)) * self.unit


def program(nc, a, out, counts):
    ctx = ExitStack()
    with ctx:
        def sb(name, shape, dt=F32):
            return ctx.enter_context(nc.sbuf_tensor(name, shape, dt))

        signals = {}

        def sg(name, unit=1, credit=0):
            h = ctx.enter_context(nc.semaphore(name))
            signals[name] = Signal(h, name, counts.get(name, 1000), unit, credit)
            return signals[name]

        raw = sb("raw", [P, RAW, 1024])
        whi = sb("whi", [P, CONV, 1024], F32R)
        wlo = sb("wlo", [P, CONV, 1024], F32R)
        hhi = sb("hhi", [P, KD, TILES * P], F32R)
        hlo = sb("hlo", [P, KD, TILES * P], F32R)
        bhi = [sb(f"bhi{i}", [P, 4, TILES * P], F32R) for i in range(2)]
        blo = [sb(f"blo{i}", [P, 4, TILES * P], F32R) for i in range(2)]
        pA = sb("pA", [P, 4, TILES, 512])
        pB_at = (nc.sbuf_base + 31) // 32 * 32
        pB = sb("pB", [P, 3, TILES, 512])
        pC = sb("pC", [P, TILES, 768])
        bhi.append(nc.alloc_sbuf_tensor_at("bhi2", [P, 4, TILES * P], F32R, offset=pB_at))
        blo.append(nc.alloc_sbuf_tensor_at("blo2", [P, 4, TILES * P], F32R, offset=pB_at + 4 * 4 * TILES * P))
        qT = sb("qT", [P, 4, TILES * P])
        kT_at = (nc.sbuf_base + 31) // 32 * 32
        kT = sb("kT", [P, 4, TILES * P + PAST])
        ehi = nc.alloc_sbuf_tensor_at("ehi", [P, 2, TILES * P], F32R, offset=kT_at)
        elo = nc.alloc_sbuf_tensor_at("elo", [P, 2, TILES * P], F32R, offset=kT_at + 4 * 2 * TILES * P)
        vc = sb("vc", [P, 512])
        prob = sb("prob", [P, 2, 2, 384])
        probT = sb("probT", [P, 2, 2, 384])
        bias = sb("bias", [P, 2, 384])
        kdup = sb("kdup", [P, TILES, 2, 2, 64])
        sig = sb("sig", [P, TILES, 512])
        cst, nrow = sig[:, 2, :], sig[0:1, 0:2, :]
        small = sb("small", [P, KD, SMALL])
        smhi = sb("smhi", [P, KD, SMALL], F32R)
        smlo = sb("smlo", [P, KD, SMALL], F32R)
        pcol = sb("pcol", [P, PCOLS])
        prow = sb("prow", [P, PROWS])
        cT = sb("cT", [P, 2 * H_A, DH_A])
        modc = sb("modc", [P, 6, KD, 2])
        acol = sb("acol", [P, KD, 2])
        cond = sb("cond", [P, KD, 32])
        grow = sb("grow", [16, P])
        ident = sb("ident", [P, P])
        tri = sb("tri", [P, 2, P])
        ones = sb("ones", [P, P])
        cmask = sb("cmask", [P, 2, P])
        rope_t = sb("rope_t", [P, 2, 64 + 32])
        cval = sb("cval", [P, 5, 12])
        st = sb("st", [P, 16])
        gi = sb("gi", [P, TILES, 8])
        gf = sb("gf", [P, TILES, 8])
        ga = sb("ga", [P, TILES, 8])
        lf = sb("lf", [P, TILES, 8])
        bt = sb("bt", [P, TILES, 16])
        cc = sb("cc", [P, TILES, 8])
        ms = sb("ms", [P, 2, 64])
        mst = sb("mst", [P, 16])
        am = sb("am", [P, 2, 16])
        lam = sb("lam", [P, 8])
        rt = sb("rt", [P, TILES, 20])
        rw = sb("rw", [P, TILES, 80])
        gate = sb("gate", [P, TILES, NEXP])
        order = sb("order", [P, 4])
        zst = sb("zst", [P, 4])
        dummy = sb("sink_col", [P, 16])
        x = pA[:, 0:2, :, :].rearrange("p a t n -> p (a t n)").rearrange("p (t n) -> p t n", t=TILES)
        yacc = pA[:, 2:4, :, :].rearrange("p a t n -> p (a t n)").rearrange("p (t n) -> p t n", t=TILES)
        xn = pB[:, 0:2, :, :].rearrange("p a t n -> p (a t n)").rearrange("p (t n) -> p t n", t=TILES)
        rwf = rw[:, :, :].rearrange("p t n -> p (t n)")
        cond_t = prob[:, 0].rearrange("p a n -> p (a n)")[:, 0:32 * KD].rearrange("p (k c) -> p k c", k=KD)
        mrow = kdup[:, 0].rearrange("p a b n -> p (a b n)")
        Cq = pC[:, :, 0:512]
        Ckv = pC[:, :, 512:768]
        gbc = pC[:, :, :].rearrange("p t n -> p (t n)")[:, 0:2 * D].rearrange("p (c n) -> p c n", c=2)
        merged = [pA[:, 3, :, :], pB[:, 2, :, :]]
        slot = {"Aq": pA[:, 0], "Ak": pA[:, 1], "Av": pA[:, 2], "Ao": pA[:, 3], "Bq": pB[:, 0], "Bk": pB[:, 1],
                "Bv": pB[:, 2], "Cq": Cq, "Ckv": Ckv, "Dq": pA[:, 1], "Dk": pA[:, 2], "Dv": pA[:, 0]}
        hid = sig[:, :, :].rearrange("p t n -> p (t n)")[:, 0:TILES * DEXP].rearrange("p (t n) -> p t n", t=TILES)
        gact = sig[:, :, :].rearrange("p t n -> p (t n)")[:, TILES * DEXP:].rearrange("p (t n) -> p t n", t=TILES)

        def row(name, lo=0, hi=None):
            s, e = ROWS[name]
            return prow[:, s + lo:(s + hi if hi is not None else e)]

        G = ctx.enter_context(nc.psum_tensor("G", [P, 3, 512], F32))
        S = ctx.enter_context(nc.psum_tensor("S", [P, 2, 512], F32))
        T = ctx.enter_context(nc.psum_tensor("T", [P, 2, 512], F32))
        O = ctx.enter_context(nc.psum_tensor("O", [P, 512], F32))

        w_in = [sg(f"w_in{i}", 16) for i in range(RAW)]
        hi_done = sg("hi_done", credit=RAW)
        lo_done = sg("lo_done", credit=RAW)
        unit_pe = sg("unit_pe", credit=CONV)
        tile_pe = sg("tile_pe")
        ev_act = sg("ev_act")
        ev_dve = sg("ev_dve")
        ev_pool = sg("ev_pool")
        mod_pe, mod_act, modt_pe, mod_dve = sg("mod_pe"), sg("mod_act"), sg("modt_pe"), sg("mod_dve")
        par_in, x_saved, x_in = sg("par_in", 16), sg("x_saved", 16), sg("x_in", 16)
        sq_act, rstd_pool, xn_dve, nt_pe = sg("sq_act"), sg("rstd_pool"), sg("xn_dve"), sg("nt_pe")
        hf_dve, hh_act, hl_dve = sg("hf_dve"), sg("hh_act"), sg("hl_dve")
        smh_act, sml_dve = sg("smh_act"), sg("sml_dve")
        mg_pe, mg_dve, ln_act, lf_dve = sg("mg_pe"), sg("mg_dve"), sg("ln_act"), sg("lf_dve")
        mb_pe, cc_dve = sg("mb_pe"), sg("cc_dve")
        tp_pe, tp_act, rope_dve = sg("tp_pe"), sg("tp_act"), sg("rope_dve")
        diag_pool, m1_pe, mmax_dve, mexp_act, ms_dve = (sg("diag_pool"), sg("m1_pe"), sg("mmax_dve"), sg("mexp_act"),
                                                        sg("ms_dve"))
        kw_pool, m2_pe, sT_act, m3_pe, mh_dve = sg("kw_pool"), sg("m2_pe"), sg("sT_act"), sg("m3_pe"), sg("mh_dve")
        mc_act, ct_dve, m_out = sg("mc_act"), sg("ct_dve"), sg("m_out", 16)
        ct_in = sg("ct_in", 16)
        bz_pool = sg("bz_pool")
        keys_in, vals_in, bias_in = sg("keys_in", 16), sg("vals_in", 16), sg("bias_in", 16)
        kv_out = {ty: sg(f"kv_out{ty}", 16) for ty in "BCD"}
        sc_pe, sa_dve, nm_dve, ex_act, pn_dve = sg("sc_pe"), sg("sa_dve"), sg("nm_dve"), sg("ex_act"), sg("pn_dve")
        pt_pe, pa_act, pb_dve, pv_pe = sg("pt_pe"), sg("pa_act"), sg("pb_dve"), sg("pv_pe")
        oh_act, ol_dve, yd_act = sg("oh_act"), sg("ol_dve"), sg("yd_act")
        hs_dve, hr_pool, tanh_act, hn_dve = sg("hs_dve"), sg("hr_pool"), sg("tanh_act"), sg("hn_dve")
        to_pe, th_act, tl_dve = sg("to_pe"), sg("th_act"), sg("tl_dve")
        lam_dve, lam_act = sg("lam_dve"), sg("lam_act")
        gt_pe, gr_act, g_out, g_in = sg("gt_pe"), sg("gr_act"), sg("g_out", 16), sg("g_in", 16)
        mt_pe, mh_act, ml_dve = sg("mt_pe"), sg("mh_act"), sg("ml_dve")
        sp_pe, sp_act = sg("sp_pe"), sg("sp_act")
        rt_pe, rt_dve, rt_act, gate_dve = sg("rt_pe"), sg("rt_dve"), sg("rt_act"), sg("gate_dve")
        yz_pool = sg("yz_pool")
        e_unit, e_tile, e_down = sg("e_unit", credit=3), sg("e_tile", credit=3), sg("e_down", credit=6)
        e_tanh, e_hid, e_pt = sg("e_tanh"), sg("e_hid", credit=3), sg("e_pt")
        e_hh, e_hl, e_y = sg("e_hh"), sg("e_hl", credit=2), sg("e_y", credit=6)
        layer_end = sg("layer_end", credit=1)
        dve_ord, act_ord, pool_ord = sg("dve_ord"), sg("act_ord"), sg("pool_ord")
        e_dve = sg("e_dve")
        const_in = ctx.enter_context(nc.semaphore("const_in"))
        cond_act = ctx.enter_context(nc.semaphore("cond_act"))
        start_dve = ctx.enter_context(nc.semaphore("start_dve"))
        cond_dve = ctx.enter_context(nc.semaphore("cond_dve"))
        fin_sq_act = ctx.enter_context(nc.semaphore("fin_sq_act"))
        fin_rstd_pool = ctx.enter_context(nc.semaphore("fin_rstd_pool"))
        fin_gain_in = ctx.enter_context(nc.semaphore("fin_gain_in"))
        fin_y_dve = ctx.enter_context(nc.semaphore("fin_y_dve"))
        fin_out = ctx.enter_context(nc.semaphore("fin_out"))
        NCONST = 9

        def unit_done(g):
            c, i, n = GEMM[g]
            if i == n - 1:
                return tile_pe, TILES * c + TILES - 1
            return unit_pe, g - c

        def evacuated(c, t):
            if CHUNKS[c][0] in ("proj", "gate"):
                return ev_act, TILES * sum(CHUNKS[i][0] in ("proj", "gate") for i in range(c)) + t
            return ev_dve, TILES * sum(CHUNKS[i][0] not in ("proj", "gate") for i in range(c)) + t

        def pooled(c, t):
            n = sum(CHUNKS[i][0] == "wout" or (CHUNKS[i][0] == "branch" and CHUNKS[i][1][0] > 0) for i in range(c))
            return TILES * n + t

        def load_bias(sp, need, l, b):
            ty, t, j = AU[BIASED[b]]
            if ty == "B":
                bias_in.of(sp.dma_start(bias[:, :, 0:T_LAT], a["nat_bias"][bass.ds((l * 2 + t) * 4 + j, 1)]
                                        .rearrange("a p m n -> p (a m) n")))
            else:
                for m in range(2):
                    bias_in.of(sp.dma_start(bias[:, m, 0:T_LAT], a["swa_mask"][t]))

        def bias_index(b):
            return b if b < 8 else (9 if b < 12 else 11)

        def route(dve, need, own, tt):
            V = nc.vector
            need(rt_pe, 0)
            own(V.tensor_copy(rt[:, :, :], O[:, 0:60].rearrange("p (t n) -> p t n", t=TILES)))
            gl, el = rt[:, :, 0:4], rt[:, :, 4:20]

            def b4(c):
                return c.to_broadcast([P, TILES, 4])


            def first_max(values, mx, eq):
                own(V.tensor_reduce(mx, values, AX, ALU.max))
                own(tt(eq, values, b4(mx), ALU.is_equal))
                own(tt(eq, eq, order[:, :].unsqueeze(1).to_broadcast([P, TILES, 4]), ALU.mult))
                own(V.tensor_reduce(rw[:, :, 7:8], eq, AX, ALU.max))
                own(tt(eq, eq, b4(rw[:, :, 7:8]), ALU.is_equal))

            gsel, sel1, sel2 = rw[:, :, 16:20], rw[:, :, 20:24], rw[:, :, 24:28]
            gmax, m1, m2 = rw[:, :, 5:6], rw[:, :, 6:7], rw[:, :, 13:14]
            first_max(gl, gmax, gsel)
            own(tt(rw[:, :, 8:12], gl, b4(gmax), ALU.subtract))
            prod = rw[:, :, 32:48].rearrange("p t (g e) -> p t g e", g=4)
            for t in range(TILES):
                own(tt(prod[:, t], el[:, t].rearrange("p (g e) -> p g e", g=4),
                       gsel[:, t].unsqueeze(2).to_broadcast([P, 4, 4]), ALU.mult))
                own(V.tensor_reduce(rw[:, t, 28:32], prod[:, t].rearrange("p g e -> p e g"), AX, ALU.add))
            eg = rw[:, :, 28:32]
            first_max(eg, m1, sel1)
            own(V.tensor_scalar(rw[:, :, 48:52], sel1, NEG, None, ALU.mult))
            own(tt(rw[:, :, 48:52], rw[:, :, 48:52], eg, ALU.add))
            first_max(rw[:, :, 48:52], m2, sel2)
            rt_dve.of(tt(rw[:, :, 12:13], m2, m1, ALU.subtract))
            need(rt_act, 0)
            own(V.tensor_reduce(rw[:, :, 14:15], rw[:, :, 0:4], AX, ALU.add))
            own(V.tensor_scalar(rw[:, :, 15:16], rw[:, :, 4:5], 1.0, 2.0, ALU.add, ALU.mult))
            own(tt(rw[:, :, 14:15], rw[:, :, 14:15], rw[:, :, 15:16], ALU.mult))
            own(V.reciprocal(rw[:, :, 15:16], rw[:, :, 14:15]))
            own(tt(sel2, sel2, b4(rw[:, :, 4:5]), ALU.mult))
            own(tt(sel1, sel1, sel2, ALU.add))
            own(tt(sel1, sel1, b4(rw[:, :, 15:16]), ALU.mult))
            for t in range(TILES):
                own(tt(gate[:, t, :].rearrange("p (g e) -> p g e", g=4), gsel[:, t].unsqueeze(2).to_broadcast([P, 4, 4]),
                       sel1[:, t].unsqueeze(1).to_broadcast([P, 4, 4]), ALU.mult))
            gate_dve.of(V.memset(dummy[:, 3:4], 0.0))

        block = ctx.enter_context(nc.Block())

        @block.sync
        def _(sp):
            rows = a["tokens"]
            for dst, src in ((ident[:, :], a["ident"]), (tri[:, :, :], a["tri"]), (cmask[:, :, :], a["cmask"]),
                             (rope_t[:, :, :], a["rope"]), (cond[:, :, :], a["cond"]),
                             (order[:, :], a["order"]), (x[:, 0, :], rows[0]), (x[:, 1, :], rows[1]), (x[:, 2, :], rows[2])):
                sp.dma_start(dst, src).then_inc(const_in, 16)
            with sp.Fori(0, DEPTH) as l:
                def need(s, i):
                    sp.wait_ge(s.handle, s.value(l, i))

                def needs(*pairs):
                    for s, i in pairs:
                        sp.wait_ge(s.handle, s.value(l, i))

                gs = [None if s[0] == "mod" else s[1] for s in STREAM]

                def released(p):
                    if p < 0:
                        need(hi_done, p)
                        need(lo_done, p)
                    elif gs[p] is None:
                        need(mod_pe, STREAM[p][1])
                    else:
                        need(hi_done, gs[p])
                        need(lo_done, gs[p])

                def load(p):
                    w_in[p % RAW].of(sp.dma_start(raw[:, p % RAW, :], a["units"][bass.ds(l * NU + p, 1), :, :]
                                                  .rearrange("a p n -> p (a n)")))

                def layer_of(name, n=1):
                    return a[name][bass.ds(l, 1)]

                for p in range(RAW):
                    released(p - RAW)
                    load(p)
                need(layer_end, -1)
                par_in.of(sp.dma_start(pcol[:, :], layer_of("pcol").rearrange("a p n -> p (a n)")))
                par_in.of(sp.dma_start(prow[:, :], layer_of("prow").rearrange("a n -> (a n)").partition_broadcast(P)))
                par_in.of(sp.dma_start(small[:, :, :], layer_of("small").rearrange("a p k n -> p (a k) n")))
                sp.wait_ge(const_in, 16 * NCONST)
                x_saved.of(sp.dma_start(a["x_scratch"].rearrange("t p n -> p t n"), x))
                ct_in.of(sp.dma_start(cT[:, :, :], layer_of("state_C").rearrange("a p h n -> p (a h) n")))
                p = 0
                for s in SCHEDULE:
                    if s[0] in ("mod", "gemm"):
                        if p + RAW < len(STREAM) + EU:
                            released(p)
                            load(p + RAW)
                        p += 1
                    elif s == ("dma", "outB"):
                        for w, n in (("k", "Bk"), ("v", "Bv")):
                            need(*evacuated(CHUNK_NO[n], 2))
                            kv_out["B"].of(sp.dma_start(out["nat_" + w][bass.ds(l, 1)].rearrange("a p n -> p (a n)"),
                                                        slot[n][:, 2, :]))
                    elif s == ("dma", "outC"):
                        need(*evacuated(CHUNK_NO["Ckv"], 2))
                        for w, o in (("k", 0), ("v", 128)):
                            kv_out["C"].of(sp.dma_start(out["swa_" + w][bass.ds(l, 1)].rearrange("a p n -> p (a n)"),
                                                        Ckv[:, 2, o:o + 128]))
                    elif s == ("dma", "outD"):
                        for w, n in (("k", "Dk"), ("v", "Dv")):
                            need(*evacuated(CHUNK_NO[n], 2))
                            kv_out["D"].of(sp.dma_start(out["diff_" + w][bass.ds(l, 1)].rearrange("a p n -> p (a n)"),
                                                        slot[n][:, 2, :]))
                    elif s[0] == "m3" and MU[s[1]][1] == 2:
                        d = MU[s[1]][0]
                        need(mc_act, d)
                        m_out.of(sp.dma_start(out["C"][bass.ds(l * 2 + d, 1)].rearrange("a h v k -> v (a h) k"),
                                              cst.rearrange("p (h k) -> p h k", h=H_A)))
                        m_out.of(sp.dma_start(out["n"][bass.ds(l * 2 + d, 1)], nrow[0:1, d, :]))
                        need(mh_dve, s[1])
                        m_out.of(sp.dma_start(out["m"][bass.ds(l * 2 + d, 1)], mst[0:1, 8 + 4 * d:12 + 4 * d]))
                    elif s[0] == "dma" and s[1] in ("loadB", "keysC", "keysD"):
                        ty = s[1][-1]
                        i = "BCD".index(ty)
                        if i:
                            need(sc_pe, 12 * i - 1)
                        keys_in.of(sp.dma_start(kT[:, :, 384:512], a["keys"][bass.ds(l * 3 + i, 1)]
                                                .rearrange("a p j n -> p (a j) n")))
                        if i == 0:
                            need(m3_pe, 3)
                            vals_in.of(sp.dma_start(vc[:, :], a["vals"][bass.ds(l * 3 + i, 1)]
                                                    .rearrange("a p n -> p (a n)")))
                            need(bz_pool, 0)
                            load_bias(sp, need, l, 0)
                    elif s[0] == "dma" and s[1] in ("valuesC", "valuesD"):
                        i = "BCD".index(s[1][-1])
                        need(pv_pe, 12 * i - 1)
                        vals_in.of(sp.dma_start(vc[:, :], a["vals"][bass.ds(l * 3 + i, 1)]
                                                .rearrange("a p n -> p (a n)")))
                    elif s[0] == "sc" and s[1] in BIASED:
                        b = BIASED.index(s[1])
                        if b < 8 or b == 11:
                            need(sa_dve, b)
                            load_bias(sp, need, l, b + 1)
                    elif s[0] == "gt":
                        i = s[1]
                        need(gr_act, i)
                        g_out.of(sp.dma_start(a["g_scratch"][i], grow[:, :]))
                    elif s == ("dma", "gate1") or s == ("dma", "gate2"):
                        i = int(s[1][-1]) - 1
                        if i == 0:
                            needs((g_out, i), (pv_pe, 23))
                        else:
                            needs((g_out, i), evacuated(CHUNK_NO["wout", 1], 2))
                        for c in range(2):
                            src = a["g_scratch"][i].rearrange("(j c) n -> c j n", c=2)[c]
                            g_in.of(sp.dma_start(gbc[:, c, :].rearrange("p (j n) -> p j n", j=KD),
                                                 bass.AP(src.tensor, src.offset, [[0, P], [2 * P, KD], [1, P]])))
                    elif s == ("dma", "loadX"):
                        needs((kv_out["D"], 1), (th_act, 7))
                        x_in.of(sp.dma_start(x, a["x_scratch"].rearrange("t p n -> p t n")))
                    elif s == ("experts",):
                        with sp.Fori(0, NEXP - 1) as e:
                            for i in range(EU):
                                k = NG + i
                                sp.wait_ge(hi_done.handle, hi_done.value(l, k) + e * EU)
                                sp.wait_ge(lo_done.handle, lo_done.value(l, k) + e * EU)
                                w_in[i].of(sp.dma_start(
                                    raw[:, i, :], a["units"][bass.ds(l * NU + e * EU + (len(STREAM) + EU + i), 1), :, :]
                                    .rearrange("a p n -> p (a n)")))
                        for i in range(EU):
                            w_in[i].n += NEXP - 2
            sp.wait_ge(layer_end.handle, DEPTH + 1)
            sp.dma_start(yacc[:, 0, :], a["norm_final"].partition_broadcast(P)).then_inc(fin_gain_in, 16)
            for t in range(TILES):
                sp.wait_ge(fin_y_dve, t + 1)
                sp.dma_start(out["tokens"][t], xn[:, t, :]).then_inc(fin_out, 16)
            sp.wait_ge(fin_out, 16 * TILES)
            for s, n in ((kv_out["B"], 2), (kv_out["C"], 2), (kv_out["D"], 2), (m_out, 6), (x_saved, 1), (g_out, 2)):
                sp.wait_ge(s.handle, 16 * n * DEPTH)

        @block.gpsimd
        def _(pool):
            pool.memset(ones[:, :], 1.0).then_inc(start_dve, 1)
            for i, v in enumerate((-0.5, 1.0 / D, 1.0 / P, EPS, 0.5)):
                pool.memset(cval[:, i, :], v).then_inc(start_dve, 1)
            pool.memset(ms[:, :, :], 0.0).then_inc(start_dve, 1)
            pool.memset(zst[:, :], 0.0).then_inc(start_dve, 1)
            pool.memset(dummy[:, 0:1], 0.0).then_inc(lo_done.handle, RAW)
            with pool.Fori(0, DEPTH) as l:
                chain = [0]

                def need(s, i):
                    pool.wait_ge(s.handle, s.value(l, i))

                def own(ins):
                    pool_ord.of(ins)
                    chain[0] += 1
                    need(pool_ord, chain[0] - 1)

                def split(g):
                    need(hi_done, g)
                    k = g % CONV
                    lo_done.of(nc.gpsimd.tensor_tensor(wlo[:, k, :], raw[:, POS_OF[g] % RAW, :], whi[:, k, :].bitcast(F32),
                                                       ALU.subtract))

                def rstd(dst, src, n, width, signal):
                    own(nc.gpsimd.tensor_tensor(dst, src, cval[:, 1 if n == D else 2, 0:width], ALU.mult))
                    own(nc.gpsimd.tensor_tensor(dst, dst, cval[:, 3, 0:width], ALU.add))
                    return nc.gpsimd.tensor_tensor(dst, dst, cval[:, 0, 0:width], ALU.pow)

                first = True
                for s in SCHEDULE:
                    if s[0] == "norm":
                        need(sq_act, 3 * s[1] + 2)
                        if first:
                            pool.wait_ge(start_dve, 6)
                            first = False
                        rstd_pool.of(rstd(st[:, 0:3], st[:, 0:3], D, 3, None))
                        if s[1] == 0:
                            split(0)
                            split(1)
                    elif s[0] == "gemm":
                        g = s[1]
                        if g + 2 < NG:
                            split(g + 2)
                        c, i, n = GEMM[g]
                        kind, arg = CHUNKS[c][:2]
                        if i == n - 1 and kind == "branch" and arg[0] > 0:
                            for t in range(TILES):
                                need(*evacuated(c, t))
                                ev_pool.of(nc.gpsimd.tensor_tensor(merged[arg[1]][:, t, :], merged[arg[1]][:, t, :],
                                                                   sig[:, t, :], ALU.add))
                        if i == n - 1 and kind == "wout":
                            for t in range(TILES):
                                need(*evacuated(c, t))
                                xs = x[:, t, arg * 512:(arg + 1) * 512]
                                ev_pool.of(nc.gpsimd.tensor_tensor(xs, xs, sig[:, t, :], ALU.add))
                    elif s[0] == "m1":
                        m = s[1]
                        d, t = MU[m]
                        need(cc_dve, 0)
                        if m:
                            need(m1_pe, m - 1)
                        dv = bias[:, :, :].rearrange("p a n -> p (a n)")[:, 0:512].rearrange("p (h n) -> p h n", h=4)
                        diag_pool.of(nc.gpsimd.tensor_tensor(
                            dv, ident[:, :].unsqueeze(1).to_broadcast([P, 4, P]),
                            cc[:, t, 4 * d:4 * d + 4].unsqueeze(2).to_broadcast([P, 4, P]), ALU.mult))
                    elif s[0] == "m2" and s[1] in MUPD:
                        m = s[1]
                        d, t = MU[m]
                        need(mexp_act, m)
                        need(*evacuated(CHUNK_NO["Ak"], t))
                        if m:
                            need(m3_pe, m - 1)
                        kw_pool.of(nc.gpsimd.tensor_tensor(
                            vc[:, :].rearrange("p (h n) -> p h n", h=4),
                            slot["Ak"][:, t, :].rearrange("p (h n) -> p h n", h=4),
                            ms[:, m % 2, 24:28].unsqueeze(2).to_broadcast([P, 4, P]), ALU.mult))
                    elif s == ("dma", "loadB"):
                        need(m1_pe, len(MU) - 1)
                        wide1 = ones[:, :].unsqueeze(1).to_broadcast([P, 2, P])
                        bz_pool.of(nc.gpsimd.tensor_tensor(bias[:, :, T_LAT:], wide1, wide1, ALU.subtract))
                    elif s[0] == "hn":
                        i = s[1]
                        need(hs_dve, 3 * i + 2)
                        own(rstd(st[:, 3:15], st[:, 3:15], P, 12, None))
                        f = cval[:, 4, :] if i == 0 else row("lam", 1, 2).to_broadcast([P, 12])
                        hr_pool.of(nc.gpsimd.tensor_tensor(st[:, 3:15], st[:, 3:15], f, ALU.mult))
                    elif s == ("route",):
                        need(th_act, 7)
                        need(mt_pe, 7)
                        nc.gpsimd.tensor_tensor(dummy[:, 0:1], ones[:, 0:1], ones[:, 0:1], ALU.mult)
                        yz_pool.of(nc.gpsimd.memset(yacc, 0.0))
                    elif s == ("experts",):
                        def low(e, p):
                            k = NG + 2 + p
                            pool.wait_ge(hi_done.handle, hi_done.value(l, k) + e * EU)
                            lo_done.of(nc.gpsimd.tensor_tensor(wlo[:, (2 + p) % CONV, :], raw[:, (2 + p) % RAW, :],
                                                               whi[:, (2 + p) % CONV, :].bitcast(F32), ALU.subtract))

                        low(0, -2)
                        low(0, -1)
                        with pool.Fori(0, NEXP - 1) as e:
                            for p in range(EU):
                                low(e, p)
                        for p in range(4):
                            low(NEXP - 1, p)
                        lo_done.n += (NEXP - 2) * EU

            pool.wait_ge(fin_sq_act, TILES)
            nc.gpsimd.tensor_scalar(st[:, 0:3], st[:, 0:3], 1.0 / D, EPS, ALU.mult, ALU.add).then_inc(fin_rstd_pool, 1)
            pool.wait_ge(fin_rstd_pool, 1)
            nc.gpsimd.tensor_tensor(st[:, 0:3], st[:, 0:3], cval[:, 0, 0:3], ALU.pow).then_inc(fin_rstd_pool, 1)

        @block.scalar
        def _(act):
            act.wait_ge(const_in, 16 * NCONST)
            nc.scalar.activation(cond_t, cond[:, :, :], ACT.Tanh, scale=0.5).then_inc(cond_act, 1)
            nc.scalar.activation(dummy[:, 1:2], ident[:, 0:1], ACT.Copy).then_inc(hi_done.handle, RAW)
            with act.Fori(0, DEPTH) as l:
                chain = [0]

                def need(s, i):
                    act.wait_ge(s.handle, s.value(l, i))

                def own(ins):
                    act_ord.of(ins)
                    chain[0] += 1
                    need(act_ord, chain[0] - 1)

                def split(g):
                    p = POS_OF[g]
                    w = w_in[p % RAW]
                    act.wait_ge(w.handle, w.value(l, p // RAW))
                    if g >= CONV:
                        need(*unit_done(g - CONV))
                    hi_done.of(nc.scalar.activation(whi[:, g % CONV, :], raw[:, p % RAW, :], ACT.Copy))

                def small_out(i, w):
                    need(sp_pe, i)
                    sp_act.of(nc.scalar.activation(prob[0:w, 0, 0, :], O[0:w, 0:384], ACT.Copy))

                need(par_in, 2)
                smh_act.of(nc.scalar.activation(smhi[:, :, :], small[:, :, :], ACT.Copy))
                need(lam_dve, 0)
                lam_act.of(nc.scalar.activation(lam[:, 2:4], lam[:, 0:2], ACT.Exp))
                for s in SCHEDULE:
                    if s[0] == "norm":
                        w = s[1]
                        if w == 0:
                            act.wait_ge(layer_end.handle, layer_end.value(l, -1))
                        else:
                            need(kv_out["B"], 1)
                        for t in range(TILES):
                            if w == 1:
                                need(ev_pool, pooled(CHUNK_NO["wout", 1], t))
                            sq_act.of(nc.scalar.activation(xn[:, t, :], x[:, t, :], ACT.Square,
                                                           accum_out=st[:, t:t + 1]))
                        if w == 0:
                            split(0)
                            split(1)
                        for c in range(KD):
                            need(hf_dve, KD * w + c)
                            hh_act.of(nc.scalar.activation(hhi[:, c, :], probT[:, c % 2, 0, :], ACT.Copy))
                    elif s[0] == "gemm":
                        g = s[1]
                        if g + 2 < NG:
                            split(g + 2)
                        c, i, n = GEMM[g]
                        kind, arg = CHUNKS[c][:2]
                        if i == n - 1 and kind in ("proj", "gate"):
                            for t in range(TILES):
                                need(tile_pe, TILES * c + t)
                                if kind == "gate":
                                    if CHUNKS[c - 1][0] == "proj":
                                        need(rope_dve, 8)
                                    if c >= 14 and CHUNKS[c - 1][0] == "branch":
                                        cb = c - 1
                                        if CHUNKS[cb][1][0] > 0:
                                            need(ev_pool, pooled(cb, t))
                                        else:
                                            need(*evacuated(cb, t))
                                    ev_act.of(nc.scalar.activation(sig[:, t, :], G[:, t, :], ACT.Tanh, scale=0.5))
                                else:
                                    w = CHUNKS[c][2]
                                    if arg == "Aq" and t == 0:
                                        need(x_saved, 0)
                                    if t == 0 and arg == "Dq":
                                        need(m3_pe, 3)
                                    if t == 0 and arg == "Dk":
                                        need(m3_pe, 5)
                                    if t == 0 and arg == "Dv":
                                        need(to_pe, 3)
                                    ev_act.of(nc.scalar.activation(
                                        slot[arg][:, t, :], G[:, t, 0:w], ACT.Copy,
                                        scale=DH_A ** -0.5 if arg == "Ak" else 1.0))
                    elif s[0] == "modv":
                        g = s[1]
                        need(mod_pe, KD * g + KD - 1)
                        if g:
                            need(modt_pe, g - 1)
                        if g == 2:
                            need(tp_pe, TP_NO["C", "k", 1])
                        mod_act.of(nc.scalar.activation(mrow, O[:, 256:512], ACT.Copy))
                    elif s == ("mgate",):
                        small_out(0, 16)
                        need(mg_dve, 0)
                        own(nc.scalar.activation(ga[:, :, :], ga[:, :, :], ACT.Exp))
                        ln_act.of(nc.scalar.activation(ga[:, :, :], ga[:, :, :], ACT.Ln, bias=1.0))
                    elif s[0] == "tp":
                        ty, w, j = s[1:]
                        i = TP_NO[ty, w, j]
                        need(tp_pe, i)
                        if w == "q":
                            tp_act.of(nc.scalar.activation(qT[:, j, :], T[:, i % 2, 0:384], ACT.Copy,
                                                           scale=1.0 if ty == "A" else 64 ** -0.5))
                        else:
                            tp_act.of(nc.scalar.activation(kT[:, j, 0:384], T[:, i % 2, 0:384], ACT.Copy))
                    elif s[0] == "m1":
                        m = s[1]
                        need(mmax_dve, m)
                        W = prob[:, m % 2].rearrange("p a n -> p (a n)")
                        for h in range(4):
                            nc.scalar.activation(W[:, h * P:(h + 1) * P], W[:, h * P:(h + 1) * P], ACT.Exp,
                                                 bias=ms[:, m % 2, 8 + h:9 + h])
                        mexp_act.of(nc.scalar.activation(ms[:, m % 2, 16:32], ms[:, m % 2, 32:48], ACT.Exp))
                    elif s[0] == "m2":
                        m = s[1]
                        need(m2_pe, m)
                        sT_act.of(nc.scalar.activation(probT[:, m % 2].rearrange("p a n -> p (a n)")[:, 0:512],
                                                       T[:, 0, :], ACT.Copy))
                    elif s[0] == "m3" and MU[s[1]][1] == 2:
                        m = s[1]
                        d = MU[m][0]
                        need(m3_pe, m)
                        if d:
                            need(m_out, 2)
                        nc.scalar.activation(nrow[0:1, d, :], S[0:1, 0, :], ACT.Copy)
                        mc_act.of(nc.scalar.activation(cst, T[:, 0, :], ACT.Copy))
                    elif s[0] == "sc":
                        u = s[1]
                        ty, t, j = AU[u]
                        need(nm_dve, u)
                        w = 384 if t < 2 else 128
                        for m in range(2):
                            src = prob[:, u % 2, m, 0:w] if u in BIASED else S[:, m, 0:w]
                            e = nc.scalar.activation(prob[:, u % 2, m, 0:w], src, ACT.Exp,
                                                     bias=am[:, u % 2, m:m + 1], accum_out=am[:, u % 2, 2 + m:3 + m])
                        if ty == "C":
                            e = nc.scalar.activation(am[:, u % 2, 6:8], am[:, u % 2, 4:6], ACT.Exp)
                        ex_act.of(e)
                    elif s[0] == "pt":
                        u = s[1]
                        w = 384 if AU[u][1] < 2 else 128
                        need(pt_pe, u)
                        pa_act.of(nc.scalar.activation(probT[:, u % 2, 0, 0:w], T[:, 0, 0:w], ACT.Copy))
                    elif s[0] == "pv":
                        u = s[1]
                        ty, t, j = AU[u]
                        need(pv_pe, u)
                        if ty == "D":
                            yd_act.of(nc.scalar.activation(slot["Dq"][:, t, j * P:(j + 1) * P], O[:, 0:P], ACT.Copy))
                        else:
                            n = TYPES.index(ty)
                            if u == 12:
                                need(kv_out["B"], 1)
                            oh_act.of(nc.scalar.activation(bhi[n][:, j, t * P:(t + 1) * P], O[:, 0:P], ACT.Copy))
                    elif s == ("hn", 0):
                        need(mh_dve, len(MU) - 1)
                        need(*evacuated(CHUNK_NO["Ao"], 2))
                        tanh_act.of(nc.scalar.activation(slot["Ao"], slot["Ao"], ACT.Tanh, scale=0.5))
                    elif s[0] == "to":
                        i, j = s[1:]
                        need(to_pe, 4 * i + j)
                        if (i, j) == (1, 0):
                            need(*unit_done(LAST_UNIT[CHUNK_NO["branch", (0, 1)]]))
                        th_act.of(nc.scalar.activation(bhi[0][:, j, :], T[:, j % 2, 0:384], ACT.Copy))
                    elif s[0] == "gt":
                        need(gt_pe, s[1])
                        if s[1]:
                            need(g_out, 0)
                        gr_act.of(nc.scalar.activation(grow[:, :], T[0:16, 1, 0:P], ACT.Copy))
                    elif s[0] == "mt":
                        c = s[1]
                        need(mt_pe, c)
                        mh_act.of(nc.scalar.activation(hhi[:, c, :], T[:, c % 2, 0:384], ACT.Copy, scale=0.5))
                    elif s == ("route",):
                        small_out(1, 20)
                        need(rt_dve, 0)
                        rt_act.of(nc.scalar.activation(rw[:, :, 0:5], rw[:, :, 8:13], ACT.Exp))
                    elif s == ("experts",):
                        def high(e, p):
                            n = len(STREAM) + 2 + p
                            w = w_in[n % RAW]
                            act.wait_ge(w.handle, w.value(l, n // RAW) + e * 16)
                            hi_done.of(nc.scalar.activation(whi[:, (2 + p) % CONV, :], raw[:, n % RAW, :], ACT.Copy))

                        def one_expert(e, last):
                            def eneed(sgl, n, k):
                                act.wait_ge(sgl.handle, (l * NEXP + e) * n + (k + 1 + sgl.credit))

                            eneed(e_unit, 3, 1)
                            high(e, 0)
                            eneed(e_down, 6, -1)
                            high(e, 1)
                            high(e, 2)
                            eneed(e_unit, 3, 2)
                            high(e, 3)
                            for t in range(TILES):
                                eneed(e_tile, 3, t)
                                e_tanh.of(nc.scalar.activation(gact[:, t, :], G[:, t, 0:DEXP], ACT.Tanh, scale=0.5))
                            if not last:
                                high(e, 4)
                                eneed(e_unit, 3, 3)
                                high(e, 5)
                            for f in range(2):
                                eneed(e_pt, 2, f)
                                e_hh.of(nc.scalar.activation(ehi[:, f, :], T[:, f, 0:384], ACT.Copy))

                        need(*unit_done(NG - 3))
                        high(0, -2)
                        need(*unit_done(NG - 2))
                        high(0, -1)
                        with act.Fori(0, NEXP - 1) as e:
                            one_expert(e, False)
                        one_expert(NEXP - 1, True)
                        hi_done.n += (NEXP - 2) * EU
            act.wait_ge(layer_end.handle, DEPTH + 1)
            for t in range(TILES):
                nc.scalar.activation(xn[:, t, :], x[:, t, :], ACT.Square, accum_out=st[:, t:t + 1])\
                    .then_inc(fin_sq_act, 1)

        @block.tensor
        def _(pe):
            pe.wait_ge(const_in, 16 * NCONST)
            nc.tensor.transpose(T[:, 0, 0:P], ident[:, :], ident[:, :]).then_inc(unit_pe.handle, CONV)
            nc.tensor.transpose(T[:, 0, 1*P:2*P], ident[:, :], ident[:, :]).then_inc(e_tile.handle, 3)
            nc.tensor.transpose(T[:, 0, 2*P:3*P], ident[:, :], ident[:, :]).then_inc(e_down.handle, 6)
            nc.tensor.transpose(T[:, 0, 3*P:4*P], ident[:, :], ident[:, :]).then_inc(e_unit.handle, 3)
            pe.wait_ge(start_dve, 1)
            pe.wait_ge(cond_dve, 2)
            with pe.Fori(0, DEPTH) as l:
                passed = {}

                def need(s, i):
                    if i > passed.get(s.name, -1):
                        passed[s.name] = i
                        pe.wait_ge(s.handle, s.value(l, i))

                read = {b: None for b in ("S0", "S1", "T0", "T1", "O")}

                def free(*banks):
                    for b in banks:
                        if read[b] is not None:
                            need(*read[b])

                def three(dst, st_hi, st_lo, mv_hi, mv_lo, start, stop):
                    nc.tensor.matmul(dst, st_hi, mv_hi, start=start, stop=False)
                    nc.tensor.matmul(dst, st_hi, mv_lo, start=False, stop=False)
                    return nc.tensor.matmul(dst, st_lo, mv_hi, start=False, stop=stop)

                pe.wait_ge(e_y.handle, l * (6 * NEXP) + 6)
                for s in SCHEDULE:
                    if s[0] == "mod":
                        j = s[1]
                        p = MODPOS[j]
                        w = w_in[p % RAW]
                        pe.wait_ge(w.handle, w.value(l, p // RAW))
                        free("O")
                        for k in range(KD):
                            r0, c0 = 32 * (j % 4), 256 + P * (j % KD // 4)
                            mm = nc.tensor.matmul(O[r0:r0 + 32, c0:c0 + P], cond[:, k, :],
                                                  raw[:, p % RAW, k * P:(k + 1) * P],
                                                  start=(k == 0), stop=(k == KD - 1))
                        mod_pe.of(mm)
                    elif s[0] == "modv":
                        read["O"] = (mod_act, s[1])
                    elif s[0] == "modt":
                        need(mod_act, s[1])
                        free("T1")
                        for b in range(2):
                            mm = nc.tensor.transpose(T[:, 1, b * P:(b + 1) * P], mrow[:, b * P:(b + 1) * P], ident[:, :])
                        modt_pe.of(mm)
                        read["T1"] = (mod_dve, s[1])
                    elif s[0] == "norm":
                        w = s[1]
                        need(xn_dve, 3 * w + 2)
                        for c in range(KD):
                            free(f"T{c % 2}")
                            for t in range(TILES):
                                mm = nc.tensor.transpose(T[:, c % 2, t * P:(t + 1) * P], xn[:, t, c * P:(c + 1) * P],
                                                         ident[:, :])
                            nt_pe.of(mm)
                            read[f"T{c % 2}"] = (hf_dve, KD * w + c)
                        need(hl_dve, KD * w + KD - 1)
                    elif s[0] == "gemm":
                        g = s[1]
                        c, i, n = GEMM[g]
                        kind, arg, width, _ = CHUNKS[c]
                        ku = 1024 // width
                        need(lo_done, g)
                        if i == 0 and kind == "branch":
                            need(*((tl_dve, 3), (ol_dve, 11), (ol_dve, 23), (tl_dve, 7))[arg[0]])
                        for t in range(TILES):
                            if i == 0 and c > 0:
                                need(*evacuated(c - 1, t))
                            for k in range(ku):
                                kk = i * ku + k
                                if kind == "branch":
                                    hi_, lo_ = bhi[arg[0] % 3], blo[arg[0] % 3]
                                else:
                                    hi_, lo_ = hhi, hlo
                                if kind == "wout" and arg == 0 and t == 0:
                                    need(ml_dve, kk)
                                mm = three(G[:, t, 0:width], hi_[:, kk, t * P:(t + 1) * P], lo_[:, kk, t * P:(t + 1) * P],
                                           whi[:, g % CONV, k * width:(k + 1) * width],
                                           wlo[:, g % CONV, k * width:(k + 1) * width],
                                           i == 0 and k == 0, i == n - 1 and k == ku - 1)
                            if i == n - 1:
                                tile_pe.of(mm)
                        if i < n - 1:
                            unit_pe.of(mm)
                    elif s == ("mgate",) or s == ("route",):
                        i, lo, w = (0, 0, 16) if s == ("mgate",) else (1, 16, 20)
                        need(sml_dve, 0)
                        free("O")
                        for k in range(KD):
                            mm = three(O[0:w, 0:384], smhi[:, k, lo:lo + w], smlo[:, k, lo:lo + w], hhi[:, k, :],
                                       hlo[:, k, :], k == 0, k == KD - 1)
                        sp_pe.of(mm)
                        need(sp_act, i)
                        for t in range(TILES):
                            mm = nc.tensor.matmul(O[:, t * w:(t + 1) * w], prob[0:w, 0, 0, t * P:(t + 1) * P],
                                                  ident[0:w, 0:w], start=True, stop=True)
                        if w == 16:
                            mg_pe.of(mm)
                            read["O"] = (mg_dve, 0)
                        else:
                            rt_pe.of(mm)
                    elif s == ("mcum",):
                        need(lf_dve, 0)
                        free("O")
                        for t in range(TILES):
                            o = 64 + 16 * t
                            nc.tensor.matmul(O[:, o:o + 4], tri[:, 0, :], lf[:, t, 0:4], start=True, stop=True)
                            nc.tensor.matmul(O[:, o + 4:o + 8], tri[:, 1, :], lf[:, t, 4:8], start=True, stop=True)
                            mm = nc.tensor.matmul(O[:, o + 8:o + 16], ones[:, :], lf[:, t, :], start=True, stop=True)
                        mb_pe.of(mm)
                        read["O"] = (cc_dve, 0)
                    elif s[0] == "tp":
                        ty, w, j = s[1:]
                        i = TP_NO[ty, w, j]
                        if ty in "AB":
                            need(*evacuated(CHUNK_NO[ty + w], 2))
                            src = slot[ty + w]
                        else:
                            if ty == "C":
                                need(rope_dve, 4)
                                if w == "q":
                                    need(*evacuated(CHUNK_NO["Cq"], 2))
                            else:
                                need(rope_dve, 8)
                                need(*evacuated(CHUNK_NO["D" + w], 2))
                            src = slot[ty + w] if (ty, w) != ("C", "k") else None
                        free(f"T{i % 2}")
                        for t in range(TILES):
                            blk = src[:, t, j * P:(j + 1) * P] if src is not None else \
                                kdup[:, t, j, :, :].rearrange("p a n -> p (a n)")
                            mm = nc.tensor.transpose(T[:, i % 2, t * P:(t + 1) * P], blk, ident[:, :])
                        tp_pe.of(mm)
                        read[f"T{i % 2}"] = (tp_act, i)
                    elif s[0] == "m1":
                        m = s[1]
                        d, t = MU[m]
                        need(diag_pool, m)
                        need(tp_act, 7)
                        free("S0", "S1")
                        nc.tensor.matmul(S[:, 0, :], ones[:, :], bias[:, :, :].rearrange("p a n -> p (a n)")[:, 0:512],
                                         start=True, stop=True)
                        for h in range(4):
                            mm = nc.tensor.matmul(S[:, 1, h * P:(h + 1) * P], qT[:, h, t * P:(t + 1) * P],
                                                  kT[:, h, t * P:(t + 1) * P], start=True, stop=True)
                        m1_pe.of(mm)
                        read["S0"], read["S1"] = (mmax_dve, m), (ms_dve, m)
                    elif s[0] == "m2":
                        m = s[1]
                        d, t = MU[m]
                        W = prob[:, m % 2].rearrange("p a n -> p (a n)")
                        need(ms_dve, m)
                        free("S0", "T0", "O")
                        if t < 2:
                            if m < 2:
                                need(ct_in, 0)
                                need(par_in, 2)
                            else:
                                need(ct_dve, MU.index((d, 1 - t)))
                            nv = pcol[:, PC_N:PC_N + 8]
                            for h in range(4):
                                q = qT[:, h, t * P:(t + 1) * P]
                                nc.tensor.matmul(S[:, 0, h * P:(h + 1) * P], q, cT[:, 4 * d + h, :], start=True, stop=True)
                                nc.tensor.matmul(O[:, 4 + h:5 + h], q, nv[:, 4 * d + h:4 * d + h + 1],
                                                 start=True, stop=True)
                        for h in range(4):
                            mm = nc.tensor.transpose(T[:, 0, h * P:(h + 1) * P], W[:, h * P:(h + 1) * P], ident[:, :])
                        m2_pe.of(mm)
                        read["T0"] = (sT_act, m)
                    elif s[0] == "m3":
                        m = s[1]
                        d, t = MU[m]
                        sT = probT[:, m % 2].rearrange("p a n -> p (a n)")
                        need(sT_act, m)
                        need(*evacuated(CHUNK_NO["Av"], t))
                        free("T0", "T1")
                        if m in MUPD:
                            need(kw_pool, m)
                        for h in range(4):
                            v = slot["Av"][:, t, h * P:(h + 1) * P]
                            st_ = sT[:, h * P:(h + 1) * P]
                            nc.tensor.matmul(T[:, 1, h * P:(h + 1) * P], st_, v, start=True, stop=True)
                            mm = nc.tensor.matmul(O[:, h:h + 1], st_, ones[:, 0:1], start=True, stop=True)
                            if m in MUPD:
                                kw = vc[:, h * P:(h + 1) * P]
                                if t < 2:
                                    nc.tensor.matmul(T[:, 0, h * P:(h + 1) * P], kw, v, start=True, stop=True)
                                    mm = nc.tensor.matmul(O[:, 8 + h:9 + h], kw, ones[:, 0:1], start=True, stop=True)
                                else:
                                    mm = nc.tensor.matmul(T[:, 0, h * P:(h + 1) * P], v, kw, start=True, stop=True)
                        if m in MUPD and t == 2:
                            mm = nc.tensor.matmul(S[0:1, 0, :], ones[:, 0:1], vc[:, :], start=True, stop=True)
                        m3_pe.of(mm)
                        read["T1"] = read["O"] = read["S0"] = (mh_dve, m)
                        if m in MUPD:
                            read["T0"] = (ct_dve, m) if t < 2 else (mc_act, d)
                            if t == 2:
                                read["S0"] = (mc_act, d)
                            else:
                                read["O"] = (ct_dve, m)
                    elif s[0] == "sc":
                        u = s[1]
                        ty, t, j = AU[u]
                        kj = j // 2 if ty == "C" else j
                        i = "BCD".index(ty)
                        need(tp_act, max(TP_NO[ty, "q", j], TP_NO[ty, "k", kj]))
                        if u % 12 == 0:
                            need(keys_in, i)
                        free("S0", "S1")
                        for m in range(2):
                            r = slice(64 * m, 64 * m + 64)
                            q = qT[r, j, t * P:(t + 1) * P]
                            if t < 2:
                                nc.tensor.matmul(S[:, m, 0:256], q, kT[r, kj, 0:256], start=True, stop=True)
                                mm = nc.tensor.matmul(S[:, m, 256:384], q, kT[r, kj, 384:512], start=True, stop=True)
                            else:
                                mm = nc.tensor.matmul(S[:, m, 0:128], q, kT[r, kj, 256:384], start=True, stop=True)
                        sc_pe.of(mm)
                        read["S0"] = read["S1"] = (sa_dve, BIASED.index(u)) if u in BIASED else (ex_act, u)
                    elif s[0] == "pt":
                        u = s[1]
                        ty, t, j = AU[u]
                        need(pn_dve, u)
                        maps = 1 if ty == "D" else 2
                        free(*("T0", "T1")[0:maps])
                        for m in range(maps):
                            for b in range(3 if t < 2 else 1):
                                mm = nc.tensor.transpose(T[:, m, b * P:(b + 1) * P],
                                                         prob[:, u % 2, m, b * P:(b + 1) * P], ident[:, :])
                        pt_pe.of(mm)
                        read["T0"] = (pa_act, u)
                        if maps == 2:
                            read["T1"] = (pb_dve, u)
                    elif s[0] == "pv":
                        u = s[1]
                        ty, t, j = AU[u]
                        need(pa_act, u)
                        if ty != "D":
                            need(pb_dve, u)
                        if u % 12 == 0:
                            need(vals_in, "BCD".index(ty))
                        free("O")
                        blocks = [0, 1, None] if t < 2 else [2]

                        def values(b, lo, n):
                            if b is None:
                                return vc[:, lo:lo + n]
                            return {"B": slot["Bv"], "C": Ckv[:, :, 128:256], "D": slot["Dv"]}[ty][:, b, lo:lo + n]

                        for m in range(1 if ty == "D" else 2):
                            for i, b in enumerate(blocks):
                                pr = probT[:, u % 2, m, i * P:(i + 1) * P]
                                fl = dict(start=(i == 0), stop=(i == len(blocks) - 1))
                                if ty == "D":
                                    mm = nc.tensor.matmul(O[:, 0:P], pr, values(b, j * P, P), **fl)
                                else:
                                    lo = 64 * (2 * j + m if ty == "B" else j // 2)
                                    mm = nc.tensor.matmul(O[64 * m:64 * m + 64, 0:P], values(b, lo, 64), pr, **fl)
                        pv_pe.of(mm)
                        read["O"] = (yd_act, u - 24) if ty == "D" else (ol_dve, u)
                    elif s[0] == "to":
                        i, j = s[1:]
                        need(hn_dve, 3 * i + 2)
                        free(f"T{j % 2}")
                        for t in range(TILES):
                            mm = nc.tensor.transpose(T[:, j % 2, t * P:(t + 1) * P],
                                                     slot["AD"[i] + "q"][:, t, j * P:(j + 1) * P], ident[:, :])
                        to_pe.of(mm)
                        read[f"T{j % 2}"] = (tl_dve, 4 * i + j)
                    elif s[0] == "gt":
                        need(mod_dve, 2 if s[1] == 0 else 5)
                        free("T1")
                        gt_pe.of(nc.tensor.transpose(T[0:16, 1, 0:P], modc[:, 2 + 3 * s[1], :, :]
                                                     .rearrange("p j c -> p (j c)"), ident[:, :]))
                        read["T1"] = (gr_act, s[1])
                    elif s[0] == "mt":
                        c = s[1]
                        b = CHUNK_NO["branch", (3, c // 4)]
                        need(ev_pool, pooled(b, 2))
                        free(f"T{c % 2}")
                        for t in range(TILES):
                            mm = nc.tensor.transpose(T[:, c % 2, t * P:(t + 1) * P],
                                                     merged[c // 4][:, t, (c % 4) * P:(c % 4 + 1) * P], ident[:, :])
                        mt_pe.of(mm)
                        read[f"T{c % 2}"] = (ml_dve, c)
                    elif s == ("experts",):
                        def gate_up(e, p, u, bank_free):
                            pe.wait_ge(lo_done.handle, lo_done.value(l, NG + 2 + p) + e * EU)
                            k3 = (2 + p) % CONV
                            for t in range(TILES):
                                if bank_free:
                                    bank_free(t)
                                for k in range(2):
                                    kk = 2 * u + k
                                    mm = three(G[:, t, :], hhi[:, kk, t * P:(t + 1) * P], hlo[:, kk, t * P:(t + 1) * P],
                                               whi[:, k3, k * 512:(k + 1) * 512], wlo[:, k3, k * 512:(k + 1) * 512],
                                               kk == 0, kk == KD - 1)
                                if u == 3:
                                    e_tile.of(mm)
                            if u < 3:
                                e_unit.of(mm)

                        def one_expert(e, last):
                            def eneed(sgl, n, k):
                                pe.wait_ge(sgl.handle, (l * NEXP + e) * n + (k + 1 + sgl.credit))

                            gate_up(e, 0, 2, None)
                            gate_up(e, 1, 3, None)
                            if not last:
                                gate_up(e, 2, 0, lambda t: eneed(e_hid, 3, t))
                            eneed(e_hid, 3, 2)
                            for f in range(2):
                                eneed(e_hl, 2, f - 2)
                                for t in range(TILES):
                                    mm = nc.tensor.transpose(T[:, f, t * P:(t + 1) * P], hid[:, t, f * P:(f + 1) * P],
                                                             ident[:, :])
                                e_pt.of(mm)
                            if not last:
                                gate_up(e, 3, 1, None)
                            p = 2 if last else 4
                            pe.wait_ge(lo_done.handle, lo_done.value(l, NG + 3 + p) + e * EU)
                            eneed(e_hl, 2, 1)
                            for q in range(6):
                                t, hf = divmod(q, 2)
                                bank = (S[:, 0, :], S[:, 1, :], O[:, :])[q % 3]
                                eneed(e_y, 6, q - 3)
                                for f in range(2):
                                    k = (2 + p + f) % CONV
                                    mm = three(bank, ehi[:, f, t * P:(t + 1) * P], elo[:, f, t * P:(t + 1) * P],
                                               whi[:, k, hf * 512:(hf + 1) * 512], wlo[:, k, hf * 512:(hf + 1) * 512],
                                               f == 0, f == 1)
                                e_down.of(mm)

                        need(hl_dve, 2 * KD - 1)
                        gate_up(0, -2, 0, lambda t: need(*evacuated(CHUNK_NO["wout", 1], t)))
                        gate_up(0, -1, 1, None)
                        need(gate_dve, 0)
                        free("T0", "T1", "S0", "S1", "O")
                        nc.tensor.transpose(T[:, 0, 384:512], ident[:, :], ident[:, :])
                        with pe.Fori(0, NEXP - 1) as e:
                            one_expert(e, False)
                        one_expert(NEXP - 1, True)

        @block.vector
        def _(dve):
            dve.wait_ge(const_in, 16 * NCONST)
            dve.wait_ge(cond_act, 1)
            nc.vector.scalar_tensor_tensor(cond_t, cond_t, 1.0, cond[:, :, :], ALU.add, ALU.mult)\
                .then_inc(cond_dve, 1)
            dve.wait_ge(cond_dve, 1)
            nc.vector.tensor_scalar(cond[:, :, :], cond_t, 0.5, None, ALU.mult).then_inc(cond_dve, 1)
            nc.vector.memset(dummy[:, 2:3], 0.0).then_inc(layer_end.handle, 1)
            nc.vector.memset(dummy[:, 4:5], 0.0).then_inc(e_hid.handle, 3)
            nc.vector.memset(dummy[:, 5:6], 0.0).then_inc(e_hl.handle, 2)
            nc.vector.memset(dummy[:, 6:7], 0.0).then_inc(e_y.handle, 6)
            dve.wait_ge(start_dve, 8)
            with dve.Fori(0, DEPTH) as l:
                chain = [0]

                def need(s, i):
                    dve.wait_ge(s.handle, s.value(l, i))

                def own(*instructions):
                    for ins in instructions:
                        dve_ord.of(ins)
                        chain[0] += 1
                    need(dve_ord, chain[0] - 1)

                V = nc.vector

                def tt(o, i0, i1, op):
                    return V.tensor_tensor(o, i0, i1, op)

                def heads(ap):
                    return ap.rearrange("p (h n) -> p h n", h=4)

                def wide(col4):
                    return col4.unsqueeze(2).to_broadcast([P, 4, P])

                need(par_in, 2)
                need(smh_act, 0)
                sml_dve.of(tt(smlo[:, :, :], small[:, :, :], smhi[:, :, :].bitcast(F32), ALU.subtract))
                lq = row("lq").rearrange("p (a b n) -> p a b n", a=2, b=2)
                own(tt(rwf[:, 0:128].rearrange("p (a n) -> p a n", a=2), lq[:, :, 0, :], lq[:, :, 1, :], ALU.mult))
                lam_dve.of(V.tensor_reduce(lam[:, 0:2], rwf[:, 0:128].rearrange("p (a n) -> p a n", a=2), AX, ALU.add))
                need(lam_act, 0)
                own(tt(lam[:, 4:5], lam[:, 3:4], lam[:, 2:3], ALU.subtract))
                own(tt(lam[:, 5:6], lam[:, 4:5], row("lam", 0, 1), ALU.subtract))
                own(V.tensor_copy(mst[:, 0:8], row("m0")))

                for s in SCHEDULE:
                    if s[0] == "modt":
                        g = s[1]
                        need(modt_pe, g)
                        b = pcol[:, PC_BMOD + KD * g:PC_BMOD + KD * (g + 1)]
                        mod_dve.of(tt(modc[:, g, :, :], T[:, 1, 0:256].rearrange("p (j c) -> p j c", c=32)[:, :, 0:2],
                                      b.unsqueeze(2).to_broadcast([P, KD, 2]), ALU.add))
                        if g in (1, 4):
                            need(mod_dve, g)
                            o = PC_NMIX if g == 1 else PC_NFFN
                            own(V.tensor_scalar(acol[:, :, :], modc[:, g, :, :], 1.0, None, ALU.add))
                            own(tt(acol[:, :, :], acol[:, :, :],
                                   pcol[:, o:o + KD].unsqueeze(2).to_broadcast([P, KD, 2]), ALU.mult))
                    elif s[0] == "norm":
                        w = s[1]
                        need(rstd_pool, w)
                        for t in range(TILES):
                            xn_dve.of(V.tensor_scalar(xn[:, t, :], x[:, t, :], st[:, t:t + 1], None, ALU.mult))

                        def low(c):
                            need(hh_act, KD * w + c)
                            hl_dve.of(tt(hlo[:, c, :], probT[:, c % 2, 0, :], hhi[:, c, :].bitcast(F32), ALU.subtract))

                        for c in range(KD):
                            need(nt_pe, KD * w + c)
                            if c > 1:
                                need(hl_dve, KD * w + c - 2)
                            for cn, (lo, hi) in enumerate(((0, 256), (256, 384))):
                                ins = V.tensor_scalar(probT[:, c % 2, 0, lo:hi], T[:, c % 2, lo:hi],
                                                      acol[:, c, cn:cn + 1], modc[:, 3 * w, c, cn:cn + 1],
                                                      ALU.mult, ALU.add)
                            hf_dve.of(ins)
                            if c:
                                low(c - 1)
                        low(KD - 1)
                    elif s[0] == "gemm":
                        g = s[1]
                        c, i, n = GEMM[g]
                        kind, arg = CHUNKS[c][:2]
                        if i == n - 1 and kind == "branch":
                            for t in range(TILES):
                                need(tile_pe, TILES * c + t)
                                need(*evacuated(c - 1, t))
                                dst = merged[arg[1]][:, t, :] if arg[0] == 0 else sig[:, t, :]
                                if arg == (0, 0):
                                    need(to_pe, 3)
                                if arg == (0, 1):
                                    need(pv_pe, 11)
                                    need(kv_out["B"], 1)
                                ev_dve.of(V.scalar_tensor_tensor(dst, sig[:, t, :], 1.0, G[:, t, :], ALU.add, ALU.mult))
                        if i == n - 1 and kind == "wout":
                            need(g_in, 1)
                            for t in range(TILES):
                                need(tile_pe, TILES * c + t)
                                if arg == 0:
                                    need(x_in, 0)
                                    need(ev_pool, pooled(CHUNK_NO["branch", (3, 1)], t))
                                else:
                                    need(ev_pool, pooled(c - 1, t))
                                ev_dve.of(tt(sig[:, t, :], G[:, t, :], gbc[:, t // 2, arg * 512:(arg + 1) * 512], ALU.mult))
                    elif s == ("mgate",):
                        need(mg_pe, 0)
                        g3 = O[:, 0:48].rearrange("p (t n) -> p t n", t=TILES)
                        own(tt(gi[:, :, :], g3[:, :, 0:8], row("ib").unsqueeze(1).to_broadcast([P, TILES, 8]), ALU.add),
                            tt(gf[:, :, :], g3[:, :, 8:16], row("fb").unsqueeze(1).to_broadcast([P, TILES, 8]), ALU.add))
                        mg_dve.of(V.scalar_tensor_tensor(ga[:, :, :], gf[:, :, :], -1.0, gf[:, :, :], ALU.mult, ALU.min))
                        need(ln_act, 0)
                        lf_dve.of(V.scalar_tensor_tensor(lf[:, :, :], gf[:, :, :], 0.0, ga[:, :, :], ALU.min, ALU.subtract))
                    elif s == ("mcum",):
                        need(mb_pe, 0)
                        own(V.tensor_copy(bt[:, :, :], O[:, 64:112].rearrange("p (t n) -> p t n", t=TILES)))
                        cc_dve.of(tt(cc[:, :, :], gi[:, :, :], bt[:, :, 0:8], ALU.subtract))
                    elif s[0] == "rope":
                        ty, w, t = s[1:]
                        if s[1:] != ROPE[0]:
                            need(rope_dve, rope_dve.n - 1)
                        else:
                            need(m_out, 5)
                        ch = "Ckv" if (ty, w) == ("C", "k") else ty + w
                        need(*evacuated(CHUNK_NO[ch], t))
                        nh = 2 if ch == "Ckv" else 8
                        src = slot[ch][:, t, 0:64 * nh]
                        if t == 2:
                            for cp in range(2):
                                ins = V.tensor_copy(kdup[:, t, :, cp, :], src.rearrange("p (h n) -> p h n", h=2))
                            rope_dve.of(ins)
                            continue
                        r1 = sig[:, 0, 0:64 * nh]
                        r2 = sig[:, 1, 0:64 * nh]
                        pr = "p (h f c n) -> p h f c n"
                        s5 = src.rearrange(pr, h=nh, f=2, c=2)
                        u5 = r2.rearrange(pr, h=nh, f=2, c=2)
                        sn = rope_t[:, t, 64:96].rearrange("p (f n) -> p f n", f=2).unsqueeze(1).to_broadcast([P, nh, 2, 16])
                        own(tt(r1.rearrange("p (h n) -> p h n", h=nh), src.rearrange("p (h n) -> p h n", h=nh),
                               rope_t[:, t, 0:64].unsqueeze(1).to_broadcast([P, nh, 64]), ALU.mult),
                            tt(u5[:, :, :, 0, :], s5[:, :, :, 1, :], sn, ALU.mult),
                            tt(u5[:, :, :, 1, :], s5[:, :, :, 0, :], sn, ALU.mult))
                        r15 = r1.rearrange(pr, h=nh, f=2, c=2)
                        for cp in range(2 if ch == "Ckv" else 1):
                            if ch == "Ckv":
                                dst = kdup[:, t, :, cp, :].rearrange("p h (f c n) -> p h f c n", f=2, c=2)
                            else:
                                dst = s5
                            a1 = tt(dst[:, :, :, 0, :], r15[:, :, :, 0, :], u5[:, :, :, 0, :], ALU.subtract)
                            dve_ord.of(a1)
                            chain[0] += 1
                            a2 = tt(dst[:, :, :, 1, :], r15[:, :, :, 1, :], u5[:, :, :, 1, :], ALU.add)
                            if cp == 1:
                                rope_dve.of(a2)
                            elif ch != "Ckv":
                                rope_dve.of(a2)
                    elif s[0] == "m1":
                        m = s[1]
                        d, t = MU[m]
                        q = ms[:, m % 2]
                        W = prob[:, m % 2].rearrange("p a n -> p (a n)")[:, 0:512]
                        m0 = mst[:, 4 * d:4 * d + 4] if t < 2 else zst[:, :]
                        b = bt[:, t, 4 * d:4 * d + 4]
                        tot = bt[:, t, 8 + 4 * d:12 + 4 * d]
                        c4 = cc[:, t, 4 * d:4 * d + 4]
                        need(m1_pe, m)
                        own(tt(heads(W), heads(S[:, 0, :]), cmask[:, d, :].unsqueeze(1).to_broadcast([P, 4, P]), ALU.add),
                            V.tensor_reduce(q[:, 0:4], heads(S[:, 0, :]), AX, ALU.max))
                        own(V.tensor_reduce(q[:, 4:8], heads(W), AX, ALU.max))
                        own(tt(q[:, 4:8], q[:, 4:8], m0, ALU.max), tt(q[:, 0:4], q[:, 0:4], m0, ALU.max))
                        own(tt(q[:, 32:36], m0, q[:, 4:8], ALU.subtract),
                            V.scalar_tensor_tensor(q[:, 36:40], b, -1.0, q[:, 4:8], ALU.mult, ALU.subtract),
                            tt(q[:, 40:44], c4, q[:, 0:4], ALU.subtract),
                            tt(q[:, 44:48], m0, q[:, 0:4], ALU.subtract))
                        if m in MUPD:
                            mo = mst[:, 4 * d:4 * d + 4] if t < 2 else mst[:, 8 + 4 * d:12 + 4 * d]
                            own(tt(mo, tot, q[:, 0:4], ALU.add))
                        mmax_dve.of(V.tensor_scalar(q[:, 8:12], q[:, 4:8], -1.0, None, ALU.mult))
                        need(mexp_act, m)
                        ms_dve.of(tt(W, S[:, 1, :], W, ALU.mult))
                    elif s[0] == "m3":
                        m = s[1]
                        d, t = MU[m]
                        q = ms[:, m % 2]
                        W = prob[:, m % 2].rearrange("p a n -> p (a n)")[:, 0:512]
                        ya = slot["Aq"][:, t, :]
                        need(m3_pe, m)
                        if t < 2:
                            own(tt(heads(W), heads(S[:, 0, :]), wide(q[:, 16:20]), ALU.mult),
                                tt(q[:, 48:52], O[:, 4:8], q[:, 16:20], ALU.mult))
                            own(tt(W, W, T[:, 1, :], ALU.add), tt(q[:, 48:52], q[:, 48:52], O[:, 0:4], ALU.add))
                            num = W
                        else:
                            own(V.tensor_copy(q[:, 48:52], O[:, 0:4]))
                            num = T[:, 1, :]
                        own(V.scalar_tensor_tensor(q[:, 48:52], q[:, 48:52], -1.0, q[:, 48:52], ALU.mult, ALU.max))
                        own(tt(q[:, 48:52], q[:, 48:52], q[:, 20:24], ALU.max))
                        own(V.reciprocal(q[:, 52:56], q[:, 48:52]))
                        if m in (0, 1, 2):
                            mh_dve.of(tt(heads(ya), heads(num), wide(q[:, 52:56]), ALU.mult))
                        else:
                            own(tt(heads(W), heads(num), wide(q[:, 52:56]), ALU.mult))
                            mh_dve.of(tt(ya, ya, W, ALU.add))
                        if m in MUPD and t < 2:
                            c4 = cT[:, 4 * d:4 * d + 4, :]
                            nv = pcol[:, PC_N + 4 * d:PC_N + 4 * d + 4]
                            own(tt(c4, c4, wide(q[:, 28:32]), ALU.mult), tt(nv, nv, q[:, 28:32], ALU.mult))
                            own(tt(nv, nv, O[:, 8:12], ALU.add))
                            ct_dve.of(tt(c4, c4, heads(T[:, 0, :]), ALU.add))
                    elif s[0] == "sc":
                        u = s[1]
                        ty, t, j = AU[u]
                        w = 384 if t < 2 else 128
                        q = am[:, u % 2]
                        need(sc_pe, u)
                        src = S[:, :, 0:w]
                        if u in BIASED:
                            b = BIASED.index(u)
                            need(bias_in, bias_index(b))
                            src = prob[:, u % 2, :, :]
                            sa_dve.of(tt(src, S[:, :, 0:w], bias[:, :, :], ALU.add))
                            need(sa_dve, b)
                        own(V.tensor_reduce(q[:, 8:10], src, AX, ALU.max))
                        if ty == "C":
                            sk = row("sink", 2 * j, 2 * j + 2)
                            own(tt(q[:, 8:10], q[:, 8:10], sk, ALU.max))
                            own(V.tensor_scalar(q[:, 0:2], q[:, 8:10], -1.0, None, ALU.mult))
                            nm_dve.of(tt(q[:, 4:6], sk, q[:, 0:2], ALU.add))
                        else:
                            nm_dve.of(V.tensor_scalar(q[:, 0:2], q[:, 8:10], -1.0, None, ALU.mult))
                        need(ex_act, u)
                        if ty == "C":
                            own(tt(q[:, 2:4], q[:, 2:4], q[:, 6:8], ALU.add))
                        own(V.reciprocal(q[:, 10:12], q[:, 2:4]))
                        if ty == "D":
                            own(V.tensor_scalar(prob[:, u % 2, 0, 0:w], prob[:, u % 2, 0, 0:w], q[:, 10:11], None, ALU.mult),
                                V.tensor_scalar(q[:, 11:12], q[:, 11:12], lam[:, 5:6], None, ALU.mult))
                            pn_dve.of(V.scalar_tensor_tensor(prob[:, u % 2, 0, 0:w], prob[:, u % 2, 1, 0:w], q[:, 11:12],
                                                             prob[:, u % 2, 0, 0:w], ALU.mult, ALU.add))
                        else:
                            for m in range(2):
                                ins = V.tensor_scalar(prob[:, u % 2, m, 0:w], prob[:, u % 2, m, 0:w], q[:, 10 + m:11 + m],
                                                      None, ALU.mult)
                            pn_dve.of(ins)
                    elif s[0] == "pt" and AU[s[1]][0] != "D":
                        u = s[1]
                        w = 384 if AU[u][1] < 2 else 128
                        need(pt_pe, u)
                        pb_dve.of(V.tensor_copy(probT[:, u % 2, 1, 0:w], T[:, 1, 0:w]))
                    elif s[0] == "pv" and AU[s[1]][0] != "D":
                        u = s[1]
                        ty, t, j = AU[u]
                        n = TYPES.index(ty)
                        need(oh_act, u)
                        blk = (slice(None), j, slice(t * P, (t + 1) * P))
                        ol_dve.of(tt(blo[n][blk], O[:, 0:P], bhi[n][blk].bitcast(F32), ALU.subtract))
                    elif s[0] == "hn":
                        i = s[1]
                        y = slot["AD"[i] + "q"]
                        if i == 1:
                            need(yd_act, 11)
                        for t in range(TILES):
                            own(tt(prob[:, t % 2].rearrange("p a n -> p (a n)")[:, 0:512], y[:, t, :], y[:, t, :], ALU.mult))
                            hs_dve.of(V.tensor_reduce(st[:, 3 + 4 * t:7 + 4 * t],
                                                      heads(prob[:, t % 2].rearrange("p a n -> p (a n)")[:, 0:512]), AX,
                                                      ALU.add))
                        need(hr_pool, i)
                        if i == 0:
                            need(tanh_act, 0)
                        for t in range(TILES):
                            if i == 0:
                                o = slot["Ao"][:, t, :]
                                own(tt(heads(y[:, t, :]), heads(y[:, t, :]), wide(st[:, 3 + 4 * t:7 + 4 * t]), ALU.mult),
                                    V.scalar_tensor_tensor(o, o, 1.0, row("anorm"), ALU.add, ALU.mult))
                                hn_dve.of(tt(y[:, t, :], y[:, t, :], o, ALU.mult))
                            else:
                                own(tt(heads(y[:, t, :]), heads(y[:, t, :]), wide(st[:, 3 + 4 * t:7 + 4 * t]), ALU.mult))
                                hn_dve.of(tt(heads(y[:, t, :]), heads(y[:, t, :]),
                                             row("subln").unsqueeze(1).to_broadcast([P, 4, P]), ALU.mult))
                    elif s[0] == "to":
                        i, j = s[1:]
                        need(th_act, 4 * i + j)
                        tl_dve.of(tt(blo[0][:, j, :], T[:, j % 2, 0:384], bhi[0][:, j, :].bitcast(F32), ALU.subtract))
                    elif s[0] == "mt":
                        c = s[1]
                        need(mh_act, c)
                        ml_dve.of(V.scalar_tensor_tensor(hlo[:, c, :], T[:, c % 2, 0:384], 0.5, hhi[:, c, :].bitcast(F32),
                                                         ALU.mult, ALU.subtract))
                    elif s == ("route",):
                        route(dve, need, own, tt)
                    elif s == ("experts",):
                        def one_expert(e):
                            def eneed(sgl, n, k):
                                dve.wait_ge(sgl.handle, (l * NEXP + e) * n + (k + 1 + sgl.credit))

                            for t in range(TILES):
                                eneed(e_tanh, 3, t)
                                e_dve.of(V.scalar_tensor_tensor(gact[:, t, :], gact[:, t, :], 1.0, G[:, t, 0:DEXP],
                                                                ALU.add, ALU.mult))
                                eneed(e_dve, 3, t)
                                e_hid.of(V.scalar_tensor_tensor(hid[:, t, :], gact[:, t, :], gate[:, t, bass.ds(e, 1)],
                                                                G[:, t, DEXP:], ALU.mult, ALU.mult))
                            for f in range(2):
                                eneed(e_hh, 2, f)
                                e_hl.of(tt(elo[:, f, :], T[:, f, 0:384], ehi[:, f, :].bitcast(F32), ALU.subtract))
                            for q in range(6):
                                t, hf = divmod(q, 2)
                                bank = (S[:, 0, :], S[:, 1, :], O[:, :])[q % 3]
                                eneed(e_down, 6, q)
                                if q == 0:
                                    need(yz_pool, 0)
                                ya = yacc[:, t, hf * 512:(hf + 1) * 512]
                                e_y.of(tt(ya, ya, bank, ALU.add))

                        with dve.Fori(0, NEXP) as e:
                            one_expert(e)
                        dve.wait_ge(e_y.handle, (l * NEXP + NEXP) * 6 + e_y.credit)
                    elif s == ("end",):
                        need(g_in, 3)
                        need(m_out, 5)
                        for t in range(TILES):
                            own(tt(yacc[:, t, :], yacc[:, t, :], gbc[:, t // 2, :], ALU.mult))
                            ins = tt(x[:, t, :], x[:, t, :], yacc[:, t, :], ALU.add)
                            if t < TILES - 1:
                                own(ins)
                        layer_end.of(ins)
            dve.wait_ge(fin_rstd_pool, 2)
            dve.wait_ge(fin_gain_in, 16)
            for t in range(TILES):
                nc.vector.scalar_tensor_tensor(xn[:, t, :], x[:, t, :], st[:, t:t + 1], yacc[:, 0, :], ALU.mult, ALU.mult)\
                    .then_inc(fin_y_dve, 1)

        return {k: v.n for k, v in signals.items()}


def _constants():
    i = np.arange(P)
    f = np.float32
    tri = np.stack([i[:, None] <= i[None, :], i[:, None] >= i[None, :]], 1).astype(f)
    cmask = np.stack([np.where(i[None, :] <= i[:, None], 0, NEG), np.where(i[None, :] >= i[:, None], 0, NEG)], 1).astype(f)
    nf = DH_B // 4
    inv = (10000.0 ** (-np.arange(nf, dtype=f) / f(nf))).astype(f)
    t = np.arange(T_LAT)
    ang = np.stack([(t // GRID_W).astype(f)[:, None] * inv, (t % GRID_W).astype(f)[:, None] * inv], 1)
    cos, sin = np.cos(ang), np.sin(ang)
    rope = np.concatenate([np.stack([cos, cos], 2).reshape(T_LAT, 64), sin.reshape(T_LAT, 32)], 1)
    rope = rope.reshape(2, P, 96).transpose(1, 0, 2).astype(f)
    k = np.arange(T_LAT)
    window = np.where(np.abs(k[None, :] - k[:, None]) <= 128, 0, NEG).reshape(2, P, T_LAT).astype(f)
    return {"ident": np.eye(P, dtype=f), "tri": tri, "cmask": cmask, "rope": rope, "swa_mask": window,
            "order": np.tile(np.array([4, 3, 2, 1], f), (P, 1))}


def _windows(rpb):
    L, H = rpb.shape[:2]
    rows = T_LAT // GRID_W
    out = np.full((L, H, rows, GRID_W, rows, GRID_W), NEG, np.float32)
    for r in range(rows):
        for c in range(GRID_W):
            lo = min(max(c - 8, 0), GRID_W - 16)
            out[:, :, r, c, :, lo:lo + 16] = rpb[:, :, 7 - r:7 - r + rows, lo - c + 15:lo - c + 31]
    return out.reshape(L, 4, 2, 2, P, T_LAT).transpose(0, 3, 1, 4, 2, 5).reshape(L * 8, P, 2, T_LAT)


def _stream(i):
    units = np.empty((DEPTH, NU, P, 1024), np.float32)
    o = {}
    at = 0
    for name, n in (("Aq", 512), ("Ak", 512), ("Av", 512), ("Ao", 512), ("gates", 16), ("Bq", 512), ("Bk", 512), ("Bv", 512),
                    ("Cq", 512), ("Ckv", 256), ("Dq", 512), ("Dk", 512), ("Dv", 512), ("gt", 4 * D)):
        o[name] = at
        at += n

    def put(dst, w, k, cols):
        n = cols.stop - cols.start
        for j, kk in enumerate(k):
            dst[:, :, j * n:(j + 1) * n] = w[:, kk * P:(kk + 1) * P, cols]

    for p, (what, g) in enumerate(STREAM):
        dst = units[:, p]
        if what == "mod":
            put(dst, i["w_mod"], range(KD), slice(g * P, (g + 1) * P))
            continue
        c, u, _ = GEMM[g]
        kind, arg, width, _ = CHUNKS[c]
        ku = 1024 // width
        k = range(u * ku, (u + 1) * ku)
        if kind == "proj":
            put(dst, i["w_in"], k, slice(o[arg], o[arg] + width))
        elif kind == "gate":
            lo = o["gt"] + arg[0] * D + arg[1] * 512
            put(dst, i["w_in"], k, slice(lo, lo + 512))
        elif kind == "branch":
            put(dst, i["w_branch"][:, arg[0]], k, slice(arg[1] * 512, (arg[1] + 1) * 512))
        else:
            put(dst, i["w_out"], k, slice(arg * 512, (arg + 1) * 512))
    for n, (e, u) in enumerate(EXPERT_UNITS):
        dst = units[:, len(STREAM) + n]
        if u >= 4:
            dst[:] = i["w_exp_down"][:, e, (u - 4) * P:(u - 3) * P]
            continue
        for k in range(2):
            r = slice((2 * u + k) * P, (2 * u + k + 1) * P)
            dst[:, :, k * 512:k * 512 + 256] = i["w_exp_gate"][:, e, r]
            dst[:, :, k * 512 + 256:(k + 1) * 512] = i["w_exp_up"][:, e, r]
    return units.reshape(DEPTH * NU, P, 1024), o


def _layout(i):
    L = DEPTH
    stream, o = _stream(i)

    def cols(v):
        return v.reshape(L, -1, P).transpose(0, 2, 1)

    pcol = np.concatenate([cols(i["norm_mix"]), cols(i["norm_ffn"]), cols(i["b_mod"]),
                           cols(i["state_mlstm_n"].reshape(L, 2 * H_A * P))], 2)
    lam_init = np.array([0.8 - 0.6 * np.exp(-0.3 * l) for l in range(L)])
    lam = np.stack([lam_init, 1.0 - lam_init], 1).astype(np.float32)
    prow = np.concatenate([i["mlstm_i_bias"].reshape(L, 8), i["mlstm_f_bias"].reshape(L, 8), i["swa_sink"],
                           i["diff_lq1"], i["diff_lk1"], i["diff_lq2"], i["diff_lk2"], lam,
                           i["mlstm_norm"], i["diff_subln"], i["state_mlstm_m"].reshape(L, 8)], 1)
    w = i["w_in"][:, :, o["gates"]:o["gates"] + 16]
    small = np.concatenate([w, i["router_group"], i["router_expert"]], 2).reshape(L, KD, P, SMALL).transpose(0, 2, 1, 3)

    def keys(c, dup=False):
        k = c[0].reshape(L, PAST, -1)
        if dup:
            k = c[0].reshape(L, PAST, KV_C, 1, 64)
            k = np.concatenate([k, k, k, k], 3)
            k = k.reshape(L, PAST, 512)
            k = k.reshape(L, PAST, 2, 2, P)[:, :, :, 0].reshape(L, PAST, 2, P)
            k = np.concatenate([k, k], 2).reshape(L, PAST, 512)
        return k.reshape(L, PAST, 4, P).transpose(0, 3, 2, 1)

    ks = np.stack([keys(i["cache_nat_k"]), keys(i["cache_swa_k"], True), keys(i["cache_diff_k"])], 1)
    vs = np.zeros((L, 3, P, 512), np.float32)
    vs[:, 0] = i["cache_nat_v"][0].reshape(L, PAST, 512)
    vs[:, 1, :, 0:128] = i["cache_swa_v"][0].reshape(L, PAST, 128)
    vs[:, 2] = i["cache_diff_v"][0].reshape(L, PAST, 512)
    cond = np.zeros((P, KD, 32), np.float32)
    cond[:, :, 0:2] = np.stack([i["c"][0], i["c_ctx"]], 0).reshape(2, KD, P).transpose(2, 1, 0)
    arrays = {
        "units": stream, "tokens": np.concatenate([i["x_sample"][0].reshape(2, P, D), i["x_prompt"][0].reshape(1, P, D)]),
        "cond": cond, "pcol": pcol, "prow": prow, "small": small,
        "state_C": i["state_mlstm_C"][0].reshape(L, 2 * H_A, DH_A, DH_A).transpose(0, 3, 1, 2),
        "keys": ks.reshape(L * 3, P, 4, P), "vals": vs.reshape(L * 3, P, 512), "nat_bias": _windows(i["nat_rpb"]),
        "norm_final": i["norm_final"], **_constants()}
    return {k: np.ascontiguousarray(v) for k, v in arrays.items()}


_OUTS = {"tokens": (TILES, P, D), "nat_k": (DEPTH, P, 512), "nat_v": (DEPTH, P, 512), "swa_k": (DEPTH, P, 128),
         "swa_v": (DEPTH, P, 128), "diff_k": (DEPTH, P, 512), "diff_v": (DEPTH, P, 512),
         "C": (DEPTH * 2, H_A, DH_A, DH_A), "n": (DEPTH * 2, 512), "m": (DEPTH * 2, 4)}


def _build(nc, arrays, counts):
    a = {k: nc.dram_tensor("in_" + k, v.shape, mybir.dt.from_np(v.dtype), kind="ExternalInput").ap()
         for k, v in arrays.items()}
    a["x_scratch"] = nc.dram_tensor("x_scratch", (TILES, P, D), F32, kind="Internal").ap()
    a["g_scratch"] = nc.dram_tensor("g_scratch", (2, 16, P), F32, kind="Internal").ap()
    out = {k: nc.dram_tensor("out_" + k, s, F32, kind="ExternalOutput").ap() for k, s in _OUTS.items()}
    return program(nc, a, out, counts)


def kernel(**inputs):
    import concourse.bacc as _bacc
    from concourse.bass_utils import run_bass_kernel_spmd as _run
    arrays = _layout({k: np.asarray(v) for k, v in inputs.items()})
    counts = _build(_bacc.Bacc("TRN2", target_bir_lowering=False, num_devices=1), arrays, {})
    nc = _bacc.Bacc("TRN2", target_bir_lowering=False, num_devices=1)
    _build(nc, arrays, counts)
    res = _run(nc, [{"in_" + k: v for k, v in arrays.items()}], core_ids=[0]).results[0]
    o = {k: res["out_" + k] for k in _OUTS}
    L = DEPTH
    return (o["tokens"][2].reshape(1, T_CTX, D), o["tokens"][0:2].reshape(1, T_LAT, D),
            o["nat_k"].reshape(1, L, P, H_B, DH_B), o["nat_v"].reshape(1, L, P, H_B, DH_B),
            o["swa_k"].reshape(1, L, P, KV_C, 64), o["swa_v"].reshape(1, L, P, KV_C, 64),
            o["diff_k"].reshape(1, L, P, H_D, 128), o["diff_v"].reshape(1, L, P, H_D, 128),
            o["C"].reshape(1, L, 2, H_A, DH_A, DH_A), o["n"].reshape(1, L, 2, H_A, DH_A), o["m"].reshape(1, L, 2, H_A))
```

```python
from contextlib import ExitStack

import numpy as np

import concourse.bass as bass
from concourse import mybir

F32 = mybir.dt.float32
F32R = mybir.dt.float32r
ALU = mybir.AluOpType
ACT = mybir.ActivationFunctionType
AX = mybir.AxisListType.X

P = 128
D = 1024
DEPTH = 2
T_LAT, T_CTX, PAST = 256, 128, 128
TILES = (T_LAT + T_CTX) // P
GRID_W = 64
H_A, DH_A = 4, 128
H_B, DH_B = 8, 64
KV_C = 2
H_D = 4
NEXP, DEXP = 16, 256
KD = D // P
EPS = 1e-6
NEG = -1e30

CHUNKS = [("proj", s, 512, 4) for s in ("Aq", "Ak", "Av", "Ao", "Bq", "Bk", "Bv", "Cq")]
CHUNKS += [("proj", "Ckv", 256, 2)]
CHUNKS += [("proj", s, 512, 4) for s in ("Dq", "Dk", "Dv")]
for _n in range(4):
    for _h in range(2):
        CHUNKS += [("gate", (_n, _h), 512, 4), ("branch", (_n, _h), 512, 2)]
CHUNKS += [("wout", _h, 512, 4) for _h in range(2)]
CHUNK_NO = {c[1] if c[0] == "proj" else c[:2]: i for i, c in enumerate(CHUNKS)}
GEMM = []
for _c, (_kind, _arg, _w, _nu) in enumerate(CHUNKS):
    GEMM += [(_c, _i, _nu) for _i in range(_nu)]
NG = len(GEMM)
FIRST_UNIT = {}
for _g, (_c, _i, _nu) in enumerate(GEMM):
    if _i == 0:
        FIRST_UNIT[_c] = _g
LAST_UNIT = {c: FIRST_UNIT[c] + CHUNKS[c][3] - 1 for c in FIRST_UNIT}
GRP = 4
NT = GRP + (TILES * P - GRP) // P
UNITS = [(0, 0), (0, 1), (0, 2), (0, 3)]
for _e in range(1, GRP):
    UNITS += [(_e, _u) for _u in range(4)] + [(_e - 1, 4), (_e - 1, 5)]
UNITS += [(GRP - 1, 4), (GRP - 1, 5)]
UT = len(UNITS)
NMOD = 6 * KD
TYPES = "ABCD"
TP = [(ty, w, j) for ty in "ABCD" for w in "qk" for j in range(2 if (ty, w) == ("C", "k") else 4)]
MU = [(0, 0), (1, 1), (0, 2), (1, 2), (0, 1), (1, 0)]
MUPD = [0, 1, 2, 3]
AU = [(ty, t, j) for ty in "BCD" for t in range(TILES) for j in range(4)]
ROPE = [("C", "q", 0), ("C", "q", 1), ("C", "k", 0), ("C", "k", 1), ("C", "k", 2),
        ("D", "q", 0), ("D", "q", 1), ("D", "k", 0), ("D", "k", 1)]
BIASED = [u for u, (ty, t, j) in enumerate(AU) if ty in "BC" and t < 2]
SMALL = 36


def schedule():
    after = {g: [] for g in range(-1, NG)}

    def put(g, *steps):
        after[g] += steps

    put(0, ("dma", "stateC"))
    put(4, ("mgate",))
    put(5, ("tp", "A", "q", 0), ("tp", "A", "q", 1))
    put(6, ("tp", "A", "q", 2), ("tp", "A", "q", 3), ("mcum",))
    put(9, ("tp", "A", "k", 0), ("tp", "A", "k", 1))
    put(10, ("tp", "A", "k", 2), ("tp", "A", "k", 3))
    for m in range(len(MU)):
        put(11 + 4 * m, ("m1", m))
        put(13 + 4 * m, ("m2", m))
        put(14 + 4 * m, ("m3", m))
    put(LAST_UNIT[CHUNK_NO["Bv"]] + 2, ("dma", "outB"))
    put(LAST_UNIT[CHUNK_NO["Ckv"]] + 1, ("rope", "C", "q", 0), ("rope", "C", "k", 0), ("rope", "C", "k", 2))
    put(LAST_UNIT[CHUNK_NO["Ckv"]] + 2, ("rope", "C", "q", 1), ("rope", "C", "k", 1), ("dma", "outC"))
    put(35, ("dma", "loadB"), ("hn", 0))
    put(38, ("hr", 0))
    for i in range(4):
        put(36 + i, ("tp", "B", "q", i), ("tp", "B", "k", i))
        put(41 + i, ("to", 0, i))
    put(LAST_UNIT[CHUNK_NO["Dk"]] + 1, ("rope", "D", "q", 0), ("rope", "D", "q", 1))
    put(LAST_UNIT[CHUNK_NO["Dk"]] + 2, ("rope", "D", "k", 0), ("rope", "D", "k", 1))
    put(LAST_UNIT[CHUNK_NO["Dv"]] + 2, ("dma", "outD"))

    def attention(g, first):
        for i in range(12 + 3):
            at = g + (i if i < 9 else 9 + (i - 9) // 2)
            if i >= 3:
                put(at, ("pv", first + i - 3))
            if 2 <= i < 14:
                put(at, ("pt", first + i - 2))
            if i < 12:
                put(at, ("sc", first + i))
        return g + 12

    g = attention(40, 0)
    put(g - 3, ("dma", "keysC"))
    put(g - 1, ("dma", "valuesC"))
    for i in range(4):
        put(g - 3 + i // 2, ("tp", "C", "q", i))
    put(g - 1, ("tp", "C", "k", 0), ("tp", "C", "k", 1))
    g = attention(g, 12)
    put(g - 3, ("dma", "keysD"))
    put(g - 1, ("dma", "valuesD"))
    for i in range(4):
        put(g - 3 + i // 2, ("tp", "D", "q", i))
        put(g - 2 + i // 2, ("tp", "D", "k", i))
    g = attention(g, 24)
    put(g, ("hn", 1))
    put(g + 1, ("hr", 1))
    for i in range(4):
        put(g + 3, ("to", 1, i))
    d_done = g + 3
    for j in range(16, 40):
        put(36 + j, ("mod", j))
        if j % KD == KD - 1:
            put(36 + j, ("modv", j // KD))
            put(37 + j, ("modt", j // KD))
    put(36 + 25, ("gt", 0))
    put(g - 12, ("dma", "gate1"))
    for c in range(4):
        put(LAST_UNIT[CHUNK_NO["gate", (3, 1)]], ("mt", c))
    for c in range(4, 8):
        put(LAST_UNIT[CHUNK_NO["branch", (3, 1)]], ("mt", c))
    put(max(d_done, LAST_UNIT[CHUNK_NO["gate", (3, 0)]]), ("dma", "loadX"))

    steps = [("mod", j) for j in range(4)] + [("dma", "params")] + [("mod", j) for j in range(4, 8)]
    steps += [("modv", 0), ("modt", 0)]
    steps += [("mod", j) for j in range(8, 16)] + [("modv", 1), ("modt", 1), ("dma", "saveX"), ("norm", 0), ("prepare",)]
    for g in range(NG):
        steps.append(("gemm", g))
        steps += after[g]
    branch3 = steps.index(("gemm", FIRST_UNIT[CHUNK_NO["branch", (3, 0)]]))
    assert d_done < NG
    late = [s for s in steps[branch3:] if s in [("to", 1, i) for i in range(4)] or s in (("hn", 1), ("hr", 1)) or
            (s[0] in ("sc", "pt", "pv") and s[1] >= 24)]
    steps = steps[:branch3] + late + [s for s in steps[branch3:] if s not in late]
    steps += [("norm", 1), ("route",)] + [("mod", j) for j in range(40, NMOD)]
    steps += [("modv", 5), ("modt", 5), ("gt", 1), ("experts",), ("end",)]
    return steps


SCHEDULE = schedule()
TP_NO = {s[1:]: i for i, s in enumerate(s for s in SCHEDULE if s[0] == "tp")}
assert set(TP_NO) == set(TP)
STREAM = [s for s in SCHEDULE if s[0] in ("mod", "gemm")]
NU = len(STREAM) + GRP * UT
RAW = 6
POOL_COLS = 384
CONV = 3
NBLOCK = NT * UT // RAW
assert UT % RAW == 0 and len(STREAM) % RAW == 0 and NG % CONV == 0 and UT % CONV == 0

POS_OF = [p for p, s in enumerate(STREAM) if s[0] == "gemm"]
MODPOS = [p for p, s in enumerate(STREAM) if s[0] == "mod"]

PC_NMIX, PC_NFFN, PC_BMOD, PC_N = 0, KD, 2 * KD, 2 * KD + NMOD
PCOLS = PC_N + 2 * H_A
ROWS = {}
_o = 0
for _name, _n in (("ib", 8), ("fb", 8), ("sink", 8), ("lq", 256), ("lam", 2), ("anorm", 512), ("subln", 128), ("m0", 8)):
    ROWS[_name] = (_o, _o + _n)
    _o += _n
PROWS = _o


class Signal:

    def __init__(self, handle, name, per_layer, unit=1, credit=0):
        self.handle, self.name, self.per_layer, self.unit, self.credit, self.n = handle, name, per_layer, unit, credit, 0

    def of(self, instruction):
        instruction.then_inc(self.handle, self.unit)
        self.n += 1

    def at(self, layer, index):
        return self.handle, self.value(layer, index)

    def in_tile(self, layer, tile, per_tile, index):
        return self.handle, (layer * NT + tile) * per_tile + (index + 1 + self.credit)

    def value(self, layer, index):
        return (layer * self.per_layer + (index + 1 + self.credit)) * self.unit


def program(nc, a, out, counts):
    ctx = ExitStack()
    with ctx:
        def sb(name, shape, dt=F32):
            return ctx.enter_context(nc.sbuf_tensor(name, shape, dt))

        signals = {}

        def sg(name, unit=1, credit=0):
            h = ctx.enter_context(nc.semaphore(name))
            signals[name] = Signal(h, name, counts.get(name, 1000), unit, credit)
            return signals[name]

        raw = sb("raw", [P, RAW, 1024])
        whi = sb("whi", [P, CONV, 1024], F32R)
        wlo = sb("wlo", [P, CONV, 1024], F32R)
        hhi = sb("hhi", [P, KD, TILES * P], F32R)
        hlo = sb("hlo", [P, KD, TILES * P], F32R)
        bhi0_at = (nc.sbuf_base + 31) // 32 * 32
        bhi = [sb(f"bhi{i}", [P, 4, TILES * P], F32R) for i in range(2)]
        blo = [sb(f"blo{i}", [P, 4, TILES * P], F32R) for i in range(2)]
        pA = sb("pA", [P, 4, TILES, 512])
        pB_at = (nc.sbuf_base + 31) // 32 * 32
        pB = sb("pB", [P, 3, TILES, 512])
        pC = sb("pC", [P, TILES, 768])
        bhi.append(nc.alloc_sbuf_tensor_at("bhi2", [P, 4, TILES * P], F32R, offset=pB_at))
        blo.append(nc.alloc_sbuf_tensor_at("blo2", [P, 4, TILES * P], F32R, offset=pB_at + 4 * 4 * TILES * P))
        qT_at = (nc.sbuf_base + 31) // 32 * 32
        qT = sb("qT", [P, 4, TILES * P])
        kT_at = (nc.sbuf_base + 31) // 32 * 32
        kT = sb("kT", [P, 4, TILES * P + PAST])
        ehi = nc.alloc_sbuf_tensor_at("ehi", [P, 2, TILES * P], F32R, offset=kT_at)
        elo = nc.alloc_sbuf_tensor_at("elo", [P, 2, TILES * P], F32R, offset=kT_at + 4 * 2 * TILES * P)
        hth = nc.alloc_sbuf_tensor_at("hth", [P, TILES, D], F32R, offset=bhi0_at)
        htl = nc.alloc_sbuf_tensor_at("htl", [P, TILES, D], F32R, offset=bhi0_at + 4 * TILES * D)
        sel = nc.alloc_sbuf_tensor_at("sel", [P, TILES, P], F32R, offset=qT_at)
        selT = nc.alloc_sbuf_tensor_at("selT", [P, TILES * P], F32R, offset=qT_at + 4 * TILES * P)
        yh = nc.alloc_sbuf_tensor_at("yh", [P, 2, 512], F32R, offset=pB_at)
        yl = nc.alloc_sbuf_tensor_at("yl", [P, 2, 512], F32R, offset=pB_at + 4 * 1024)
        vc = sb("vc", [P, 512])
        prob = sb("prob", [P, 2, 2, 384])
        probT = sb("probT", [P, 2, 2, 384])
        bias = sb("bias", [P, 2, 384])
        kdup = sb("kdup", [P, TILES, 2, 2, 64])
        sig = sb("sig", [P, TILES, 512])
        cst, nrow = sig[:, 2, :], sig[0:1, 0:2, :]
        small = sb("small", [P, KD, SMALL])
        smhi = sb("smhi", [P, KD, SMALL], F32R)
        smlo = sb("smlo", [P, KD, SMALL], F32R)
        pcol = sb("pcol", [P, PCOLS])
        prow = sb("prow", [P, PROWS])
        cT = sb("cT", [P, 2 * H_A, DH_A])
        modc = sb("modc", [P, 6, KD, 2])
        acol = sb("acol", [P, KD, 2])
        cond = sb("cond", [P, KD, 32])
        grow = sb("grow", [16, P])
        ident = sb("ident", [P, P])
        tri = sb("tri", [P, 2, P])
        ones = sb("ones", [P, P])
        cmask = sb("cmask", [P, 2, P])
        rope_t = sb("rope_t", [P, 2, 64 + 32])
        cval = sb("cval", [P, 5, 12])
        st = sb("st", [P, 16])
        gi = sb("gi", [P, TILES, 8])
        gf = sb("gf", [P, TILES, 8])
        ga = sb("ga", [P, TILES, 8])
        lf = sb("lf", [P, TILES, 8])
        bt = sb("bt", [P, TILES, 16])
        cc = sb("cc", [P, TILES, 8])
        ms = sb("ms", [P, 2, 64])
        mst = sb("mst", [P, 16])
        am = sb("am", [P, 2, 16])
        lam = sb("lam", [P, 8])
        rt = sb("rt", [P, TILES, 20])
        rw = sb("rw", [P, TILES, 80])
        gate = sb("gate", [P, GRP])
        rel = sb("rel", [P, NT, TILES])
        gidx = sb("gidx", [P, NBLOCK], mybir.dt.int32)
        order = sb("order", [P, 4 + NT + P])
        zst = sb("zst", [P, 4])
        dummy = sb("sink_col", [P, 16])
        x = pA[:, 0:2, :, :].rearrange("p a t n -> p (a t n)").rearrange("p (t n) -> p t n", t=TILES)
        yacc = pA[:, 2:4, :, :].rearrange("p a t n -> p (a t n)").rearrange("p (t n) -> p t n", t=TILES)
        xn = pB[:, 0:2, :, :].rearrange("p a t n -> p (a t n)").rearrange("p (t n) -> p t n", t=TILES)
        rwf = rw[:, :, :].rearrange("p t n -> p (t n)")
        cond_t = prob[:, 0].rearrange("p a n -> p (a n)")[:, 0:32 * KD].rearrange("p (k c) -> p k c", k=KD)
        mrow = kdup[:, 0].rearrange("p a b n -> p (a b n)")
        Cq = pC[:, :, 0:512]
        Ckv = pC[:, :, 512:768]
        gbc = pC[:, :, :].rearrange("p t n -> p (t n)")[:, 0:2 * D].rearrange("p (c n) -> p c n", c=2)
        merged = [pA[:, 3, :, :], pB[:, 2, :, :]]
        slot = {"Aq": pA[:, 0], "Ak": pA[:, 1], "Av": pA[:, 2], "Ao": pA[:, 3], "Bq": pB[:, 0], "Bk": pB[:, 1],
                "Bv": pB[:, 2], "Cq": Cq, "Ckv": Ckv, "Dq": pA[:, 1], "Dk": pA[:, 2], "Dv": pA[:, 0]}
        hg = prob[:, :, :, :].rearrange("p a b n -> p (a b n)")[:, 0:D].rearrange("p (h n) -> p h n", h=2)
        hid = sig[:, :, :].rearrange("p t n -> p (t n)")[:, 0:TILES * DEXP].rearrange("p (t n) -> p t n", t=TILES)
        gact = sig[:, :, :].rearrange("p t n -> p (t n)")[:, TILES * DEXP:].rearrange("p (t n) -> p t n", t=TILES)

        def row(name, lo=0, hi=None):
            s, e = ROWS[name]
            return prow[:, s + lo:(s + hi if hi is not None else e)]

        G = ctx.enter_context(nc.psum_tensor("G", [P, 3, 512], F32))
        S = ctx.enter_context(nc.psum_tensor("S", [P, 2, 512], F32))
        T = ctx.enter_context(nc.psum_tensor("T", [P, 2, 512], F32))
        O = ctx.enter_context(nc.psum_tensor("O", [P, 512], F32))

        w_in = [sg(f"w_in{i}", 16) for i in range(RAW)]
        hi_done = sg("hi_done", credit=RAW)
        lo_done = sg("lo_done", credit=RAW)
        unit_pe = sg("unit_pe", credit=CONV)
        tile_pe = sg("tile_pe")
        ev_act = sg("ev_act")
        ev_dve = sg("ev_dve")
        ev_pool = sg("ev_pool")
        mod_pe, mod_act, modt_pe, mod_dve = sg("mod_pe"), sg("mod_act"), sg("modt_pe"), sg("mod_dve")
        par_in, x_saved, x_in = sg("par_in", 16), sg("x_saved", 16), sg("x_in", 16)
        sq_act, rstd_pool, xn_dve, nt_pe = sg("sq_act"), sg("rstd_pool"), sg("xn_dve"), sg("nt_pe")
        xn_act, hl_pool = sg("xn_act"), sg("hl_pool")
        hf_dve, hh_act, hl_dve = sg("hf_dve"), sg("hh_act"), sg("hl_dve")
        smh_act, sml_dve = sg("smh_act"), sg("sml_dve")
        mg_pe, mg_dve, ln_act, lf_dve = sg("mg_pe"), sg("mg_dve"), sg("ln_act"), sg("lf_dve")
        mb_pe, cc_dve = sg("mb_pe"), sg("cc_dve")
        tp_pe, tp_act, rope_dve = sg("tp_pe"), sg("tp_act"), sg("rope_dve")
        diag_pool, m1_pe, mmax_dve, mexp_act, ms_dve = (sg("diag_pool"), sg("m1_pe"), sg("mmax_dve"), sg("mexp_act"),
                                                        sg("ms_dve"))
        kw_pool, m2_pe, sT_act, m3_pe, mh_dve = sg("kw_pool"), sg("m2_pe"), sg("sT_act"), sg("m3_pe"), sg("mh_dve")
        mc_act, ct_dve, m_out = sg("mc_act"), sg("ct_dve"), sg("m_out", 16)
        ct_in = sg("ct_in", 16)
        bz_pool = sg("bz_pool")
        keys_in, vals_in, bias_in = sg("keys_in", 16), sg("vals_in", 16), sg("bias_in", 16)
        kv_out = {ty: sg(f"kv_out{ty}", 16) for ty in "BCD"}
        sc_pe, sa_dve, nm_dve, ex_act, pn_dve = sg("sc_pe"), sg("sa_dve"), sg("nm_dve"), sg("ex_act"), sg("pn_dve")
        pt_pe, pa_act, pb_dve, pv_pe = sg("pt_pe"), sg("pa_act"), sg("pb_dve"), sg("pv_pe")
        oh_act, ol_dve, yd_act = sg("oh_act"), sg("ol_dve"), sg("yd_act")
        hs_dve, hr_pool, tanh_act, hn_dve = sg("hs_dve"), sg("hr_pool"), sg("tanh_act"), sg("hn_dve")
        to_pe, th_act, tl_dve = sg("to_pe"), sg("th_act"), sg("tl_dve")
        lam_dve, lam_act = sg("lam_dve"), sg("lam_act")
        gt_pe, gr_act, g_out, g_in = sg("gt_pe"), sg("gr_act"), sg("g_out", 16), sg("g_in", 16)
        mt_pe, mh_act, ml_dve = sg("mt_pe"), sg("mh_act"), sg("ml_dve")
        sp_pe, sp_act = sg("sp_pe"), sg("sp_act")
        rt_pe, rt_dve, rt_act = sg("rt_pe"), sg("rt_dve"), sg("rt_act")
        yz_pool = sg("yz_pool")
        nb_pe, nbh_act, nbl_dve = sg("nb_pe"), sg("nbh_act"), sg("nbl_dve")
        rg_dve, rc_pe, gidx_dve = sg("rg_dve"), sg("rc_pe"), sg("gidx_dve")
        e_unit, e_lo = sg("e_unit", credit=RAW), sg("e_lo")
        e_tanh, e_dve, e_hid, e_pt = sg("e_tanh"), sg("e_dve"), sg("e_hid", credit=2), sg("e_pt")
        e_hh, e_hl, e_y = sg("e_hh"), sg("e_hl", credit=1), sg("e_y", credit=6)
        q_sel, q_g, q_hg, q_t = sg("q_sel"), sg("q_g"), sg("q_hg"), sg("q_t")
        q_hi, q_lo, q_st, q_sa = sg("q_hi"), sg("q_lo"), sg("q_st", credit=1), sg("q_sa")
        q_yh, q_yl, q_s = sg("q_yh"), sg("q_yl", credit=2), sg("q_s")
        layer_end = sg("layer_end", credit=1)
        dve_ord, act_ord, pool_ord = sg("dve_ord"), sg("act_ord"), sg("pool_ord")
        const_in = ctx.enter_context(nc.semaphore("const_in"))
        cond_act = ctx.enter_context(nc.semaphore("cond_act"))
        start_dve = ctx.enter_context(nc.semaphore("start_dve"))
        cond_dve = ctx.enter_context(nc.semaphore("cond_dve"))
        fin_sq_act = ctx.enter_context(nc.semaphore("fin_sq_act"))
        fin_rstd_pool = ctx.enter_context(nc.semaphore("fin_rstd_pool"))
        fin_gain_in = ctx.enter_context(nc.semaphore("fin_gain_in"))
        fin_y_dve = ctx.enter_context(nc.semaphore("fin_y_dve"))
        fin_out = ctx.enter_context(nc.semaphore("fin_out"))
        NCONST = 9

        def unit_done(g):
            c, i, n = GEMM[g]
            if i == n - 1:
                return tile_pe, TILES * c + TILES - 1
            return unit_pe, g - c

        def evacuated(c, t):
            if CHUNKS[c][0] in ("proj", "gate"):
                return ev_act, TILES * sum(CHUNKS[i][0] in ("proj", "gate") for i in range(c)) + t
            return ev_dve, TILES * sum(CHUNKS[i][0] not in ("proj", "gate") for i in range(c)) + t

        def pooled(c, t):
            n = sum(CHUNKS[i][0] == "wout" or (CHUNKS[i][0] == "branch" and CHUNKS[i][1][0] > 0) for i in range(c))
            return TILES * n + t

        def load_bias(sp, need, l, b):
            ty, t, j = AU[BIASED[b]]
            if ty == "B":
                bias_in.of(sp.dma_start(bias[:, :, 0:T_LAT], a["nat_bias"][bass.ds((l * 2 + t) * 4 + j, 1)]
                                        .rearrange("a p m n -> p (a m) n")))
            else:
                for m in range(2):
                    bias_in.of(sp.dma_start(bias[:, m, 0:T_LAT], a["swa_mask"][t]))

        def bias_index(b):
            return b if b < 8 else (9 if b < 12 else 11)

        def route(dve, need, own, tt):
            V = nc.vector
            need(rt_pe, 0)
            own(V.tensor_copy(rt[:, :, :], O[:, 0:60].rearrange("p (t n) -> p t n", t=TILES)))
            gl, el = rt[:, :, 0:4], rt[:, :, 4:20]

            def b4(c):
                return c.to_broadcast([P, TILES, 4])


            def first_max(values, mx, eq):
                own(V.tensor_reduce(mx, values, AX, ALU.max))
                own(tt(eq, values, b4(mx), ALU.is_equal))
                own(tt(eq, eq, order[:, 0:4].unsqueeze(1).to_broadcast([P, TILES, 4]), ALU.mult))
                own(V.tensor_reduce(rw[:, :, 7:8], eq, AX, ALU.max))
                own(tt(eq, eq, b4(rw[:, :, 7:8]), ALU.is_equal))

            gsel, sel1, sel2 = rw[:, :, 16:20], rw[:, :, 20:24], rw[:, :, 24:28]
            gmax, m1, m2 = rw[:, :, 5:6], rw[:, :, 6:7], rw[:, :, 13:14]
            first_max(gl, gmax, gsel)
            rg_dve.of(tt(rw[:, :, 8:12], gl, b4(gmax), ALU.subtract))
            prod = rw[:, :, 32:48].rearrange("p t (g e) -> p t g e", g=4)
            for t in range(TILES):
                own(tt(prod[:, t], el[:, t].rearrange("p (g e) -> p g e", g=4),
                       gsel[:, t].unsqueeze(2).to_broadcast([P, 4, 4]), ALU.mult))
                own(V.tensor_reduce(rw[:, t, 28:32], prod[:, t].rearrange("p g e -> p e g"), AX, ALU.add))
            eg = rw[:, :, 28:32]
            first_max(eg, m1, sel1)
            own(V.tensor_scalar(rw[:, :, 48:52], sel1, NEG, None, ALU.mult))
            own(tt(rw[:, :, 48:52], rw[:, :, 48:52], eg, ALU.add))
            first_max(rw[:, :, 48:52], m2, sel2)
            rt_dve.of(tt(rw[:, :, 12:13], m2, m1, ALU.subtract))
            need(rt_act, 0)
            own(V.tensor_reduce(rw[:, :, 14:15], rw[:, :, 0:4], AX, ALU.add))
            own(V.tensor_scalar(rw[:, :, 15:16], rw[:, :, 4:5], 1.0, 2.0, ALU.add, ALU.mult))
            own(tt(rw[:, :, 14:15], rw[:, :, 14:15], rw[:, :, 15:16], ALU.mult))
            own(V.reciprocal(rw[:, :, 15:16], rw[:, :, 14:15]))
            own(tt(sel2, sel2, b4(rw[:, :, 4:5]), ALU.mult))
            own(tt(sel1, sel1, sel2, ALU.add))
            own(tt(sel1, sel1, b4(rw[:, :, 15:16]), ALU.mult))
            need(rc_pe, 0)
            cum, tot = rw[:, :, 52:56], rw[:, :, 56:60]
            own(V.tensor_copy(cum, O[:, 128:140].rearrange("p (t n) -> p t n", t=TILES)),
                V.tensor_copy(tot, O[:, 140:152].rearrange("p (t n) -> p t n", t=TILES)))
            two, size, tiles, base, first, slot = (rw[:, 1, 60:64], rw[:, 0, 60:64], rw[:, 0, 64:68], rw[:, 0, 68:72],
                                                   rw[:, 0, 72:72 + NT], rw[:, :, 79:80])
            own(tt(cum[:, 1], cum[:, 1], tot[:, 0], ALU.add), tt(two, tot[:, 0], tot[:, 1], ALU.add))
            own(tt(cum[:, 2], cum[:, 2], two, ALU.add), tt(size, two, tot[:, 2], ALU.add))
            own(V.tensor_scalar(tiles, size, 0.5, None, ALU.is_gt))
            for i in range(1, TILES):
                own(V.scalar_tensor_tensor(tiles, size, 128.0 * i + 0.5, tiles, ALU.is_gt, ALU.add))
            own(V.tensor_scalar(tiles, tiles, 128.0, None, ALU.mult))
            own(V.tensor_scalar(base[:, 0:1], tiles[:, 0:1], 0.0, None, ALU.mult),
                V.tensor_copy(base[:, 1:2], tiles[:, 0:1]))
            own(tt(base[:, 2:3], base[:, 1:2], tiles[:, 1:2], ALU.add))
            own(tt(base[:, 3:4], base[:, 2:3], tiles[:, 2:3], ALU.add))
            at = order[:, 4:4 + NT]
            own(V.tensor_scalar(first, at, base[:, 1:2], None, ALU.is_ge))
            for g in (2, 3):
                own(V.scalar_tensor_tensor(first, at, base[:, g:g + 1], first, ALU.is_ge, ALU.add))
            own(V.tensor_scalar(first, first, float(UT), None, ALU.mult))
            for k in range(UT // RAW):
                gidx_dve.of(V.tensor_scalar(gidx[:, :].rearrange("p (t k) -> p t k", t=NT)[:, :, k:k + 1],
                                            first.unsqueeze(2), float(RAW * k), None, ALU.add))
            own(tt(cum, cum, base.unsqueeze(1).to_broadcast([P, TILES, GRP]), ALU.add))
            own(tt(cum, cum, gsel, ALU.mult))
            own(V.tensor_reduce(slot, cum, AX, ALU.add))
            for i in range(NT):
                ins = V.tensor_scalar(rel[:, i, :].unsqueeze(2), slot, -128.0 * i, None, ALU.add)
            own(ins)

        block = ctx.enter_context(nc.Block())

        @block.sync
        def _(sp):
            rows = a["tokens"]
            for dst, src in ((ident[:, :], a["ident"]), (tri[:, :, :], a["tri"]), (cmask[:, :, :], a["cmask"]),
                             (rope_t[:, :, :], a["rope"]), (cond[:, :, :], a["cond"]),
                             (order[:, :], a["order"]), (x[:, 0, :], rows[0]), (x[:, 1, :], rows[1]), (x[:, 2, :], rows[2])):
                sp.dma_start(dst, src).then_inc(const_in, 16)
            with sp.Fori(0, DEPTH) as l:
                def need(s, i):
                    sp.wait_ge(s.handle, s.value(l, i))

                def load_gate(i):
                    for c in range(2):
                        src = a["g_scratch"][i].rearrange("(j c) n -> c j n", c=2)[c]
                        g_in.of(sp.dma_start(gbc[:, c, :].rearrange("p (j n) -> p j n", j=KD),
                                             bass.AP(src.tensor, src.offset, [[0, P], [2 * P, KD], [1, P]])))

                def needs(*pairs):
                    for s, i in pairs:
                        sp.wait_ge(s.handle, s.value(l, i))

                gs = [None if s[0] == "mod" else s[1] for s in STREAM]

                def released(p):
                    if p < 0:
                        sp.wait_ge(*e_unit.in_tile(l, 0, UT, p))
                    elif gs[p] is None:
                        sp.wait_ge(*mod_pe.at(l, STREAM[p][1]))
                    else:
                        sp.wait_ge(*lo_done.at(l, gs[p]))

                def load(p):
                    w_in[p % RAW].of(sp.dma_start(raw[:, p % RAW, :], a["units"][bass.ds(l * NU + p, 1), :, :]
                                                  .rearrange("a p n -> p (a n)")))

                def layer_of(name, n=1):
                    return a[name][bass.ds(l, 1)]

                for p in range(RAW):
                    released(p - RAW)
                    load(p)
                p = 0
                for s in SCHEDULE:
                    if s[0] in ("mod", "gemm"):
                        if p + RAW < len(STREAM):
                            released(p)
                            load(p + RAW)
                        p += 1
                    elif s == ("dma", "params"):
                        sp.wait_ge(*layer_end.at(l, -1))
                        par_in.of(sp.dma_start(pcol[:, :], layer_of("pcol").rearrange("a p n -> p (a n)")))
                        par_in.of(sp.dma_start(prow[:, :], layer_of("prow").rearrange("a n -> (a n)").partition_broadcast(P)))
                        par_in.of(sp.dma_start(small[:, :, :], layer_of("small").rearrange("a p k n -> p (a k) n")))
                        sp.wait_ge(const_in, 16 * NCONST)
                    elif s == ("dma", "saveX"):
                        x_saved.of(sp.dma_start(a["x_scratch"].rearrange("t p n -> p t n"), x))
                    elif s == ("dma", "stateC"):
                        ct_in.of(sp.dma_start(cT[:, :, :], layer_of("state_C").rearrange("a p h n -> p (a h) n")))
                    elif s == ("dma", "outB"):
                        for w, n in (("k", "Bk"), ("v", "Bv")):
                            need(*evacuated(CHUNK_NO[n], 2))
                            kv_out["B"].of(sp.dma_start(out["nat_" + w][bass.ds(l, 1)].rearrange("a p n -> p (a n)"),
                                                        slot[n][:, 2, :]))
                    elif s == ("dma", "outC"):
                        need(*evacuated(CHUNK_NO["Ckv"], 2))
                        for w, o in (("k", 0), ("v", 128)):
                            kv_out["C"].of(sp.dma_start(out["swa_" + w][bass.ds(l, 1)].rearrange("a p n -> p (a n)"),
                                                        Ckv[:, 2, o:o + 128]))
                    elif s == ("dma", "outD"):
                        for w, n in (("k", "Dk"), ("v", "Dv")):
                            need(*evacuated(CHUNK_NO[n], 2))
                            kv_out["D"].of(sp.dma_start(out["diff_" + w][bass.ds(l, 1)].rearrange("a p n -> p (a n)"),
                                                        slot[n][:, 2, :]))
                    elif s[0] == "m3" and MU[s[1]][1] == 2:
                        d = MU[s[1]][0]
                        sp.wait_ge(*mc_act.at(l, d))
                        m_out.of(sp.dma_start(out["C"][bass.ds(l * 2 + d, 1)].rearrange("a h v k -> v (a h) k"),
                                              cst.rearrange("p (h k) -> p h k", h=H_A)))
                        m_out.of(sp.dma_start(out["n"][bass.ds(l * 2 + d, 1)], nrow[0:1, d, :]))
                        sp.wait_ge(*mh_dve.at(l, s[1]))
                        m_out.of(sp.dma_start(out["m"][bass.ds(l * 2 + d, 1)], mst[0:1, 8 + 4 * d:12 + 4 * d]))
                    elif s[0] == "dma" and s[1] in ("loadB", "keysC", "keysD"):
                        ty = s[1][-1]
                        i = "BCD".index(ty)
                        if i:
                            sp.wait_ge(*sc_pe.at(l, 12 * i - 1))
                        keys_in.of(sp.dma_start(kT[:, :, 384:512], a["keys"][bass.ds(l * 3 + i, 1)]
                                                .rearrange("a p j n -> p (a j) n")))
                        if i == 0:
                            sp.wait_ge(*m3_pe.at(l, 3))
                            vals_in.of(sp.dma_start(vc[:, :], a["vals"][bass.ds(l * 3 + i, 1)]
                                                    .rearrange("a p n -> p (a n)")))
                            sp.wait_ge(*bz_pool.at(l, 0))
                            load_bias(sp, need, l, 0)
                    elif s[0] == "dma" and s[1] in ("valuesC", "valuesD"):
                        i = "BCD".index(s[1][-1])
                        sp.wait_ge(*pv_pe.at(l, 12 * i - 1))
                        vals_in.of(sp.dma_start(vc[:, :], a["vals"][bass.ds(l * 3 + i, 1)]
                                                .rearrange("a p n -> p (a n)")))
                    elif s[0] == "sc" and s[1] in BIASED:
                        b = BIASED.index(s[1])
                        if b < 8 or b == 11:
                            sp.wait_ge(*sa_dve.at(l, b))
                            load_bias(sp, need, l, b + 1)
                    elif s[0] == "gt":
                        i = s[1]
                        if i:
                            needs((gr_act, i), (gidx_dve, UT // RAW - 1))
                        else:
                            sp.wait_ge(*gr_act.at(l, i))
                        g_out.of(sp.dma_start(a["g_scratch"][i], grow[:, :]))
                    elif s == ("dma", "gate1"):
                        needs((g_out, 0), (pv_pe, 23))
                        load_gate(0)
                    elif s == ("dma", "loadX"):
                        needs((kv_out["D"], 1), (th_act, 7))
                        x_in.of(sp.dma_start(x, a["x_scratch"].rearrange("t p n -> p t n")))
                    elif s == ("experts",):
                        def expert_load(r, block):
                            w_in[r].of(sp.dma_start(
                                raw[:, r, :], a["units"][bass.ds(block + (l * NU + len(STREAM) + r), 1), :, :]
                                .rearrange("a p n -> p (a n)")))

                        def block_at(b):
                            return sp.value_load(gidx[0:1, bass.ds(b, 1)], min_val=0, max_val=GRP * UT - RAW)

                        block = block_at(0)
                        for r in range(RAW):
                            released(len(STREAM) - RAW + r)
                            expert_load(r, block)
                        sp.wait_ge(*g_out.at(l, 1))
                        load_gate(1)
                        with sp.Fori(0, NBLOCK - 1) as b:
                            block = block_at(b + 1)
                            for r in range(RAW):
                                sp.wait_ge(e_unit.handle, (l * NBLOCK + b) * RAW + (r + 1 + e_unit.credit))
                                expert_load(r, block)
                        for r in range(RAW):
                            w_in[r].n += NBLOCK - 2
            sp.wait_ge(layer_end.handle, DEPTH + 1)
            sp.dma_start(yacc[:, 0, :], a["norm_final"].partition_broadcast(P)).then_inc(fin_gain_in, 16)
            for t in range(TILES):
                sp.wait_ge(fin_y_dve, t + 1)
                sp.dma_start(out["tokens"][t], xn[:, t, :]).then_inc(fin_out, 16)
            sp.wait_ge(fin_out, 16 * TILES)
            for s, n in ((kv_out["B"], 2), (kv_out["C"], 2), (kv_out["D"], 2), (m_out, 6), (x_saved, 1), (g_out, 2)):
                sp.wait_ge(s.handle, 16 * n * DEPTH)

        @block.gpsimd
        def _(pool):
            pool.memset(ones[:, :], 1.0).then_inc(start_dve, 1)
            for i, v in enumerate((-0.5, 1.0 / D, 1.0 / P, EPS, 0.5)):
                pool.memset(cval[:, i, :], v).then_inc(start_dve, 1)
            pool.memset(ms[:, :, :], 0.0).then_inc(start_dve, 1)
            pool.memset(zst[:, :], 0.0).then_inc(start_dve, 1)
            pool.memset(dummy[:, 0:1], 0.0).then_inc(lo_done.handle, RAW)
            pool.memset(dummy[:, 9:10], 0.0).then_inc(e_unit.handle, RAW)
            with pool.Fori(0, DEPTH) as l:
                chain = [0]

                def need(s, i):
                    pool.wait_ge(s.handle, s.value(l, i))

                def own(ins):
                    pool_ord.of(ins)
                    chain[0] += 1
                    pool.wait_ge(*pool_ord.at(l, chain[0] - 1))

                def split(g):
                    pool.wait_ge(*hi_done.at(l, g))
                    k = g % CONV
                    lo_done.of(nc.gpsimd.tensor_tensor(wlo[:, k, :], raw[:, POS_OF[g] % RAW, :], whi[:, k, :].bitcast(F32),
                                                       ALU.subtract))

                def rstd(dst, src, n, width, signal):
                    own(nc.gpsimd.tensor_tensor(dst, src, cval[:, 1 if n == D else 2, 0:width], ALU.mult))
                    own(nc.gpsimd.tensor_tensor(dst, dst, cval[:, 3, 0:width], ALU.add))
                    return nc.gpsimd.tensor_tensor(dst, dst, cval[:, 0, 0:width], ALU.pow)

                first = True
                for s in SCHEDULE:
                    if s[0] == "norm":
                        pool.wait_ge(*sq_act.at(l, 3 * s[1] + 2))
                        if first:
                            pool.wait_ge(start_dve, 6)
                            first = False
                        rstd_pool.of(rstd(st[:, 0:3], st[:, 0:3], D, 3, None))
                        if s[1] == 0:
                            split(0)
                            split(1)
                        for c in range(1, KD, 2):
                            pool.wait_ge(*hf_dve.at(l, KD * s[1] + c))
                            pool.wait_ge(*hh_act.at(l, KD * s[1] + c))
                            hl_pool.of(nc.gpsimd.tensor_tensor(hlo[:, c, :], probT[:, 1, 0, :],
                                                               hhi[:, c, :].bitcast(F32), ALU.subtract))
                    elif s[0] == "gemm":
                        g = s[1]
                        if g + 2 < NG:
                            split(g + 2)
                        c, i, n = GEMM[g]
                        kind, arg = CHUNKS[c][:2]
                        if i == n - 1 and kind == "branch" and arg[0] > 0:
                            for t in range(TILES):
                                need(*evacuated(c, t))
                                ev_pool.of(nc.gpsimd.tensor_tensor(merged[arg[1]][:, t, :], merged[arg[1]][:, t, :],
                                                                   sig[:, t, :], ALU.add))
                        if i == n - 1 and kind == "wout":
                            for t in range(TILES):
                                need(*evacuated(c, t))
                                xs = x[:, t, arg * 512:(arg + 1) * 512]
                                ev_pool.of(nc.gpsimd.tensor_tensor(xs, xs, sig[:, t, :], ALU.add))
                    elif s[0] == "m1":
                        m = s[1]
                        d, t = MU[m]
                        pool.wait_ge(*cc_dve.at(l, 0))
                        if m:
                            pool.wait_ge(*m1_pe.at(l, m - 1))
                        dv = bias[:, :, :].rearrange("p a n -> p (a n)")[:, 0:512].rearrange("p (h n) -> p h n", h=4)
                        diag_pool.of(nc.gpsimd.tensor_tensor(
                            dv, ident[:, :].unsqueeze(1).to_broadcast([P, 4, P]),
                            cc[:, t, 4 * d:4 * d + 4].unsqueeze(2).to_broadcast([P, 4, P]), ALU.mult))
                    elif s[0] == "m2" and s[1] in MUPD:
                        m = s[1]
                        d, t = MU[m]
                        pool.wait_ge(*mexp_act.at(l, m))
                        need(*evacuated(CHUNK_NO["Ak"], t))
                        if m:
                            pool.wait_ge(*m3_pe.at(l, m - 1))
                        kw_pool.of(nc.gpsimd.tensor_tensor(
                            vc[:, :].rearrange("p (h n) -> p h n", h=4),
                            slot["Ak"][:, t, :].rearrange("p (h n) -> p h n", h=4),
                            ms[:, m % 2, 24:28].unsqueeze(2).to_broadcast([P, 4, P]), ALU.mult))
                    elif s == ("dma", "loadB"):
                        pool.wait_ge(*m1_pe.at(l, len(MU) - 1))
                        wide1 = ones[:, :].unsqueeze(1).to_broadcast([P, 2, P])
                        bz_pool.of(nc.gpsimd.tensor_tensor(bias[:, :, T_LAT:], wide1, wide1, ALU.subtract))
                    elif s[0] == "hr":
                        i = s[1]
                        pool.wait_ge(*hs_dve.at(l, 3 * i + 2))
                        own(rstd(st[:, 3:15], st[:, 3:15], P, 12, None))
                        f = cval[:, 4, :] if i == 0 else row("lam", 1, 2).to_broadcast([P, 12])
                        hr_pool.of(nc.gpsimd.tensor_tensor(st[:, 3:15], st[:, 3:15], f, ALU.mult))
                    elif s == ("route",):
                        pool.wait_ge(*th_act.at(l, 7))
                        pool.wait_ge(*mt_pe.at(l, 7))
                        nc.gpsimd.tensor_tensor(dummy[:, 0:1], ones[:, 0:1], ones[:, 0:1], ALU.mult)
                        yz_pool.of(nc.gpsimd.memset(yacc, 0.0))
                    elif s == ("experts",):
                        def low(i, n):
                            pool.wait_ge(hi_done.handle, hi_done.value(l, NG + n) + i * UT)
                            lo_done.of(nc.gpsimd.tensor_tensor(wlo[:, n % CONV, 0:POOL_COLS], raw[:, n % RAW, 0:POOL_COLS],
                                                               whi[:, n % CONV, 0:POOL_COLS].bitcast(F32), ALU.subtract))

                        for n in range(3):
                            low(0, n)
                        with pool.Fori(0, NT - 1) as i:
                            for n in range(3, UT + 3):
                                low(i, n)
                        for n in range(3, UT):
                            low(NT - 1, n)
                        lo_done.n += (NT - 2) * UT

            pool.wait_ge(fin_sq_act, TILES)
            nc.gpsimd.tensor_scalar(st[:, 0:3], st[:, 0:3], 1.0 / D, EPS, ALU.mult, ALU.add).then_inc(fin_rstd_pool, 1)
            pool.wait_ge(fin_rstd_pool, 1)
            nc.gpsimd.tensor_tensor(st[:, 0:3], st[:, 0:3], cval[:, 0, 0:3], ALU.pow).then_inc(fin_rstd_pool, 1)

        @block.scalar
        def _(act):
            act.wait_ge(const_in, 16 * NCONST)
            nc.scalar.activation(cond_t, cond[:, :, :], ACT.Tanh, scale=0.5).then_inc(cond_act, 1)
            nc.scalar.activation(dummy[:, 1:2], ident[:, 0:1], ACT.Copy).then_inc(hi_done.handle, RAW)
            with act.Fori(0, DEPTH) as l:
                chain = [0]

                def need(s, i):
                    act.wait_ge(s.handle, s.value(l, i))

                def own(ins):
                    act_ord.of(ins)
                    chain[0] += 1
                    act.wait_ge(*act_ord.at(l, chain[0] - 1))

                def split(g):
                    p = POS_OF[g]
                    w = w_in[p % RAW]
                    act.wait_ge(w.handle, w.value(l, p // RAW))
                    if g >= CONV:
                        need(*unit_done(g - CONV))
                    hi_done.of(nc.scalar.activation(whi[:, g % CONV, :], raw[:, p % RAW, :], ACT.Copy))

                def small_out(i, w):
                    act.wait_ge(*sp_pe.at(l, i))
                    sp_act.of(nc.scalar.activation(prob[0:w, 0, 0, :], O[0:w, 0:384], ACT.Copy))

                for s in SCHEDULE:
                    if s[0] == "norm":
                        w = s[1]
                        if w == 0:
                            act.wait_ge(layer_end.handle, layer_end.value(l, -1))
                        else:
                            need(kv_out["B"], 1)
                        for t in range(TILES):
                            if w == 1:
                                act.wait_ge(*ev_pool.at(l, pooled(CHUNK_NO["wout", 1], t)))
                            sq_act.of(nc.scalar.activation(xn[:, t, :], x[:, t, :], ACT.Square,
                                                           accum_out=st[:, t:t + 1]))
                        if w == 0:
                            split(0)
                            split(1)
                        def back(c):
                            act.wait_ge(*nb_pe.at(l, c))
                            nbh_act.of(nc.scalar.activation(hth[:, :, c * P:(c + 1) * P], S[:, c % 2, 0:384]
                                                            .rearrange("p (t n) -> p t n", t=TILES), ACT.Copy))

                        act.wait_ge(*rstd_pool.at(l, w))
                        xn_act.of(nc.scalar.activation(xn[:, 1, :], x[:, 1, :], ACT.Copy, scale=st[:, 1:2]))
                        for c in range(KD):
                            act.wait_ge(*hf_dve.at(l, KD * w + c))
                            hh_act.of(nc.scalar.activation(hhi[:, c, :], probT[:, c % 2, 0, :], ACT.Copy))
                            if w and c:
                                back(c - 1)
                        if w:
                            back(KD - 1)
                    elif s[0] == "gemm":
                        g = s[1]
                        if g + 2 < NG:
                            split(g + 2)
                        c, i, n = GEMM[g]
                        kind, arg = CHUNKS[c][:2]
                        if i == n - 1 and kind in ("proj", "gate"):
                            for t in range(TILES):
                                act.wait_ge(*tile_pe.at(l, TILES * c + t))
                                if kind == "gate":
                                    if CHUNKS[c - 1][0] == "proj":
                                        act.wait_ge(*rope_dve.at(l, 8))
                                    if c >= 14 and CHUNKS[c - 1][0] == "branch":
                                        cb = c - 1
                                        if CHUNKS[cb][1][0] > 0:
                                            act.wait_ge(*ev_pool.at(l, pooled(cb, t)))
                                        else:
                                            need(*evacuated(cb, t))
                                    ev_act.of(nc.scalar.activation(sig[:, t, :], G[:, t, :], ACT.Tanh, scale=0.5))
                                else:
                                    w = CHUNKS[c][2]
                                    if arg == "Aq" and t == 0:
                                        act.wait_ge(*x_saved.at(l, 0))
                                    if t == 0 and arg == "Dq":
                                        act.wait_ge(*m3_pe.at(l, 3))
                                    if t == 0 and arg == "Dk":
                                        act.wait_ge(*m3_pe.at(l, 5))
                                    if t == 0 and arg == "Dv":
                                        act.wait_ge(*to_pe.at(l, 3))
                                    ev_act.of(nc.scalar.activation(
                                        slot[arg][:, t, :], G[:, t, 0:w], ACT.Copy,
                                        scale=DH_A ** -0.5 if arg == "Ak" else 1.0))
                    elif s == ("prepare",):
                        act.wait_ge(*par_in.at(l, 2))
                        smh_act.of(nc.scalar.activation(smhi[:, :, :], small[:, :, :], ACT.Copy))
                        act.wait_ge(*lam_dve.at(l, 0))
                        lam_act.of(nc.scalar.activation(lam[:, 2:4], lam[:, 0:2], ACT.Exp))
                    elif s[0] == "modv":
                        g = s[1]
                        act.wait_ge(*mod_pe.at(l, KD * g + KD - 1))
                        if g:
                            act.wait_ge(*modt_pe.at(l, g - 1))
                        if g == 2:
                            act.wait_ge(*tp_pe.at(l, TP_NO["C", "k", 1]))
                        mod_act.of(nc.scalar.activation(mrow, T[:, 0, 256:512] if g == 5 else O[:, 256:512], ACT.Copy))
                    elif s == ("mgate",):
                        small_out(0, 16)
                        act.wait_ge(*mg_dve.at(l, 0))
                        own(nc.scalar.activation(ga[:, :, :], ga[:, :, :], ACT.Exp))
                        ln_act.of(nc.scalar.activation(ga[:, :, :], ga[:, :, :], ACT.Ln, bias=1.0))
                    elif s[0] == "tp":
                        ty, w, j = s[1:]
                        i = TP_NO[ty, w, j]
                        act.wait_ge(*tp_pe.at(l, i))
                        if w == "q":
                            tp_act.of(nc.scalar.activation(qT[:, j, :], T[:, i % 2, 0:384], ACT.Copy,
                                                           scale=1.0 if ty == "A" else 64 ** -0.5))
                        else:
                            tp_act.of(nc.scalar.activation(kT[:, j, 0:384], T[:, i % 2, 0:384], ACT.Copy))
                    elif s[0] == "m1":
                        m = s[1]
                        act.wait_ge(*mmax_dve.at(l, m))
                        W = prob[:, m % 2].rearrange("p a n -> p (a n)")
                        for h in range(4):
                            nc.scalar.activation(W[:, h * P:(h + 1) * P], W[:, h * P:(h + 1) * P], ACT.Exp,
                                                 bias=ms[:, m % 2, 8 + h:9 + h])
                        mexp_act.of(nc.scalar.activation(ms[:, m % 2, 16:32], ms[:, m % 2, 32:48], ACT.Exp))
                    elif s[0] == "m2":
                        m = s[1]
                        act.wait_ge(*m2_pe.at(l, m))
                        sT_act.of(nc.scalar.activation(probT[:, m % 2].rearrange("p a n -> p (a n)")[:, 0:512],
                                                       T[:, 0, :], ACT.Copy))
                    elif s[0] == "m3" and MU[s[1]][1] == 2:
                        m = s[1]
                        d = MU[m][0]
                        act.wait_ge(*m3_pe.at(l, m))
                        if d:
                            act.wait_ge(*m_out.at(l, 2))
                        nc.scalar.activation(nrow[0:1, d, :], S[0:1, 0, :], ACT.Copy)
                        mc_act.of(nc.scalar.activation(cst, T[:, 0, :], ACT.Copy))
                    elif s[0] == "sc":
                        u = s[1]
                        ty, t, j = AU[u]
                        act.wait_ge(*nm_dve.at(l, u))
                        w = 384 if t < 2 else 128
                        for m in range(2):
                            src = prob[:, u % 2, m, 0:w] if u in BIASED else S[:, m, 0:w]
                            e = nc.scalar.activation(prob[:, u % 2, m, 0:w], src, ACT.Exp,
                                                     bias=am[:, u % 2, m:m + 1], accum_out=am[:, u % 2, 2 + m:3 + m])
                        if ty == "C":
                            e = nc.scalar.activation(am[:, u % 2, 6:8], am[:, u % 2, 4:6], ACT.Exp)
                        ex_act.of(e)
                    elif s[0] == "pt":
                        u = s[1]
                        w = 384 if AU[u][1] < 2 else 128
                        act.wait_ge(*pt_pe.at(l, u))
                        pa_act.of(nc.scalar.activation(probT[:, u % 2, 0, 0:w], T[:, 0, 0:w], ACT.Copy))
                    elif s[0] == "pv":
                        u = s[1]
                        ty, t, j = AU[u]
                        act.wait_ge(*pv_pe.at(l, u))
                        if ty == "D":
                            yd_act.of(nc.scalar.activation(slot["Dq"][:, t, j * P:(j + 1) * P], O[:, 0:P], ACT.Copy))
                        else:
                            n = TYPES.index(ty)
                            if u == 12:
                                need(kv_out["B"], 1)
                            oh_act.of(nc.scalar.activation(bhi[n][:, j, t * P:(t + 1) * P], O[:, 0:P], ACT.Copy))
                    elif s == ("hn", 0):
                        need(*evacuated(CHUNK_NO["Ao"], 2))
                        tanh_act.of(nc.scalar.activation(slot["Ao"], slot["Ao"], ACT.Tanh, scale=0.5))
                    elif s[0] == "to":
                        i, j = s[1:]
                        act.wait_ge(*to_pe.at(l, 4 * i + j))
                        if (i, j) == (1, 0):
                            need(*unit_done(LAST_UNIT[CHUNK_NO["branch", (0, 1)]]))
                        th_act.of(nc.scalar.activation(bhi[0][:, j, :], T[:, j % 2, 0:384], ACT.Copy))
                    elif s[0] == "gt":
                        act.wait_ge(*gt_pe.at(l, s[1]))
                        if s[1]:
                            act.wait_ge(*g_out.at(l, 0))
                        gr_act.of(nc.scalar.activation(grow[:, :], T[0:16, 1, 0:P], ACT.Copy))
                    elif s[0] == "mt":
                        c = s[1]
                        act.wait_ge(*mt_pe.at(l, c))
                        mh_act.of(nc.scalar.activation(hhi[:, c, :], T[:, c % 2, 0:384], ACT.Copy, scale=0.5))
                    elif s == ("route",):
                        small_out(1, 20)
                        act.wait_ge(*rt_dve.at(l, 0))
                        rt_act.of(nc.scalar.activation(rw[:, :, 0:5], rw[:, :, 8:13], ACT.Exp))
                    elif s == ("experts",):
                        def high(i, n):
                            p = len(STREAM) + n
                            w = w_in[p % RAW]
                            act.wait_ge(w.handle, w.value(l, p // RAW) + i * (16 * (UT // RAW)))
                            act.wait_ge(*e_unit.in_tile(l, i, UT, n - CONV))
                            hi_done.of(nc.scalar.activation(whi[:, n % CONV, :], raw[:, n % RAW, :], ACT.Copy))

                        def gathered(i):
                            for hf in range(2):
                                act.wait_ge(*q_g.in_tile(l, i, 2, hf))
                                q_hg.of(nc.scalar.activation(hg[:, hf, :], (T[:, 1, :], G[:, 2, :])[hf], ACT.Copy))

                        def turned(i):
                            for hf in range(2):
                                act.wait_ge(*q_t.in_tile(l, i, 2, hf))
                                q_hi.of(nc.scalar.activation(
                                    hhi[:, 4 * hf:4 * hf + 4, 0:P],
                                    (T[:, 1, :], G[:, 2, :])[hf].rearrange("p (c n) -> p c n", c=4), ACT.Copy))

                        def selection(i):
                            act.wait_ge(*q_st.in_tile(l, i, 1, 0))
                            nc.scalar.activation(selT[:, :], O[:, 0:TILES * P], ACT.Copy)
                            q_sa.of(nc.scalar.activation(gate[:, :], O[:, TILES * P:TILES * P + GRP], ACT.Copy))

                        def one_tile(i, last):
                            def tanh(e):
                                act.wait_ge(*e_unit.in_tile(l, i, UT, UNITS.index((e, 3))))
                                e_tanh.of(nc.scalar.activation(gact[:, e % 2, :], G[:, e % 2, 0:DEXP], ACT.Tanh, scale=0.5))

                            def turned_hid(e):
                                act.wait_ge(*e_pt.in_tile(l, i, GRP, e))
                                e_hh.of(nc.scalar.activation(ehi[:, :, 0:P], T[:, 0, 0:2 * P]
                                                             .rearrange("p (f n) -> p f n", f=2), ACT.Copy))

                            for n in range(3, UT):
                                high(i, n)
                                for e in range(GRP):
                                    if n == UNITS.index((e, 3)) + 3:
                                        tanh(e)
                                    if n == (8, 14, 20, UT)[e]:
                                        turned_hid(e)
                            if not last:
                                gathered(i + 1)
                            turned_hid(GRP - 1)
                            if not last:
                                high(i, UT)
                                high(i, UT + 1)
                            for hf in range(2):
                                act.wait_ge(*e_unit.in_tile(l, i, UT, UT - 1))
                                q_yh.of(nc.scalar.activation(yh[:, hf, :], S[:, hf, :], ACT.Copy))
                            if not last:
                                turned(i + 1)
                                high(i, UT + 2)
                                selection(i + 1)

                        need(*unit_done(NG - 1))
                        for n in range(3):
                            high(0, n)
                        gathered(0)
                        turned(0)
                        selection(0)
                        with act.Fori(0, NT - 1) as i:
                            one_tile(i, False)
                        one_tile(NT - 1, True)
                        hi_done.n += (NT - 2) * UT
            act.wait_ge(layer_end.handle, DEPTH + 1)
            for t in range(TILES):
                nc.scalar.activation(xn[:, t, :], x[:, t, :], ACT.Square, accum_out=st[:, t:t + 1])\
                    .then_inc(fin_sq_act, 1)

        @block.tensor
        def _(pe):
            pe.wait_ge(const_in, 16 * NCONST)
            nc.tensor.transpose(T[:, 0, 0:P], ident[:, :], ident[:, :]).then_inc(unit_pe.handle, CONV)
            nc.tensor.transpose(T[:, 0, 2 * P:3 * P], ident[:, :], ident[:, :]).then_inc(q_st.handle, 1)
            pe.wait_ge(start_dve, 1)
            pe.wait_ge(cond_dve, 2)
            with pe.Fori(0, DEPTH) as l:
                passed = {}

                def need(s, i):
                    if i > passed.get(s.name, -1):
                        passed[s.name] = i
                        pe.wait_ge(s.handle, s.value(l, i))

                read = {b: None for b in ("S0", "S1", "T0", "T1", "O")}

                def free(*banks):
                    last = {}
                    for b in banks:
                        if read[b] is not None:
                            sgl, i = read[b]
                            last[sgl.name] = (sgl, max(i, last.get(sgl.name, (sgl, i))[1]))
                    for sgl, i in last.values():
                        need(sgl, i)

                def three(dst, st_hi, st_lo, mv_hi, mv_lo, start, stop):
                    nc.tensor.matmul(dst, st_hi, mv_hi, start=start, stop=False)
                    nc.tensor.matmul(dst, st_hi, mv_lo, start=False, stop=False)
                    return nc.tensor.matmul(dst, st_lo, mv_hi, start=False, stop=stop)

                pe.wait_ge(e_y.handle, l * (6 * NT) + 6)
                for s in SCHEDULE:
                    if s[0] == "mod":
                        j = s[1]
                        p = MODPOS[j]
                        w = w_in[p % RAW]
                        pe.wait_ge(w.handle, w.value(l, p // RAW))
                        bank = T[:, 0, :] if j >= 40 else O[:, :]
                        free("T0" if j >= 40 else "O")
                        for k in range(KD):
                            r0, c0 = 32 * (j % 4), 256 + P * (j % KD // 4)
                            mm = nc.tensor.matmul(bank[r0:r0 + 32, c0:c0 + P], cond[:, k, :],
                                                  raw[:, p % RAW, k * P:(k + 1) * P],
                                                  start=(k == 0), stop=(k == KD - 1))
                        mod_pe.of(mm)
                    elif s[0] == "modv":
                        read["T0" if s[1] == 5 else "O"] = (mod_act, s[1])
                    elif s[0] == "modt":
                        need(mod_act, s[1])
                        free("T1")
                        for b in range(2):
                            mm = nc.tensor.transpose(T[:, 1, b * P:(b + 1) * P], mrow[:, b * P:(b + 1) * P], ident[:, :])
                        modt_pe.of(mm)
                        read["T1"] = (mod_dve, s[1])
                    elif s[0] == "norm":
                        w = s[1]
                        def back(c):
                            need(hf_dve, KD + c)
                            free(f"S{c % 2}")
                            for t in range(TILES):
                                mm = nc.tensor.transpose(S[:, c % 2, t * P:(t + 1) * P],
                                                         probT[:, c % 2, 0, t * P:(t + 1) * P], ident[:, :])
                            nb_pe.of(mm)
                            read[f"S{c % 2}"] = (nbl_dve, c)

                        need(xn_dve, 2 * w + 1)
                        need(xn_act, w)
                        for c in range(KD):
                            free(f"T{c % 2}")
                            for t in range(TILES):
                                mm = nc.tensor.transpose(T[:, c % 2, t * P:(t + 1) * P], xn[:, t, c * P:(c + 1) * P],
                                                         ident[:, :])
                            nt_pe.of(mm)
                            read[f"T{c % 2}"] = (hf_dve, KD * w + c)
                            if w and c:
                                back(c - 1)
                        if w:
                            back(KD - 1)
                    elif s[0] == "gemm":
                        g = s[1]
                        c, i, n = GEMM[g]
                        kind, arg, width, _ = CHUNKS[c]
                        ku = 1024 // width
                        need(lo_done, g)
                        if i == 0 and kind == "branch":
                            need(*((tl_dve, 3), (ol_dve, 11), (ol_dve, 23), (tl_dve, 7))[arg[0]])
                        for t in range(TILES):
                            if i == 0 and c > 0:
                                need(*evacuated(c - 1, t))
                            for k in range(ku):
                                kk = i * ku + k
                                if kind == "branch":
                                    hi_, lo_ = bhi[arg[0] % 3], blo[arg[0] % 3]
                                else:
                                    hi_, lo_ = hhi, hlo
                                if kind == "wout" and arg == 0 and t == 0:
                                    need(ml_dve, kk)
                                if c == 0 and t == 0:
                                    need((hl_dve, hl_pool)[kk % 2], kk // 2)
                                mm = three(G[:, t, 0:width], hi_[:, kk, t * P:(t + 1) * P], lo_[:, kk, t * P:(t + 1) * P],
                                           whi[:, g % CONV, k * width:(k + 1) * width],
                                           wlo[:, g % CONV, k * width:(k + 1) * width],
                                           i == 0 and k == 0, i == n - 1 and k == ku - 1)
                            if i == n - 1:
                                tile_pe.of(mm)
                        if i < n - 1:
                            unit_pe.of(mm)
                    elif s == ("mgate",) or s == ("route",):
                        i, lo, w = (0, 0, 16) if s == ("mgate",) else (1, 16, 20)
                        need(sml_dve, 0)
                        free("O")
                        for k in range(KD):
                            if w == 20:
                                need((hl_dve, hl_pool)[k % 2], KD // 2 + k // 2)
                            mm = three(O[0:w, 0:384], smhi[:, k, lo:lo + w], smlo[:, k, lo:lo + w], hhi[:, k, :],
                                       hlo[:, k, :], k == 0, k == KD - 1)
                        sp_pe.of(mm)
                        need(sp_act, i)
                        for t in range(TILES):
                            mm = nc.tensor.matmul(O[:, t * w:(t + 1) * w], prob[0:w, 0, 0, t * P:(t + 1) * P],
                                                  ident[0:w, 0:w], start=True, stop=True)
                        if w == 16:
                            mg_pe.of(mm)
                            read["O"] = (mg_dve, 0)
                        else:
                            rt_pe.of(mm)
                            need(rg_dve, 0)
                            for o, m in ((128, tri[:, 0, :]), (140, ones[:, :])):
                                mm = nc.tensor.matmul(O[:, o:o + 12].rearrange("p (t n) -> p t n", t=TILES), m,
                                                      rw[:, :, 16:20], start=True, stop=True)
                            rc_pe.of(mm)
                    elif s == ("mcum",):
                        need(lf_dve, 0)
                        free("O")
                        for t in range(TILES):
                            o = 64 + 16 * t
                            nc.tensor.matmul(O[:, o:o + 4], tri[:, 0, :], lf[:, t, 0:4], start=True, stop=True)
                            nc.tensor.matmul(O[:, o + 4:o + 8], tri[:, 1, :], lf[:, t, 4:8], start=True, stop=True)
                            mm = nc.tensor.matmul(O[:, o + 8:o + 16], ones[:, :], lf[:, t, :], start=True, stop=True)
                        mb_pe.of(mm)
                        read["O"] = (cc_dve, 0)
                    elif s[0] == "tp":
                        ty, w, j = s[1:]
                        i = TP_NO[ty, w, j]
                        if ty in "AB":
                            need(*evacuated(CHUNK_NO[ty + w], 2))
                            src = slot[ty + w]
                        else:
                            if ty == "C":
                                need(rope_dve, 4)
                                if w == "q":
                                    need(*evacuated(CHUNK_NO["Cq"], 2))
                            else:
                                need(rope_dve, 8)
                                need(*evacuated(CHUNK_NO["D" + w], 2))
                            src = slot[ty + w] if (ty, w) != ("C", "k") else None
                        free(f"T{i % 2}")
                        for t in range(TILES):
                            blk = src[:, t, j * P:(j + 1) * P] if src is not None else \
                                kdup[:, t, j, :, :].rearrange("p a n -> p (a n)")
                            mm = nc.tensor.transpose(T[:, i % 2, t * P:(t + 1) * P], blk, ident[:, :])
                        tp_pe.of(mm)
                        read[f"T{i % 2}"] = (tp_act, i)
                    elif s[0] == "m1":
                        m = s[1]
                        d, t = MU[m]
                        need(diag_pool, m)
                        need(tp_act, 7)
                        free("S0", "S1")
                        nc.tensor.matmul(S[:, 0, :], ones[:, :], bias[:, :, :].rearrange("p a n -> p (a n)")[:, 0:512],
                                         start=True, stop=True)
                        for h in range(4):
                            mm = nc.tensor.matmul(S[:, 1, h * P:(h + 1) * P], qT[:, h, t * P:(t + 1) * P],
                                                  kT[:, h, t * P:(t + 1) * P], start=True, stop=True)
                        m1_pe.of(mm)
                        read["S0"], read["S1"] = (mmax_dve, m), (ms_dve, m)
                    elif s[0] == "m2":
                        m = s[1]
                        d, t = MU[m]
                        W = prob[:, m % 2].rearrange("p a n -> p (a n)")
                        need(ms_dve, m)
                        free("S0", "T0", "O")
                        if t < 2:
                            if m < 2:
                                need(ct_in, 0)
                                need(par_in, 2)
                            else:
                                need(ct_dve, MU.index((d, 1 - t)))
                            nv = pcol[:, PC_N:PC_N + 8]
                            for h in range(4):
                                q = qT[:, h, t * P:(t + 1) * P]
                                nc.tensor.matmul(S[:, 0, h * P:(h + 1) * P], q, cT[:, 4 * d + h, :], start=True, stop=True)
                                nc.tensor.matmul(O[:, 4 + h:5 + h], q, nv[:, 4 * d + h:4 * d + h + 1],
                                                 start=True, stop=True)
                        for h in range(4):
                            mm = nc.tensor.transpose(T[:, 0, h * P:(h + 1) * P], W[:, h * P:(h + 1) * P], ident[:, :])
                        m2_pe.of(mm)
                        read["T0"] = (sT_act, m)
                    elif s[0] == "m3":
                        m = s[1]
                        d, t = MU[m]
                        sT = probT[:, m % 2].rearrange("p a n -> p (a n)")
                        need(sT_act, m)
                        need(*evacuated(CHUNK_NO["Av"], t))
                        free("T0", "T1")
                        if m in MUPD:
                            need(kw_pool, m)
                        for h in range(4):
                            v = slot["Av"][:, t, h * P:(h + 1) * P]
                            st_ = sT[:, h * P:(h + 1) * P]
                            nc.tensor.matmul(T[:, 1, h * P:(h + 1) * P], st_, v, start=True, stop=True)
                            mm = nc.tensor.matmul(O[:, h:h + 1], st_, ones[:, 0:1], start=True, stop=True)
                            if m in MUPD:
                                kw = vc[:, h * P:(h + 1) * P]
                                if t < 2:
                                    nc.tensor.matmul(T[:, 0, h * P:(h + 1) * P], kw, v, start=True, stop=True)
                                    mm = nc.tensor.matmul(O[:, 8 + h:9 + h], kw, ones[:, 0:1], start=True, stop=True)
                                else:
                                    mm = nc.tensor.matmul(T[:, 0, h * P:(h + 1) * P], v, kw, start=True, stop=True)
                        if m in MUPD and t == 2:
                            mm = nc.tensor.matmul(S[0:1, 0, :], ones[:, 0:1], vc[:, :], start=True, stop=True)
                        m3_pe.of(mm)
                        read["T1"] = read["O"] = read["S0"] = (mh_dve, m)
                        if m in MUPD:
                            read["T0"] = (ct_dve, m) if t < 2 else (mc_act, d)
                            if t == 2:
                                read["S0"] = (mc_act, d)
                            else:
                                read["O"] = (ct_dve, m)
                    elif s[0] == "sc":
                        u = s[1]
                        ty, t, j = AU[u]
                        kj = j // 2 if ty == "C" else j
                        i = "BCD".index(ty)
                        need(tp_act, max(TP_NO[ty, "q", j], TP_NO[ty, "k", kj]))
                        if u % 12 == 0:
                            need(keys_in, i)
                        free("S0", "S1")
                        for m in range(2):
                            r = slice(64 * m, 64 * m + 64)
                            q = qT[r, j, t * P:(t + 1) * P]
                            if t < 2:
                                nc.tensor.matmul(S[:, m, 0:256], q, kT[r, kj, 0:256], start=True, stop=True)
                                mm = nc.tensor.matmul(S[:, m, 256:384], q, kT[r, kj, 384:512], start=True, stop=True)
                            else:
                                mm = nc.tensor.matmul(S[:, m, 0:128], q, kT[r, kj, 256:384], start=True, stop=True)
                        sc_pe.of(mm)
                        read["S0"] = read["S1"] = (sa_dve, BIASED.index(u)) if u in BIASED else (ex_act, u)
                    elif s[0] == "pt":
                        u = s[1]
                        ty, t, j = AU[u]
                        need(pn_dve, u)
                        maps = 1 if ty == "D" else 2
                        free(*("T0", "T1")[0:maps])
                        for m in range(maps):
                            for b in range(3 if t < 2 else 1):
                                mm = nc.tensor.transpose(T[:, m, b * P:(b + 1) * P],
                                                         prob[:, u % 2, m, b * P:(b + 1) * P], ident[:, :])
                        pt_pe.of(mm)
                        read["T0"] = (pa_act, u)
                        if maps == 2:
                            read["T1"] = (pb_dve, u)
                    elif s[0] == "pv":
                        u = s[1]
                        ty, t, j = AU[u]
                        need(pa_act, u)
                        if ty != "D":
                            need(pb_dve, u)
                        if u % 12 == 0:
                            need(vals_in, "BCD".index(ty))
                        free("O")
                        blocks = [0, 1, None] if t < 2 else [2]

                        def values(b, lo, n):
                            if b is None:
                                return vc[:, lo:lo + n]
                            return {"B": slot["Bv"], "C": Ckv[:, :, 128:256], "D": slot["Dv"]}[ty][:, b, lo:lo + n]

                        for m in range(1 if ty == "D" else 2):
                            for i, b in enumerate(blocks):
                                pr = probT[:, u % 2, m, i * P:(i + 1) * P]
                                fl = dict(start=(i == 0), stop=(i == len(blocks) - 1))
                                if ty == "D":
                                    mm = nc.tensor.matmul(O[:, 0:P], pr, values(b, j * P, P), **fl)
                                else:
                                    lo = 64 * (2 * j + m if ty == "B" else j // 2)
                                    mm = nc.tensor.matmul(O[64 * m:64 * m + 64, 0:P], values(b, lo, 64), pr, **fl)
                        pv_pe.of(mm)
                        read["O"] = (yd_act, u - 24) if ty == "D" else (ol_dve, u)
                    elif s[0] == "to":
                        i, j = s[1:]
                        need(hn_dve, 3 * i + 2)
                        free(f"T{j % 2}")
                        for t in range(TILES):
                            mm = nc.tensor.transpose(T[:, j % 2, t * P:(t + 1) * P],
                                                     slot["AD"[i] + "q"][:, t, j * P:(j + 1) * P], ident[:, :])
                        to_pe.of(mm)
                        read[f"T{j % 2}"] = (tl_dve, 4 * i + j)
                    elif s[0] == "gt":
                        need(mod_dve, 2 if s[1] == 0 else 5)
                        free("T1")
                        gt_pe.of(nc.tensor.transpose(T[0:16, 1, 0:P], modc[:, 2 + 3 * s[1], :, :]
                                                     .rearrange("p j c -> p (j c)"), ident[:, :]))
                        read["T1"] = (gr_act, s[1])
                    elif s[0] == "mt":
                        c = s[1]
                        b = CHUNK_NO["branch", (3, c // 4)]
                        need(ev_pool, pooled(b, 2))
                        free(f"T{c % 2}")
                        for t in range(TILES):
                            mm = nc.tensor.transpose(T[:, c % 2, t * P:(t + 1) * P],
                                                     merged[c // 4][:, t, (c % 4) * P:(c % 4 + 1) * P], ident[:, :])
                        mt_pe.of(mm)
                        read[f"T{c % 2}"] = (ml_dve, c)
                    elif s == ("experts",):
                        def converted(i, n):
                            pe.wait_ge(lo_done.handle, lo_done.value(l, NG + n) + i * UT)
                            pe.wait_ge(*e_lo.in_tile(l, i, UT, n))

                        def gate_up(i, e, u):
                            n = UNITS.index((e, u))
                            converted(i, n)
                            for k in range(2):
                                kk = 2 * u + k
                                mm = three(G[:, e % 2, :], hhi[:, kk, 0:P], hlo[:, kk, 0:P],
                                           whi[:, n % CONV, k * 512:(k + 1) * 512], wlo[:, n % CONV, k * 512:(k + 1) * 512],
                                           kk == 0, kk == KD - 1)
                            e_unit.of(mm)

                        def down(i, e):
                            for f in range(2):
                                n = UNITS.index((e, 4 + f))
                                converted(i, n)
                                for hf in range(2):
                                    mm = three(S[:, hf, :], ehi[:, f, 0:P], elo[:, f, 0:P],
                                               whi[:, n % CONV, hf * 512:(hf + 1) * 512],
                                               wlo[:, n % CONV, hf * 512:(hf + 1) * 512],
                                               e == 0 and f == 0, e == GRP - 1 and f == 1)
                                e_unit.of(mm)

                        def turn_hid(i, e):
                            pe.wait_ge(*e_hid.in_tile(l, i, GRP, e))
                            pe.wait_ge(*e_hl.in_tile(l, i, GRP, e - 1))
                            for f in range(2):
                                mm = nc.tensor.transpose(T[:, 0, f * P:(f + 1) * P], hid[:, e % 2, f * P:(f + 1) * P],
                                                         ident[:, :])
                            e_pt.of(mm)

                        def gather(i):
                            pe.wait_ge(*q_sel.in_tile(l, i, 1, 0))
                            for hf in range(2):
                                for t in range(TILES):
                                    for part, h in enumerate((hth, htl)):
                                        mm = nc.tensor.matmul((T[:, 1, :], G[:, 2, :])[hf], sel[:, t, :],
                                                              h[:, t, hf * 512:(hf + 1) * 512],
                                                              start=(t == 0 and part == 0), stop=(t == TILES - 1 and part == 1))
                                q_g.of(mm)

                        def turn(i):
                            for hf in range(2):
                                pe.wait_ge(*q_hg.in_tile(l, i, 2, 1))
                                for c in range(4):
                                    mm = nc.tensor.transpose((T[:, 1, :], G[:, 2, :])[hf][:, c * P:(c + 1) * P],
                                                             hg[:, hf, c * P:(c + 1) * P], ident[:, :])
                                q_t.of(mm)

                        def selection(i):
                            for t in range(TILES):
                                nc.tensor.transpose(O[:, t * P:(t + 1) * P], sel[:, t, :].bitcast(F32), ident[:, :])
                            for t in range(TILES):
                                mm = nc.tensor.matmul(O[:, TILES * P:TILES * P + GRP], sel[:, t, :].bitcast(F32),
                                                      rw[:, t, 20:24], start=(t == 0), stop=(t == TILES - 1))
                            q_st.of(mm)

                        def first_units(i):
                            pe.wait_ge(*q_lo.in_tile(l, i, 2, 1))
                            pe.wait_ge(*e_hid.in_tile(l, i, GRP, -2))
                            gate_up(i, 0, 0)
                            gate_up(i, 0, 1)

                        def one_tile(i, last):
                            gate_up(i, 0, 2)
                            gate_up(i, 0, 3)
                            for e in range(GRP):
                                if e < GRP - 1:
                                    pe.wait_ge(*e_hid.in_tile(l, i, GRP, e - 1))
                                    if e == 0:
                                        pe.wait_ge(*e_y.in_tile(l, i, 6, -1))
                                    gate_up(i, e + 1, 0)
                                    gate_up(i, e + 1, 1)
                                elif not last:
                                    gather(i + 1)
                                turn_hid(i, e)
                                if e < GRP - 1:
                                    gate_up(i, e + 1, 2)
                                    gate_up(i, e + 1, 3)
                                pe.wait_ge(*e_hl.in_tile(l, i, GRP, e))
                                if e == 0:
                                    pe.wait_ge(*q_yl.in_tile(l, i, 2, -1))
                                down(i, e)
                            if not last:
                                turn(i + 1)
                                first_units(i + 1)
                            pe.wait_ge(*q_sa.in_tile(l, i, 1, 0))
                            for q in range(6):
                                t, hf = divmod(q, 2)
                                pe.wait_ge(*q_yl.in_tile(l, i, 2, hf))
                                pe.wait_ge(*e_y.in_tile(l, i, 6, q - 3))
                                bank = (O[:, :], T[:, 0, :], G[:, 1, :])[q % 3]
                                nc.tensor.matmul(bank, selT[:, t * P:(t + 1) * P], yh[:, hf, :], start=True, stop=False)
                                q_s.of(nc.tensor.matmul(bank, selT[:, t * P:(t + 1) * P], yl[:, hf, :],
                                                        start=False, stop=True))
                            if not last:
                                pe.wait_ge(*e_y.in_tile(l, i, 6, 5))
                                selection(i + 1)

                        free("T0", "T1", "S0", "S1", "O")
                        need(*evacuated(CHUNK_NO["wout", 1], 2))
                        need(nbl_dve, KD - 1)
                        gather(0)
                        turn(0)
                        selection(0)
                        first_units(0)
                        with pe.Fori(0, NT - 1) as i:
                            one_tile(i, False)
                        one_tile(NT - 1, True)

        @block.vector
        def _(dve):
            dve.wait_ge(const_in, 16 * NCONST)
            dve.wait_ge(cond_act, 1)
            nc.vector.scalar_tensor_tensor(cond_t, cond_t, 1.0, cond[:, :, :], ALU.add, ALU.mult)\
                .then_inc(cond_dve, 1)
            dve.wait_ge(cond_dve, 1)
            nc.vector.tensor_scalar(cond[:, :, :], cond_t, 0.5, None, ALU.mult).then_inc(cond_dve, 1)
            nc.vector.memset(dummy[:, 2:3], 0.0).then_inc(layer_end.handle, 1)
            nc.vector.memset(dummy[:, 4:5], 0.0).then_inc(e_hid.handle, 2)
            nc.vector.memset(dummy[:, 5:6], 0.0).then_inc(e_hl.handle, 1)
            nc.vector.memset(dummy[:, 6:7], 0.0).then_inc(e_y.handle, 6)
            nc.vector.memset(dummy[:, 7:8], 0.0).then_inc(q_yl.handle, 2)
            dve.wait_ge(start_dve, 8)
            with dve.Fori(0, DEPTH) as l:
                chain = [0]

                def need(s, i):
                    dve.wait_ge(s.handle, s.value(l, i))

                def own(*instructions):
                    for ins in instructions:
                        dve_ord.of(ins)
                        chain[0] += 1
                    dve.wait_ge(*dve_ord.at(l, chain[0] - 1))

                V = nc.vector

                def tt(o, i0, i1, op):
                    return V.tensor_tensor(o, i0, i1, op)

                def heads(ap):
                    return ap.rearrange("p (h n) -> p h n", h=4)

                def wide(col4):
                    return col4.unsqueeze(2).to_broadcast([P, 4, P])

                for s in SCHEDULE:
                    if s == ("prepare",):
                        dve.wait_ge(*smh_act.at(l, 0))
                        sml_dve.of(tt(smlo[:, :, :], small[:, :, :], smhi[:, :, :].bitcast(F32), ALU.subtract))
                        lq = row("lq").rearrange("p (a b n) -> p a b n", a=2, b=2)
                        own(tt(rwf[:, 0:128].rearrange("p (a n) -> p a n", a=2), lq[:, :, 0, :], lq[:, :, 1, :], ALU.mult))
                        lam_dve.of(V.tensor_reduce(lam[:, 0:2], rwf[:, 0:128].rearrange("p (a n) -> p a n", a=2), AX, ALU.add))
                        dve.wait_ge(*lam_act.at(l, 0))
                        own(tt(lam[:, 4:5], lam[:, 3:4], lam[:, 2:3], ALU.subtract))
                        own(tt(lam[:, 5:6], lam[:, 4:5], row("lam", 0, 1), ALU.subtract))
                        own(V.tensor_copy(mst[:, 0:8], row("m0")))
                    elif s[0] == "modt":
                        g = s[1]
                        if g == 0:
                            dve.wait_ge(*par_in.at(l, 2))
                        dve.wait_ge(*modt_pe.at(l, g))
                        b = pcol[:, PC_BMOD + KD * g:PC_BMOD + KD * (g + 1)]
                        mod_dve.of(tt(modc[:, g, :, :], T[:, 1, 0:256].rearrange("p (j c) -> p j c", c=32)[:, :, 0:2],
                                      b.unsqueeze(2).to_broadcast([P, KD, 2]), ALU.add))
                        if g in (1, 4):
                            dve.wait_ge(*mod_dve.at(l, g))
                            o = PC_NMIX if g == 1 else PC_NFFN
                            own(V.tensor_scalar(acol[:, :, :], modc[:, g, :, :], 1.0, None, ALU.add))
                            own(tt(acol[:, :, :], acol[:, :, :],
                                   pcol[:, o:o + KD].unsqueeze(2).to_broadcast([P, KD, 2]), ALU.mult))
                    elif s[0] == "norm":
                        w = s[1]
                        dve.wait_ge(*rstd_pool.at(l, w))
                        for t in (0, 2):
                            xn_dve.of(V.tensor_scalar(xn[:, t, :], x[:, t, :], st[:, t:t + 1], None, ALU.mult))

                        def back(c):
                            dve.wait_ge(*nbh_act.at(l, c))
                            part = slice(c * P, (c + 1) * P)
                            nbl_dve.of(tt(htl[:, :, part], S[:, c % 2, 0:384].rearrange("p (t n) -> p t n", t=TILES),
                                          hth[:, :, part].bitcast(F32), ALU.subtract))

                        def low(c):
                            if c % 2 == 0:
                                dve.wait_ge(*hh_act.at(l, KD * w + c))
                                hl_dve.of(tt(hlo[:, c, :], probT[:, c % 2, 0, :], hhi[:, c, :].bitcast(F32), ALU.subtract))

                        for c in range(KD):
                            dve.wait_ge(*nt_pe.at(l, KD * w + c))
                            if c > 1:
                                need((hl_dve, hl_pool)[c % 2], KD // 2 * w + (c - 2) // 2)
                                if w:
                                    dve.wait_ge(*nb_pe.at(l, c - 2))
                            for cn, (lo, hi) in enumerate(((0, 256), (256, 384))):
                                ins = V.tensor_scalar(probT[:, c % 2, 0, lo:hi], T[:, c % 2, lo:hi],
                                                      acol[:, c, cn:cn + 1], modc[:, 3 * w, c, cn:cn + 1],
                                                      ALU.mult, ALU.add)
                            hf_dve.of(ins)
                            if c:
                                low(c - 1)
                            if w and c > 1:
                                back(c - 2)
                        low(KD - 1)
                        if w:
                            back(KD - 2)
                            back(KD - 1)
                    elif s[0] == "gemm":
                        g = s[1]
                        c, i, n = GEMM[g]
                        kind, arg = CHUNKS[c][:2]
                        if i == n - 1 and kind == "branch":
                            for t in range(TILES):
                                dve.wait_ge(*tile_pe.at(l, TILES * c + t))
                                need(*evacuated(c - 1, t))
                                dst = merged[arg[1]][:, t, :] if arg[0] == 0 else sig[:, t, :]
                                if arg == (0, 0):
                                    dve.wait_ge(*to_pe.at(l, 3))
                                if arg == (0, 1):
                                    dve.wait_ge(*pv_pe.at(l, 11))
                                    need(kv_out["B"], 1)
                                ev_dve.of(V.scalar_tensor_tensor(dst, sig[:, t, :], 1.0, G[:, t, :], ALU.add, ALU.mult))
                        if i == n - 1 and kind == "wout":
                            dve.wait_ge(*g_in.at(l, 1))
                            for t in range(TILES):
                                dve.wait_ge(*tile_pe.at(l, TILES * c + t))
                                if arg == 0:
                                    dve.wait_ge(*x_in.at(l, 0))
                                    dve.wait_ge(*ev_pool.at(l, pooled(CHUNK_NO["branch", (3, 1)], t)))
                                else:
                                    dve.wait_ge(*ev_pool.at(l, pooled(c - 1, t)))
                                ev_dve.of(tt(sig[:, t, :], G[:, t, :], gbc[:, t // 2, arg * 512:(arg + 1) * 512], ALU.mult))
                    elif s == ("mgate",):
                        dve.wait_ge(*mg_pe.at(l, 0))
                        g3 = O[:, 0:48].rearrange("p (t n) -> p t n", t=TILES)
                        own(tt(gi[:, :, :], g3[:, :, 0:8], row("ib").unsqueeze(1).to_broadcast([P, TILES, 8]), ALU.add),
                            tt(gf[:, :, :], g3[:, :, 8:16], row("fb").unsqueeze(1).to_broadcast([P, TILES, 8]), ALU.add))
                        mg_dve.of(V.scalar_tensor_tensor(ga[:, :, :], gf[:, :, :], -1.0, gf[:, :, :], ALU.mult, ALU.min))
                        dve.wait_ge(*ln_act.at(l, 0))
                        lf_dve.of(V.scalar_tensor_tensor(lf[:, :, :], gf[:, :, :], 0.0, ga[:, :, :], ALU.min, ALU.subtract))
                    elif s == ("mcum",):
                        dve.wait_ge(*mb_pe.at(l, 0))
                        own(V.tensor_copy(bt[:, :, :], O[:, 64:112].rearrange("p (t n) -> p t n", t=TILES)))
                        cc_dve.of(tt(cc[:, :, :], gi[:, :, :], bt[:, :, 0:8], ALU.subtract))
                    elif s[0] == "rope":
                        ty, w, t = s[1:]
                        if s[1:] != ROPE[0]:
                            dve.wait_ge(*rope_dve.at(l, rope_dve.n - 1))
                        else:
                            dve.wait_ge(*m_out.at(l, 5))
                        ch = "Ckv" if (ty, w) == ("C", "k") else ty + w
                        need(*evacuated(CHUNK_NO[ch], t))
                        nh = 2 if ch == "Ckv" else 8
                        src = slot[ch][:, t, 0:64 * nh]
                        if t == 2:
                            for cp in range(2):
                                ins = V.tensor_copy(kdup[:, t, :, cp, :], src.rearrange("p (h n) -> p h n", h=2))
                            rope_dve.of(ins)
                            continue
                        r1 = sig[:, 0, 0:64 * nh]
                        r2 = sig[:, 1, 0:64 * nh]
                        pr = "p (h f c n) -> p h f c n"
                        s5 = src.rearrange(pr, h=nh, f=2, c=2)
                        u5 = r2.rearrange(pr, h=nh, f=2, c=2)
                        sn = rope_t[:, t, 64:96].rearrange("p (f n) -> p f n", f=2).unsqueeze(1).to_broadcast([P, nh, 2, 16])
                        own(tt(r1.rearrange("p (h n) -> p h n", h=nh), src.rearrange("p (h n) -> p h n", h=nh),
                               rope_t[:, t, 0:64].unsqueeze(1).to_broadcast([P, nh, 64]), ALU.mult),
                            tt(u5[:, :, :, 0, :], s5[:, :, :, 1, :], sn, ALU.mult),
                            tt(u5[:, :, :, 1, :], s5[:, :, :, 0, :], sn, ALU.mult))
                        r15 = r1.rearrange(pr, h=nh, f=2, c=2)
                        for cp in range(2 if ch == "Ckv" else 1):
                            if ch == "Ckv":
                                dst = kdup[:, t, :, cp, :].rearrange("p h (f c n) -> p h f c n", f=2, c=2)
                            else:
                                dst = s5
                            a1 = tt(dst[:, :, :, 0, :], r15[:, :, :, 0, :], u5[:, :, :, 0, :], ALU.subtract)
                            dve_ord.of(a1)
                            chain[0] += 1
                            a2 = tt(dst[:, :, :, 1, :], r15[:, :, :, 1, :], u5[:, :, :, 1, :], ALU.add)
                            if cp == 1:
                                rope_dve.of(a2)
                            elif ch != "Ckv":
                                rope_dve.of(a2)
                    elif s[0] == "m1":
                        m = s[1]
                        d, t = MU[m]
                        q = ms[:, m % 2]
                        W = prob[:, m % 2].rearrange("p a n -> p (a n)")[:, 0:512]
                        m0 = mst[:, 4 * d:4 * d + 4] if t < 2 else zst[:, :]
                        b = bt[:, t, 4 * d:4 * d + 4]
                        tot = bt[:, t, 8 + 4 * d:12 + 4 * d]
                        c4 = cc[:, t, 4 * d:4 * d + 4]
                        dve.wait_ge(*m1_pe.at(l, m))
                        own(tt(heads(W), heads(S[:, 0, :]), cmask[:, d, :].unsqueeze(1).to_broadcast([P, 4, P]), ALU.add),
                            V.tensor_reduce(q[:, 0:4], heads(S[:, 0, :]), AX, ALU.max))
                        own(V.tensor_reduce(q[:, 4:8], heads(W), AX, ALU.max))
                        own(tt(q[:, 4:8], q[:, 4:8], m0, ALU.max), tt(q[:, 0:4], q[:, 0:4], m0, ALU.max))
                        own(tt(q[:, 32:36], m0, q[:, 4:8], ALU.subtract),
                            V.scalar_tensor_tensor(q[:, 36:40], b, -1.0, q[:, 4:8], ALU.mult, ALU.subtract),
                            tt(q[:, 40:44], c4, q[:, 0:4], ALU.subtract),
                            tt(q[:, 44:48], m0, q[:, 0:4], ALU.subtract))
                        if m in MUPD:
                            mo = mst[:, 4 * d:4 * d + 4] if t < 2 else mst[:, 8 + 4 * d:12 + 4 * d]
                            own(tt(mo, tot, q[:, 0:4], ALU.add))
                        mmax_dve.of(V.tensor_scalar(q[:, 8:12], q[:, 4:8], -1.0, None, ALU.mult))
                        dve.wait_ge(*mexp_act.at(l, m))
                        ms_dve.of(tt(W, S[:, 1, :], W, ALU.mult))
                    elif s[0] == "m3":
                        m = s[1]
                        d, t = MU[m]
                        q = ms[:, m % 2]
                        W = prob[:, m % 2].rearrange("p a n -> p (a n)")[:, 0:512]
                        ya = slot["Aq"][:, t, :]
                        dve.wait_ge(*m3_pe.at(l, m))
                        if t < 2:
                            own(tt(heads(W), heads(S[:, 0, :]), wide(q[:, 16:20]), ALU.mult),
                                tt(q[:, 48:52], O[:, 4:8], q[:, 16:20], ALU.mult))
                            own(tt(W, W, T[:, 1, :], ALU.add), tt(q[:, 48:52], q[:, 48:52], O[:, 0:4], ALU.add))
                            num = W
                        else:
                            own(V.tensor_copy(q[:, 48:52], O[:, 0:4]))
                            num = T[:, 1, :]
                        own(V.scalar_tensor_tensor(q[:, 48:52], q[:, 48:52], -1.0, q[:, 48:52], ALU.mult, ALU.max))
                        own(tt(q[:, 48:52], q[:, 48:52], q[:, 20:24], ALU.max))
                        own(V.reciprocal(q[:, 52:56], q[:, 48:52]))
                        if m in (0, 1, 2):
                            mh_dve.of(tt(heads(ya), heads(num), wide(q[:, 52:56]), ALU.mult))
                        else:
                            own(tt(heads(W), heads(num), wide(q[:, 52:56]), ALU.mult))
                            mh_dve.of(tt(ya, ya, W, ALU.add))
                        if m in MUPD and t < 2:
                            c4 = cT[:, 4 * d:4 * d + 4, :]
                            nv = pcol[:, PC_N + 4 * d:PC_N + 4 * d + 4]
                            own(tt(c4, c4, wide(q[:, 28:32]), ALU.mult), tt(nv, nv, q[:, 28:32], ALU.mult))
                            own(tt(nv, nv, O[:, 8:12], ALU.add))
                            ct_dve.of(tt(c4, c4, heads(T[:, 0, :]), ALU.add))
                    elif s[0] == "sc":
                        u = s[1]
                        ty, t, j = AU[u]
                        w = 384 if t < 2 else 128
                        q = am[:, u % 2]
                        dve.wait_ge(*sc_pe.at(l, u))
                        src = S[:, :, 0:w]
                        if u in BIASED:
                            b = BIASED.index(u)
                            dve.wait_ge(*bias_in.at(l, bias_index(b)))
                            src = prob[:, u % 2, :, :]
                            sa_dve.of(tt(src, S[:, :, 0:w], bias[:, :, :], ALU.add))
                            dve.wait_ge(*sa_dve.at(l, b))
                        own(V.tensor_reduce(q[:, 8:10], src, AX, ALU.max))
                        if ty == "C":
                            sk = row("sink", 2 * j, 2 * j + 2)
                            own(tt(q[:, 8:10], q[:, 8:10], sk, ALU.max))
                            own(V.tensor_scalar(q[:, 0:2], q[:, 8:10], -1.0, None, ALU.mult))
                            nm_dve.of(tt(q[:, 4:6], sk, q[:, 0:2], ALU.add))
                        else:
                            nm_dve.of(V.tensor_scalar(q[:, 0:2], q[:, 8:10], -1.0, None, ALU.mult))
                        dve.wait_ge(*ex_act.at(l, u))
                        if ty == "C":
                            own(tt(q[:, 2:4], q[:, 2:4], q[:, 6:8], ALU.add))
                        own(V.reciprocal(q[:, 10:12], q[:, 2:4]))
                        if ty == "D":
                            own(V.tensor_scalar(prob[:, u % 2, 0, 0:w], prob[:, u % 2, 0, 0:w], q[:, 10:11], None, ALU.mult),
                                V.tensor_scalar(q[:, 11:12], q[:, 11:12], lam[:, 5:6], None, ALU.mult))
                            pn_dve.of(V.scalar_tensor_tensor(prob[:, u % 2, 0, 0:w], prob[:, u % 2, 1, 0:w], q[:, 11:12],
                                                             prob[:, u % 2, 0, 0:w], ALU.mult, ALU.add))
                        else:
                            for m in range(2):
                                ins = V.tensor_scalar(prob[:, u % 2, m, 0:w], prob[:, u % 2, m, 0:w], q[:, 10 + m:11 + m],
                                                      None, ALU.mult)
                            pn_dve.of(ins)
                    elif s[0] == "pt" and AU[s[1]][0] != "D":
                        u = s[1]
                        w = 384 if AU[u][1] < 2 else 128
                        dve.wait_ge(*pt_pe.at(l, u))
                        pb_dve.of(V.tensor_copy(probT[:, u % 2, 1, 0:w], T[:, 1, 0:w]))
                    elif s[0] == "pv" and AU[s[1]][0] != "D":
                        u = s[1]
                        ty, t, j = AU[u]
                        n = TYPES.index(ty)
                        dve.wait_ge(*oh_act.at(l, u))
                        blk = (slice(None), j, slice(t * P, (t + 1) * P))
                        ol_dve.of(tt(blo[n][blk], O[:, 0:P], bhi[n][blk].bitcast(F32), ALU.subtract))
                    elif s[0] == "hn":
                        i = s[1]
                        y = slot["AD"[i] + "q"]
                        if i == 1:
                            dve.wait_ge(*yd_act.at(l, 11))
                        for t in range(TILES):
                            own(tt(prob[:, t % 2].rearrange("p a n -> p (a n)")[:, 0:512], y[:, t, :], y[:, t, :], ALU.mult))
                            hs_dve.of(V.tensor_reduce(st[:, 3 + 4 * t:7 + 4 * t],
                                                      heads(prob[:, t % 2].rearrange("p a n -> p (a n)")[:, 0:512]), AX,
                                                      ALU.add))
                    elif s[0] == "hr":
                        i = s[1]
                        y = slot["AD"[i] + "q"]
                        dve.wait_ge(*hr_pool.at(l, i))
                        if i == 0:
                            dve.wait_ge(*tanh_act.at(l, 0))
                        for t in range(TILES):
                            if i == 0:
                                o = slot["Ao"][:, t, :]
                                own(tt(heads(y[:, t, :]), heads(y[:, t, :]), wide(st[:, 3 + 4 * t:7 + 4 * t]), ALU.mult),
                                    V.scalar_tensor_tensor(o, o, 1.0, row("anorm"), ALU.add, ALU.mult))
                                hn_dve.of(tt(y[:, t, :], y[:, t, :], o, ALU.mult))
                            else:
                                own(tt(heads(y[:, t, :]), heads(y[:, t, :]), wide(st[:, 3 + 4 * t:7 + 4 * t]), ALU.mult))
                                hn_dve.of(tt(heads(y[:, t, :]), heads(y[:, t, :]),
                                             row("subln").unsqueeze(1).to_broadcast([P, 4, P]), ALU.mult))
                    elif s[0] == "to":
                        i, j = s[1:]
                        dve.wait_ge(*th_act.at(l, 4 * i + j))
                        tl_dve.of(tt(blo[0][:, j, :], T[:, j % 2, 0:384], bhi[0][:, j, :].bitcast(F32), ALU.subtract))
                    elif s[0] == "mt":
                        c = s[1]
                        dve.wait_ge(*mh_act.at(l, c))
                        ml_dve.of(V.scalar_tensor_tensor(hlo[:, c, :], T[:, c % 2, 0:384], 0.5, hhi[:, c, :].bitcast(F32),
                                                         ALU.mult, ALU.subtract))
                    elif s == ("route",):
                        route(dve, need, own, tt)
                    elif s == ("experts",):
                        def low(i, n):
                            dve.wait_ge(hi_done.handle, hi_done.value(l, NG + n) + i * UT)
                            e_lo.of(tt(wlo[:, n % CONV, POOL_COLS:], raw[:, n % RAW, POOL_COLS:],
                                       whi[:, n % CONV, POOL_COLS:].bitcast(F32), ALU.subtract))

                        def select(i):
                            dve.wait_ge(*q_st.in_tile(l, i, 1, -1))
                            for t in range(TILES):
                                ins = V.tensor_scalar(sel[:, t, :], order[:, 4 + NT:], rel[:, bass.ds(i, 1), t:t + 1]
                                                      .rearrange("p a n -> p (a n)"), None, ALU.is_equal)
                            q_sel.of(ins)

                        def turned(i):
                            for hf in range(2):
                                dve.wait_ge(*q_hi.in_tile(l, i, 2, hf))
                                c4 = slice(4 * hf, 4 * hf + 4)
                                q_lo.of(tt(hlo[:, c4, 0:P], (T[:, 1, :], G[:, 2, :])[hf].rearrange("p (c n) -> p c n", c=4),
                                           hhi[:, c4, 0:P].bitcast(F32), ALU.subtract))

                        def one_tile(i, last):
                            def hidden(e):
                                dve.wait_ge(*e_tanh.in_tile(l, i, GRP, e))
                                ga_, b = gact[:, e % 2, :], G[:, e % 2, :]
                                e_dve.of(V.scalar_tensor_tensor(ga_, ga_, 1.0, b[:, 0:DEXP], ALU.add, ALU.mult))
                                dve.wait_ge(*e_dve.in_tile(l, i, GRP, e))
                                if e == 0:
                                    dve.wait_ge(*q_sa.in_tile(l, i, 1, 0))
                                e_hid.of(V.scalar_tensor_tensor(hid[:, e % 2, :], ga_, gate[:, e:e + 1], b[:, DEXP:],
                                                                ALU.mult, ALU.mult))

                            def turned_hid(e):
                                dve.wait_ge(*e_hh.in_tile(l, i, GRP, e))
                                e_hl.of(tt(elo[:, :, 0:P], T[:, 0, 0:2 * P].rearrange("p (f n) -> p f n", f=2),
                                           ehi[:, :, 0:P].bitcast(F32), ALU.subtract))

                            for n in range(3, UT):
                                low(i, n)
                                if n in (6, 10, 16, 22):
                                    hidden((6, 10, 16, 22).index(n))
                                if n in (8, 14, 20, 23):
                                    turned_hid((8, 14, 20, 23).index(n))
                                if n == 10 and not last:
                                    select(i + 1)
                            if not last:
                                low(i, UT)
                                low(i, UT + 1)
                            for hf in range(2):
                                dve.wait_ge(*q_yh.in_tile(l, i, 2, hf))
                                q_yl.of(tt(yl[:, hf, :], S[:, hf, :], yh[:, hf, :].bitcast(F32), ALU.subtract))
                            if not last:
                                turned(i + 1)
                                low(i, UT + 2)
                            for q in range(6):
                                t, hf = divmod(q, 2)
                                dve.wait_ge(*q_s.in_tile(l, i, 6, q))
                                if q == 0:
                                    dve.wait_ge(*yz_pool.at(l, 0))
                                ya = yacc[:, t, hf * 512:(hf + 1) * 512]
                                e_y.of(tt(ya, ya, (O[:, :], T[:, 0, :], G[:, 1, :])[q % 3], ALU.add))

                        select(0)
                        for n in range(3):
                            low(0, n)
                        turned(0)
                        with dve.Fori(0, NT - 1) as i:
                            one_tile(i, False)
                        one_tile(NT - 1, True)
                        dve.wait_ge(e_y.handle, (l * NT + NT) * 6 + e_y.credit)
                    elif s == ("end",):
                        dve.wait_ge(*g_in.at(l, 3))
                        dve.wait_ge(*m_out.at(l, 5))
                        for t in range(TILES):
                            own(tt(yacc[:, t, :], yacc[:, t, :], gbc[:, t // 2, :], ALU.mult))
                            ins = tt(x[:, t, :], x[:, t, :], yacc[:, t, :], ALU.add)
                            if t < TILES - 1:
                                own(ins)
                        layer_end.of(ins)
            dve.wait_ge(fin_rstd_pool, 2)
            dve.wait_ge(fin_gain_in, 16)
            for t in range(TILES):
                nc.vector.scalar_tensor_tensor(xn[:, t, :], x[:, t, :], st[:, t:t + 1], yacc[:, 0, :], ALU.mult, ALU.mult)\
                    .then_inc(fin_y_dve, 1)

        return {k: v.n for k, v in signals.items()}


def _constants():
    i = np.arange(P)
    f = np.float32
    tri = np.stack([i[:, None] <= i[None, :], i[:, None] >= i[None, :]], 1).astype(f)
    cmask = np.stack([np.where(i[None, :] <= i[:, None], 0, NEG), np.where(i[None, :] >= i[:, None], 0, NEG)], 1).astype(f)
    nf = DH_B // 4
    inv = (10000.0 ** (-np.arange(nf, dtype=f) / f(nf))).astype(f)
    t = np.arange(T_LAT)
    ang = np.stack([(t // GRID_W).astype(f)[:, None] * inv, (t % GRID_W).astype(f)[:, None] * inv], 1)
    cos, sin = np.cos(ang), np.sin(ang)
    rope = np.concatenate([np.stack([cos, cos], 2).reshape(T_LAT, 64), sin.reshape(T_LAT, 32)], 1)
    rope = rope.reshape(2, P, 96).transpose(1, 0, 2).astype(f)
    k = np.arange(T_LAT)
    window = np.where(np.abs(k[None, :] - k[:, None]) <= 128, 0, NEG).reshape(2, P, T_LAT).astype(f)
    return {"ident": np.eye(P, dtype=f), "tri": tri, "cmask": cmask, "rope": rope, "swa_mask": window,
            "order": np.tile(np.concatenate([[4, 3, 2, 1], 128 * np.arange(NT), 1 + np.arange(P)]).astype(f), (P, 1))}


def _windows(rpb):
    L, H = rpb.shape[:2]
    rows = T_LAT // GRID_W
    out = np.full((L, H, rows, GRID_W, rows, GRID_W), NEG, np.float32)
    for r in range(rows):
        for c in range(GRID_W):
            lo = min(max(c - 8, 0), GRID_W - 16)
            out[:, :, r, c, :, lo:lo + 16] = rpb[:, :, 7 - r:7 - r + rows, lo - c + 15:lo - c + 31]
    return out.reshape(L, 4, 2, 2, P, T_LAT).transpose(0, 3, 1, 4, 2, 5).reshape(L * 8, P, 2, T_LAT)


def _stream(i):
    units = np.empty((DEPTH, NU, P, 1024), np.float32)
    o = {}
    at = 0
    for name, n in (("Aq", 512), ("Ak", 512), ("Av", 512), ("Ao", 512), ("gates", 16), ("Bq", 512), ("Bk", 512), ("Bv", 512),
                    ("Cq", 512), ("Ckv", 256), ("Dq", 512), ("Dk", 512), ("Dv", 512), ("gt", 4 * D)):
        o[name] = at
        at += n

    def put(dst, w, k, cols):
        n = cols.stop - cols.start
        for j, kk in enumerate(k):
            dst[:, :, j * n:(j + 1) * n] = w[:, kk * P:(kk + 1) * P, cols]

    for p, (what, g) in enumerate(STREAM):
        dst = units[:, p]
        if what == "mod":
            put(dst, i["w_mod"], range(KD), slice(g * P, (g + 1) * P))
            continue
        c, u, _ = GEMM[g]
        kind, arg, width, _ = CHUNKS[c]
        ku = 1024 // width
        k = range(u * ku, (u + 1) * ku)
        if kind == "proj":
            put(dst, i["w_in"], k, slice(o[arg], o[arg] + width))
        elif kind == "gate":
            lo = o["gt"] + arg[0] * D + arg[1] * 512
            put(dst, i["w_in"], k, slice(lo, lo + 512))
        elif kind == "branch":
            put(dst, i["w_branch"][:, arg[0]], k, slice(arg[1] * 512, (arg[1] + 1) * 512))
        else:
            put(dst, i["w_out"], k, slice(arg * 512, (arg + 1) * 512))
    for group in range(GRP):
        for n, (j, u) in enumerate(UNITS):
            e = group * GRP + j
            dst = units[:, len(STREAM) + group * UT + n]
            if u >= 4:
                dst[:] = i["w_exp_down"][:, e, (u - 4) * P:(u - 3) * P]
                continue
            for k in range(2):
                r = slice((2 * u + k) * P, (2 * u + k + 1) * P)
                dst[:, :, k * 512:k * 512 + 256] = i["w_exp_gate"][:, e, r]
                dst[:, :, k * 512 + 256:(k + 1) * 512] = i["w_exp_up"][:, e, r]
    return units.reshape(DEPTH * NU, P, 1024), o


def _layout(i):
    L = DEPTH
    stream, o = _stream(i)

    def cols(v):
        return v.reshape(L, -1, P).transpose(0, 2, 1)

    pcol = np.concatenate([cols(i["norm_mix"]), cols(i["norm_ffn"]), cols(i["b_mod"]),
                           cols(i["state_mlstm_n"].reshape(L, 2 * H_A * P))], 2)
    lam_init = np.array([0.8 - 0.6 * np.exp(-0.3 * l) for l in range(L)])
    lam = np.stack([lam_init, 1.0 - lam_init], 1).astype(np.float32)
    prow = np.concatenate([i["mlstm_i_bias"].reshape(L, 8), i["mlstm_f_bias"].reshape(L, 8), i["swa_sink"],
                           i["diff_lq1"], i["diff_lk1"], i["diff_lq2"], i["diff_lk2"], lam,
                           i["mlstm_norm"], i["diff_subln"], i["state_mlstm_m"].reshape(L, 8)], 1)
    w = i["w_in"][:, :, o["gates"]:o["gates"] + 16]
    small = np.concatenate([w, i["router_group"], i["router_expert"]], 2).reshape(L, KD, P, SMALL).transpose(0, 2, 1, 3)

    def keys(c, dup=False):
        k = c[0].reshape(L, PAST, -1)
        if dup:
            k = c[0].reshape(L, PAST, KV_C, 1, 64)
            k = np.concatenate([k, k, k, k], 3)
            k = k.reshape(L, PAST, 512)
            k = k.reshape(L, PAST, 2, 2, P)[:, :, :, 0].reshape(L, PAST, 2, P)
            k = np.concatenate([k, k], 2).reshape(L, PAST, 512)
        return k.reshape(L, PAST, 4, P).transpose(0, 3, 2, 1)

    ks = np.stack([keys(i["cache_nat_k"]), keys(i["cache_swa_k"], True), keys(i["cache_diff_k"])], 1)
    vs = np.zeros((L, 3, P, 512), np.float32)
    vs[:, 0] = i["cache_nat_v"][0].reshape(L, PAST, 512)
    vs[:, 1, :, 0:128] = i["cache_swa_v"][0].reshape(L, PAST, 128)
    vs[:, 2] = i["cache_diff_v"][0].reshape(L, PAST, 512)
    cond = np.zeros((P, KD, 32), np.float32)
    cond[:, :, 0:2] = np.stack([i["c"][0], i["c_ctx"]], 0).reshape(2, KD, P).transpose(2, 1, 0)
    arrays = {
        "units": stream, "tokens": np.concatenate([i["x_sample"][0].reshape(2, P, D), i["x_prompt"][0].reshape(1, P, D)]),
        "cond": cond, "pcol": pcol, "prow": prow, "small": small,
        "state_C": i["state_mlstm_C"][0].reshape(L, 2 * H_A, DH_A, DH_A).transpose(0, 3, 1, 2),
        "keys": ks.reshape(L * 3, P, 4, P), "vals": vs.reshape(L * 3, P, 512), "nat_bias": _windows(i["nat_rpb"]),
        "norm_final": i["norm_final"], **_constants()}
    return {k: np.ascontiguousarray(v) for k, v in arrays.items()}


_OUTS = {"tokens": (TILES, P, D), "nat_k": (DEPTH, P, 512), "nat_v": (DEPTH, P, 512), "swa_k": (DEPTH, P, 128),
         "swa_v": (DEPTH, P, 128), "diff_k": (DEPTH, P, 512), "diff_v": (DEPTH, P, 512),
         "C": (DEPTH * 2, H_A, DH_A, DH_A), "n": (DEPTH * 2, 512), "m": (DEPTH * 2, 4)}


def _build(nc, arrays, counts):
    a = {k: nc.dram_tensor("in_" + k, v.shape, mybir.dt.from_np(v.dtype), kind="ExternalInput").ap()
         for k, v in arrays.items()}
    a["x_scratch"] = nc.dram_tensor("x_scratch", (TILES, P, D), F32, kind="Internal").ap()
    a["g_scratch"] = nc.dram_tensor("g_scratch", (2, 16, P), F32, kind="Internal").ap()
    out = {k: nc.dram_tensor("out_" + k, s, F32, kind="ExternalOutput").ap() for k, s in _OUTS.items()}
    return program(nc, a, out, counts)


def kernel(**inputs):
    import concourse.bacc as _bacc
    from concourse.bass_utils import run_bass_kernel_spmd as _run
    arrays = _layout({k: np.asarray(v) for k, v in inputs.items()})
    counts = _build(_bacc.Bacc("TRN2", target_bir_lowering=False, num_devices=1), arrays, {})
    nc = _bacc.Bacc("TRN2", target_bir_lowering=False, num_devices=1)
    _build(nc, arrays, counts)
    res = _run(nc, [{"in_" + k: v for k, v in arrays.items()}], core_ids=[0]).results[0]
    o = {k: res["out_" + k] for k in _OUTS}
    L = DEPTH
    return (o["tokens"][2].reshape(1, T_CTX, D), o["tokens"][0:2].reshape(1, T_LAT, D),
            o["nat_k"].reshape(1, L, P, H_B, DH_B), o["nat_v"].reshape(1, L, P, H_B, DH_B),
            o["swa_k"].reshape(1, L, P, KV_C, 64), o["swa_v"].reshape(1, L, P, KV_C, 64),
            o["diff_k"].reshape(1, L, P, H_D, 128), o["diff_v"].reshape(1, L, P, H_D, 128),
            o["C"].reshape(1, L, 2, H_A, DH_A, DH_A), o["n"].reshape(1, L, 2, H_A, DH_A), o["m"].reshape(1, L, 2, H_A))
```
